# Optimizing a Trainium2 kernel written in Bass

```python
import math
import jax, jax.numpy as jnp
from jax import lax
import numpy as np

D_MODEL = 1024
BATCH = 1
SEQ = 512
DEPTH = 1

H_A = 8
DQK_A = D_MODEL // 16
DV_A = D_MODEL // 8
QK_A = H_A * DQK_A
V_A = H_A * DV_A
CHUNK = 64
CONV_K = 4
H_B = 8
HD_B = D_MODEL // 8
W_B = H_B * HD_B
QBLK = 128
D_FF = 4 * D_MODEL
EPS = 1e-6
IN_SIZES = (QK_A, QK_A, V_A, V_A, H_A, H_A, W_B, W_B, W_B, D_MODEL, D_MODEL)
IN_COLS = sum(IN_SIZES)


def rms_norm(x, g):
    xf = x.astype(jnp.float32)
    y = xf * lax.rsqrt(jnp.mean(xf * xf, axis=-1, keepdims=True) + EPS)
    return (y * g.astype(jnp.float32)).astype(x.dtype)

def head_rms_norm(x, g):
    xf = x.astype(jnp.float32)
    y = xf * lax.rsqrt(jnp.mean(xf * xf, axis=-1, keepdims=True) + EPS)
    return y * g.astype(jnp.float32)

def causal_conv(x, w):
    S = x.shape[1]
    xp = jnp.pad(x, ((0, 0), (CONV_K - 1, 0), (0, 0)))
    y = xp[:, 0:S] * w[0]
    for j in range(1, CONV_K):
        y = y + xp[:, j:j + S] * w[j]
    return y

def mlstm_chunkwise(q, k, v, i_pre, f_pre):
    B, S, H, _ = q.shape
    NC = S // CHUNK
    to_chunks = lambda a: jnp.moveaxis(a.astype(jnp.float32).reshape(B, NC, CHUNK, H, -1), 3, 1)
    q = to_chunks(q)
    k = to_chunks(k) * (DQK_A ** -0.5)
    v = to_chunks(v)
    gate = lambda a: jnp.moveaxis(a.astype(jnp.float32).reshape(B, NC, CHUNK, H), 3, 1)
    logf = jax.nn.log_sigmoid(gate(f_pre))
    ig = gate(i_pre)
    b = jnp.cumsum(logf, axis=-1)
    b_last = b[..., -1]

    a = b_last[..., None] - b + ig
    m_loc = jnp.max(a, axis=-1)
    w = jnp.exp(a - m_loc[..., None])
    S_loc = jnp.einsum('bhcs,bhcsk,bhcsv->bhckv', w, k, v)
    n_loc = jnp.einsum('bhcs,bhcsk->bhck', w, k)

    def step(carry, inp):
        S_prev, n_prev, m_prev = carry
        S_l, n_l, m_l, bl = inp
        m_new = jnp.maximum(bl + m_prev, m_l)
        sp = jnp.exp(bl + m_prev - m_new)
        sl = jnp.exp(m_l - m_new)
        S_new = sp[..., None, None] * S_prev + sl[..., None, None] * S_l
        n_new = sp[..., None] * n_prev + sl[..., None] * n_l
        return (S_new, n_new, m_new), (S_prev, n_prev, m_prev)

    init = (jnp.zeros_like(S_loc[:, :, 0]), jnp.zeros_like(n_loc[:, :, 0]), jnp.zeros_like(m_loc[:, :, 0]))
    xs = (jnp.moveaxis(S_loc, 2, 0), jnp.moveaxis(n_loc, 2, 0), jnp.moveaxis(m_loc, 2, 0), jnp.moveaxis(b_last, 2, 0))
    _, (S0, n0, m0) = lax.scan(step, init, xs)
    S0 = jnp.moveaxis(S0, 0, 2)
    n0 = jnp.moveaxis(n0, 0, 2)
    m0 = jnp.moveaxis(m0, 0, 2)

    causal = jnp.tril(jnp.ones((CHUNK, CHUNK), dtype=bool))
    D = jnp.where(causal, b[..., :, None] - b[..., None, :] + ig[..., None, :], -jnp.inf)
    b_inter = b + m0[..., None]
    m_t = jnp.maximum(b_inter, jnp.max(D, axis=-1))
    P = jnp.exp(D - m_t[..., None]) * jnp.einsum('bhctk,bhcsk->bhcts', q, k)
    inter = jnp.exp(b_inter - m_t)
    num = jnp.einsum('bhcts,bhcsv->bhctv', P, v) + inter[..., None] * jnp.einsum('bhctk,bhckv->bhctv', q, S0)
    den = jnp.sum(P, axis=-1) + inter * jnp.einsum('bhctk,bhck->bhct', q, n0)
    h = num / jnp.maximum(jnp.abs(den), jnp.exp(-m_t))[..., None]
    return jnp.moveaxis(h, 1, 3).reshape(B, S, H, DV_A)

def stick_breaking(q, k, v):
    S = q.shape[1]
    scale = HD_B ** -0.5
    outs = []
    for blk in range(S // QBLK):
        t0, t1 = blk * QBLK, (blk + 1) * QBLK
        z = jnp.einsum('bqhd,bshd->bhqs', q[:, t0:t1], k[:, :t1]) * scale
        t_idx = t0 + jnp.arange(QBLK)
        s_idx = jnp.arange(t1)
        strict = s_idx[None, :] < t_idx[:, None]
        log_keep = jnp.where(strict, jax.nn.log_sigmoid(-z), 0.0)
        suffix = lax.cumsum(log_keep, axis=3, reverse=True) - log_keep
        A = jnp.where(strict, jnp.exp(jax.nn.log_sigmoid(z) + suffix), 0.0)
        outs.append(jnp.einsum('bhqs,bshd->bqhd', A, v[:, :t1]))
    return jnp.concatenate(outs, axis=1)

def first_inputs(seed: int = 0) -> dict:
    key = jax.random.key(seed)
    ks = jax.random.split(key, 15)
    n = jax.random.normal
    f32 = jnp.float32
    x = n(ks[0], (BATCH, SEQ, D_MODEL), f32)
    norm_mix_g = 1.0 + 0.1 * n(ks[1], (DEPTH, D_MODEL), f32)
    w_in = n(ks[2], (DEPTH, D_MODEL, IN_COLS), f32) * D_MODEL ** -0.5
    b_if = jnp.concatenate([0.5 * n(ks[3], (DEPTH, H_A), f32),
                            3.0 + 0.5 * n(ks[4], (DEPTH, H_A), f32)], axis=-1)
    b_gate = 0.02 * n(ks[5], (DEPTH, 2 * D_MODEL), f32)
    conv_w = n(ks[6], (DEPTH, CONV_K, 2 * QK_A), f32) * CONV_K ** -0.5
    mlstm_norm_g = 1.0 + 0.1 * n(ks[7], (DEPTH, V_A), f32)
    sb_q_norm_g = 1.0 + 0.1 * n(ks[8], (DEPTH, HD_B), f32)
    sb_k_norm_g = 1.0 + 0.1 * n(ks[9], (DEPTH, HD_B), f32)
    w_out = n(ks[10], (DEPTH, D_MODEL, D_MODEL), f32) * D_MODEL ** -0.5
    norm_mlp_g = 1.0 + 0.1 * n(ks[11], (DEPTH, D_MODEL), f32)
    w_up = n(ks[12], (DEPTH, D_MODEL, D_FF), f32) * D_MODEL ** -0.5
    w_down = n(ks[13], (DEPTH, D_FF, D_MODEL), f32) * D_FF ** -0.5
    return {"x": x, "norm_mix_g": norm_mix_g, "w_in": w_in, "b_if": b_if, "b_gate": b_gate,
            "conv_w": conv_w, "mlstm_norm_g": mlstm_norm_g, "sb_q_norm_g": sb_q_norm_g,
            "sb_k_norm_g": sb_k_norm_g, "w_out": w_out, "norm_mlp_g": norm_mlp_g,
            "w_up": w_up, "w_down": w_down}

def first_block(x, norm_mix_g, w_in, b_if, b_gate, conv_w, mlstm_norm_g, sb_q_norm_g, sb_k_norm_g,
              w_out, norm_mlp_g, w_up, w_down):
    B, S, _ = x.shape
    split_idx = np.cumsum(IN_SIZES)[:-1].tolist()
    for l in range(DEPTH):
        h = rms_norm(x, norm_mix_g[l])
        p = h @ w_in[l]
        q_a, k_a, v_a, o_a, i_a, f_a, q_b, k_b, v_b, g_a, g_b = jnp.split(p, split_idx, axis=-1)
        qk_a = jax.nn.silu(causal_conv(jnp.concatenate([q_a, k_a], axis=-1), conv_w[l]))
        q_a, k_a = qk_a[..., :QK_A], qk_a[..., QK_A:]
        i_pre = i_a.astype(jnp.float32) + b_if[l, :H_A].astype(jnp.float32)
        f_pre = f_a.astype(jnp.float32) + b_if[l, H_A:].astype(jnp.float32)
        h_a = mlstm_chunkwise(q_a.reshape(B, S, H_A, DQK_A), k_a.reshape(B, S, H_A, DQK_A),
                              v_a.reshape(B, S, H_A, DV_A), i_pre, f_pre)
        h_a = head_rms_norm(h_a, mlstm_norm_g[l].reshape(H_A, DV_A)).reshape(B, S, V_A)
        y_a = jax.nn.sigmoid(o_a.astype(jnp.float32)) * h_a
        qn = head_rms_norm(q_b.reshape(B, S, H_B, HD_B), sb_q_norm_g[l])
        kn = head_rms_norm(k_b.reshape(B, S, H_B, HD_B), sb_k_norm_g[l])
        y_b = stick_breaking(qn, kn, v_b.reshape(B, S, H_B, HD_B).astype(jnp.float32)).reshape(B, S, W_B)
        gates = jax.nn.sigmoid(jnp.concatenate([g_a, g_b], axis=-1).astype(jnp.float32)
                               + b_gate[l].astype(jnp.float32))
        y = gates[..., :D_MODEL] * y_a + gates[..., D_MODEL:] * y_b
        x = x + y.astype(x.dtype) @ w_out[l]
        h2 = rms_norm(x, norm_mlp_g[l])
        x = x + jnp.square(jax.nn.relu(h2 @ w_up[l])) @ w_down[l]
    return x


N_MIXERS = 2
RMS_EPS = 1e-6
GN_EPS = 1e-6
NEG_INF = -1e30

NSA_HEADS = 16
NSA_HEAD_DIM = 64
NSA_KV_GROUPS = 4
NSA_Q_PER_GROUP = NSA_HEADS // NSA_KV_GROUPS
NSA_WIDTH = NSA_HEADS * NSA_HEAD_DIM
NSA_KV_WIDTH = NSA_KV_GROUPS * NSA_HEAD_DIM
CMP_BLOCK = 32
CMP_STRIDE = 16
CMP_HIDDEN = 256
SLC_BLOCK = 64
SLC_TOPN = 16
SLC_Q_BLOCK = 32
WIN_SIZE = 512
WIN_Q_BLOCK = 128
FORCED_SCORE = 1e3
NSA_PROJ = NSA_WIDTH + 6 * NSA_KV_WIDTH + 3 * NSA_HEADS + 3 * NSA_WIDTH

REL_BUCKETS = 32
REL_MAX_DIST = 128

RET_HEADS = 4
RET_QK_DIM = 256
RET_V_DIM = 512
RET_QK_WIDTH = RET_HEADS * RET_QK_DIM
RET_WIDTH = RET_HEADS * RET_V_DIM
RET_CHUNK = 128
ROPE_BASE = 10000.0
RET_PROJ = 2 * RET_QK_WIDTH + 2 * RET_WIDTH


def rms_norm_2(x, gain):
    xf = x.astype(jnp.float32)
    y = xf * lax.rsqrt(jnp.mean(xf * xf, axis=-1, keepdims=True) + RMS_EPS)
    return (y * gain.astype(jnp.float32)).astype(x.dtype)

def split_cols(a, sizes):
    return jnp.split(a, list(np.cumsum(sizes)[:-1]), axis=-1)

def masked_softmax(logits, mask):
    p = jax.nn.softmax(jnp.where(mask, logits, NEG_INF), axis=-1)
    return jnp.where(mask, p, 0.0)

def t5_bucket(dist):
    n = jnp.maximum(dist, 0)
    max_exact = REL_BUCKETS // 2
    nf = jnp.maximum(n, 1).astype(jnp.float32)
    large = max_exact + (jnp.log(nf / max_exact) / math.log(REL_MAX_DIST / max_exact)
                         * (REL_BUCKETS - max_exact)).astype(jnp.int32)
    large = jnp.minimum(large, REL_BUCKETS - 1)
    return jnp.where(n < max_exact, n, large)

def compress_kv(kv, pos, w1, w2):
    B, S, G, dh = kv.shape
    n_cmp = (S - CMP_BLOCK) // CMP_STRIDE + 1
    idx = jnp.arange(n_cmp)[:, None] * CMP_STRIDE + jnp.arange(CMP_BLOCK)[None, :]
    blocks = kv[:, idx] + pos[None, None, :, None, :].astype(kv.dtype)
    flat = blocks.transpose(0, 1, 3, 2, 4).reshape(B, n_cmp, G, CMP_BLOCK * dh)
    return jax.nn.silu(flat @ w1) @ w2

def nsa_compressed(q, kc, vc, table):
    B, S, H, dh = q.shape
    n_cmp = kc.shape[1]
    qg = q.reshape(B, S, NSA_KV_GROUPS, NSA_Q_PER_GROUP, dh)
    logits = jnp.einsum('bsgrd,bcgd->bgrsc', qg, kc).astype(jnp.float32) * (dh ** -0.5)
    t = jnp.arange(S)
    end = jnp.arange(n_cmp) * CMP_STRIDE + CMP_BLOCK - 1
    dist = t[:, None] - end[None, :]
    bias = table[t5_bucket(dist)].astype(jnp.float32)
    bias = bias.reshape(S, n_cmp, NSA_KV_GROUPS, NSA_Q_PER_GROUP).transpose(2, 3, 0, 1)
    p = masked_softmax(logits + bias, dist >= 0)
    o = jnp.einsum('bgrsc,bcgd->bsgrd', p.astype(vc.dtype), vc).reshape(B, S, H, dh)
    return o, p

def select_blocks(p_cmp, S):
    n_cmp = p_cmp.shape[-1]
    n_sel = S // SLC_BLOCK
    cs = jnp.arange(n_cmp) * CMP_STRIDE
    j = jnp.arange(n_sel)
    overlap = ((cs[:, None] < (j[None, :] + 1) * SLC_BLOCK)
               & (cs[:, None] + CMP_BLOCK > j[None, :] * SLC_BLOCK)).astype(jnp.float32)
    imp = jnp.einsum('bgrsc,cj->bgsj', p_cmp, overlap)
    t = jnp.arange(S)
    cur = t // SLC_BLOCK
    valid = j[None, :] * SLC_BLOCK <= t[:, None]
    forced = (j[None, :] == 0) | (j[None, :] == cur[:, None]) | (j[None, :] == cur[:, None] - 1)
    score = jnp.where(valid, imp + jnp.where(forced, FORCED_SCORE, 0.0), NEG_INF)
    _, sel = lax.top_k(score, min(SLC_TOPN, n_sel))
    return sel

def nsa_selected(q, k, v, sel, table):
    B, S, H, dh = q.shape
    G, R = NSA_KV_GROUPS, NSA_Q_PER_GROUP
    n_sel = S // SLC_BLOCK
    n_top = sel.shape[-1]
    n_keys = n_top * SLC_BLOCK
    kb = k.reshape(B, n_sel, SLC_BLOCK, G, dh).transpose(0, 3, 1, 2, 4)
    vb = v.reshape(B, n_sel, SLC_BLOCK, G, dh).transpose(0, 3, 1, 2, 4)
    nq = S // SLC_Q_BLOCK
    q_blk = q.reshape(B, nq, SLC_Q_BLOCK, G, R, dh).transpose(1, 0, 2, 3, 4, 5)
    sel_blk = sel.reshape(B, G, nq, SLC_Q_BLOCK, n_top).transpose(2, 0, 1, 3, 4)
    bi = jnp.arange(B)[:, None, None, None]
    gi = jnp.arange(G)[None, :, None, None]
    tbl = table.reshape(REL_BUCKETS, G, R)

    def one(args):
        qb, sb, blk = args
        t = blk * SLC_Q_BLOCK + jnp.arange(SLC_Q_BLOCK)
        kg = kb[bi, gi, sb].reshape(B, G, SLC_Q_BLOCK, n_keys, dh)
        vg = vb[bi, gi, sb].reshape(B, G, SLC_Q_BLOCK, n_keys, dh)
        pos = (sb[..., None] * SLC_BLOCK + jnp.arange(SLC_BLOCK)).reshape(B, G, SLC_Q_BLOCK, n_keys)
        dist = t[None, None, :, None] - pos
        bias = tbl[t5_bucket(dist), gi].astype(jnp.float32).transpose(0, 1, 4, 2, 3)
        logits = jnp.einsum('bqgrd,bgqkd->bgrqk', qb, kg).astype(jnp.float32) * (dh ** -0.5)
        p = masked_softmax(logits + bias, (dist >= 0)[:, :, None])
        return jnp.einsum('bgrqk,bgqkd->bqgrd', p.astype(vg.dtype), vg)

    out = lax.map(one, (q_blk, sel_blk, jnp.arange(nq)))
    return out.transpose(1, 0, 2, 3, 4, 5).reshape(B, S, H, dh)

def nsa_window(q, k, v, table):
    B, S, H, dh = q.shape
    G, R = NSA_KV_GROUPS, NSA_Q_PER_GROUP
    nq = S // WIN_Q_BLOCK
    span = WIN_SIZE + WIN_Q_BLOCK
    kp = jnp.pad(k, ((0, 0), (WIN_SIZE, 0), (0, 0), (0, 0)))
    vp = jnp.pad(v, ((0, 0), (WIN_SIZE, 0), (0, 0), (0, 0)))
    q_blk = q.reshape(B, nq, WIN_Q_BLOCK, G, R, dh).transpose(1, 0, 2, 3, 4, 5)

    def one(args):
        qb, blk = args
        start = blk * WIN_Q_BLOCK
        kw = lax.dynamic_slice_in_dim(kp, start, span, axis=1)
        vw = lax.dynamic_slice_in_dim(vp, start, span, axis=1)
        t = start + jnp.arange(WIN_Q_BLOCK)
        pos = start - WIN_SIZE + jnp.arange(span)
        dist = t[:, None] - pos[None, :]
        mask = (dist >= 0) & (dist < WIN_SIZE) & (pos[None, :] >= 0)
        bias = table[t5_bucket(dist)].astype(jnp.float32)
        bias = bias.reshape(WIN_Q_BLOCK, span, G, R).transpose(2, 3, 0, 1)
        logits = jnp.einsum('bqgrd,bkgd->bgrqk', qb, kw).astype(jnp.float32) * (dh ** -0.5)
        p = masked_softmax(logits + bias, mask)
        return jnp.einsum('bgrqk,bkgd->bqgrd', p.astype(vw.dtype), vw)

    out = lax.map(one, (q_blk, jnp.arange(nq)))
    return out.transpose(1, 0, 2, 3, 4, 5).reshape(B, S, H, dh)

def nsa_mixer(h, w_in, w_out, k_pos, k_w1, k_w2, v_pos, v_w1, v_w2, table):
    B, S, _ = h.shape
    H, dh, G = NSA_HEADS, NSA_HEAD_DIM, NSA_KV_GROUPS
    q, kv, g, z = split_cols(h @ w_in, [NSA_WIDTH, 6 * NSA_KV_WIDTH, 3 * H, 3 * NSA_WIDTH])
    q = q.reshape(B, S, H, dh)
    k_c, v_c, k_s, v_s, k_w, v_w = [a.reshape(B, S, G, dh) for a in jnp.split(kv, 6, axis=-1)]
    gates = jax.nn.sigmoid(g).reshape(B, S, 3, H, 1)
    zs = jax.nn.silu(z).reshape(B, S, 3, H, dh)
    kc = compress_kv(k_c, k_pos, k_w1, k_w2)
    vc = compress_kv(v_c, v_pos, v_w1, v_w2)
    o_cmp, p_cmp = nsa_compressed(q, kc, vc, table)
    sel = select_blocks(p_cmp, S)
    o_slc = nsa_selected(q, k_s, v_s, sel, table)
    o_win = nsa_window(q, k_w, v_w, table)
    o = jnp.stack([o_cmp, o_slc, o_win], axis=2)
    y = jnp.sum(gates * o * zs, axis=2).reshape(B, S, NSA_WIDTH)
    return y @ w_out

def rotary(x):
    S, d = x.shape[1], x.shape[-1]
    inv = 1.0 / (ROPE_BASE ** jnp.linspace(0.0, 1.0, d // 2, dtype=jnp.float32))
    ang = jnp.arange(S, dtype=jnp.float32)[:, None] * inv[None, :]
    cos = jnp.cos(ang)[None, :, None, :].astype(x.dtype)
    sin = jnp.sin(ang)[None, :, None, :].astype(x.dtype)
    x1, x2 = x[..., :d // 2], x[..., d // 2:]
    return jnp.concatenate([x1 * cos - x2 * sin, x1 * sin + x2 * cos], axis=-1)

def chunkwise_retention(q, k, v):
    B, S, H, dk = q.shape
    dv = v.shape[-1]
    C = RET_CHUNK
    nc = S // C
    dt = q.dtype
    log_g = jnp.log(1.0 - 2.0 ** (-5.0 - jnp.arange(H, dtype=jnp.float32)))
    i = jnp.arange(C, dtype=jnp.float32)
    diff = i[:, None] - i[None, :]
    inner = jnp.where(diff >= 0, jnp.exp(diff[None] * log_g[:, None, None]), 0.0).astype(dt)
    xi = jnp.exp((i + 1.0)[None, :] * log_g[:, None]).astype(dt)
    zeta = jnp.exp((C - 1.0 - i)[None, :] * log_g[:, None]).astype(dt)
    chunk_decay = jnp.exp(C * log_g).astype(dt)
    qc = q.reshape(B, nc, C, H, dk).transpose(1, 0, 3, 2, 4)
    kc = k.reshape(B, nc, C, H, dk).transpose(1, 0, 3, 2, 4)
    vc = v.reshape(B, nc, C, H, dv).transpose(1, 0, 3, 2, 4)

    def step(state, inp):
        qi, ki, vi = inp
        attn = jnp.einsum('bhid,bhjd->bhij', qi, ki) * inner[None]
        o = (jnp.einsum('bhij,bhjv->bhiv', attn, vi)
             + jnp.einsum('bhid,bhdv->bhiv', qi, state) * xi[None, :, :, None])
        state = (state * chunk_decay[None, :, None, None]
                 + jnp.einsum('bhjd,bhjv->bhdv', ki * zeta[None, :, :, None], vi))
        return state, o

    state0 = jnp.zeros((B, H, dk, dv), dt)
    _, o = lax.scan(step, state0, (qc, kc, vc))
    return o.transpose(1, 0, 3, 2, 4).reshape(B, S, H, dv)

def retention_mixer(h, w_in, w_out, gn_gain):
    B, S, _ = h.shape
    q, k, v, z = split_cols(h @ w_in, [RET_QK_WIDTH, RET_QK_WIDTH, RET_WIDTH, RET_WIDTH])
    q = rotary(q.reshape(B, S, RET_HEADS, RET_QK_DIM))
    k = rotary(k.reshape(B, S, RET_HEADS, RET_QK_DIM)) * (RET_QK_DIM ** -0.5)
    v = v.reshape(B, S, RET_HEADS, RET_V_DIM)
    o = chunkwise_retention(q, k, v).astype(jnp.float32)
    mu = jnp.mean(o, axis=-1, keepdims=True)
    var = jnp.mean(jnp.square(o - mu), axis=-1, keepdims=True)
    o = (o - mu) * lax.rsqrt(var + GN_EPS) * gn_gain.reshape(RET_HEADS, RET_V_DIM).astype(jnp.float32)
    o = o.astype(h.dtype).reshape(B, S, RET_WIDTH)
    return (o * jax.nn.silu(z)) @ w_out

def second_inputs(seed: int = 0) -> dict:
    key = jax.random.key(seed)
    ks = jax.random.split(key, 16)
    n_nsa = (DEPTH + N_MIXERS - 1) // N_MIXERS
    n_ret = DEPTH // N_MIXERS

    def nrm(k, shape, scale):
        return jax.random.normal(k, shape, jnp.float32) * scale

    return {
        "x": nrm(ks[0], (BATCH, SEQ, D_MODEL), 1.0),
        "pre_norm_gain": 1.0 + nrm(ks[1], (DEPTH, D_MODEL), 0.1),
        "post_norm_gain": 1.0 + nrm(ks[2], (DEPTH, D_MODEL), 0.1),
        "rel_bias_table": nrm(ks[3], (REL_BUCKETS, NSA_HEADS), 0.5),
        "nsa_w_in": nrm(ks[4], (n_nsa, D_MODEL, NSA_PROJ), D_MODEL ** -0.5),
        "nsa_w_out": nrm(ks[5], (n_nsa, NSA_WIDTH, D_MODEL), NSA_WIDTH ** -0.5),
        "nsa_cmp_k_pos": nrm(ks[6], (n_nsa, CMP_BLOCK, NSA_HEAD_DIM), 0.5),
        "nsa_cmp_k_w1": nrm(ks[7], (n_nsa, CMP_BLOCK * NSA_HEAD_DIM, CMP_HIDDEN), (CMP_BLOCK * NSA_HEAD_DIM) ** -0.5),
        "nsa_cmp_k_w2": nrm(ks[8], (n_nsa, CMP_HIDDEN, NSA_HEAD_DIM), CMP_HIDDEN ** -0.5),
        "nsa_cmp_v_pos": nrm(ks[9], (n_nsa, CMP_BLOCK, NSA_HEAD_DIM), 0.5),
        "nsa_cmp_v_w1": nrm(ks[10], (n_nsa, CMP_BLOCK * NSA_HEAD_DIM, CMP_HIDDEN), (CMP_BLOCK * NSA_HEAD_DIM) ** -0.5),
        "nsa_cmp_v_w2": nrm(ks[11], (n_nsa, CMP_HIDDEN, NSA_HEAD_DIM), CMP_HIDDEN ** -0.5),
        "ret_w_in": nrm(ks[12], (n_ret, D_MODEL, RET_PROJ), D_MODEL ** -0.5),
        "ret_w_out": nrm(ks[13], (n_ret, RET_WIDTH, D_MODEL), RET_WIDTH ** -0.5),
        "ret_gn_gain": 1.0 + nrm(ks[14], (n_ret, RET_WIDTH), 0.1),
    }

def second_block(x, pre_norm_gain, post_norm_gain, rel_bias_table, nsa_w_in, nsa_w_out,
              nsa_cmp_k_pos, nsa_cmp_k_w1, nsa_cmp_k_w2, nsa_cmp_v_pos, nsa_cmp_v_w1, nsa_cmp_v_w2,
              ret_w_in, ret_w_out, ret_gn_gain):
    h = x
    for layer in range(DEPTH):
        slot = layer // N_MIXERS
        u = rms_norm_2(h, pre_norm_gain[layer])
        if layer % N_MIXERS == 0:
            y = nsa_mixer(u, nsa_w_in[slot], nsa_w_out[slot],
                          nsa_cmp_k_pos[slot], nsa_cmp_k_w1[slot], nsa_cmp_k_w2[slot],
                          nsa_cmp_v_pos[slot], nsa_cmp_v_w1[slot], nsa_cmp_v_w2[slot],
                          rel_bias_table)
        else:
            y = retention_mixer(u, ret_w_in[slot], ret_w_out[slot], ret_gn_gain[slot])
        h = h + rms_norm_2(y, post_norm_gain[layer])
    return h


def setup_inputs(seed=0):
    out = dict(first_inputs(seed))
    for name, value in second_inputs(seed + 1).items():
        if name != "x":
            out[name + "_2"] = value
    return out


def reference(
    x, norm_mix_g, w_in, b_if, b_gate, conv_w, mlstm_norm_g, sb_q_norm_g, sb_k_norm_g, w_out,
    norm_mlp_g, w_up, w_down, pre_norm_gain_2, post_norm_gain_2, rel_bias_table_2, nsa_w_in_2,
    nsa_w_out_2, nsa_cmp_k_pos_2, nsa_cmp_k_w1_2, nsa_cmp_k_w2_2, nsa_cmp_v_pos_2,
    nsa_cmp_v_w1_2, nsa_cmp_v_w2_2, ret_w_in_2, ret_w_out_2, ret_gn_gain_2,
):
    x = first_block(
        x, norm_mix_g, w_in, b_if, b_gate, conv_w, mlstm_norm_g, sb_q_norm_g, sb_k_norm_g,
        w_out, norm_mlp_g, w_up, w_down,
    )
    return second_block(
        x, pre_norm_gain_2, post_norm_gain_2, rel_bias_table_2, nsa_w_in_2, nsa_w_out_2,
        nsa_cmp_k_pos_2, nsa_cmp_k_w1_2, nsa_cmp_k_w2_2, nsa_cmp_v_pos_2, nsa_cmp_v_w1_2,
        nsa_cmp_v_w2_2, ret_w_in_2, ret_w_out_2, ret_gn_gain_2,
    )


_drawn_inputs = setup_inputs


def setup_inputs(seed=0):
    import zlib

    import numpy as np

    out = dict(_drawn_inputs(seed))
    spreads = {}
    factors = {'b_gate': 8.0, 'sb_q_norm_g': 3.121, 'sb_k_norm_g': 2.911, 'nsa_cmp_k_pos_2': 2.681}
    for name, (base, spread) in spreads.items():
        noise = np.random.default_rng([zlib.crc32(name.encode()), seed]).standard_normal(out[name].shape)
        drawn = base * np.exp(spread * noise) if base else spread * noise
        out[name] = __import__('jax').numpy.asarray(drawn.astype(out[name].dtype))
    for name, factor in factors.items():
        out[name] = (out[name] * factor).astype(out[name].dtype)
    return out
```

```python
from contextlib import ExitStack

import numpy as np
import concourse.bass as bass
from concourse import mybir

ALU = mybir.AluOpType
ACT = mybir.ActivationFunctionType
AX_X = mybir.AxisListType.X
F32 = mybir.dt.float32
F32R = mybir.dt.float32r

P = 128
S = 512
D = 1024
TB = S // P
KT = D // P
SLAB = 256
EPS = 1e-6
HA = 8
DQK = 64
HB = 8
HD = 128
DFF = 4 * D
HN = 16
DH = 64
GN = 4
NCMP = 31
CSTRIDE = 16
CLEN = 32
BUCKETS = 32
NEG = -1e30

QA, KA, VA, OA, IF = 0, 512, 1024, 2048, 3072
QB, KB, VB, GA, GB = 3088, 4112, 5136, 6160, 7184
NQ, NKC, NVC, NKS, NVS, NKW, NVW, NG, NZ = 0, 1024, 1280, 1536, 1792, 2048, 2304, 2560, 2608

CAUSAL_AT = (0, 512, 1024, 896)
CAUSAL_W = (512, 384, 256, 128)
CAUSAL = 1280
ROWS_AT = (896, 1024, 512, 0)
ROWS_W = (128, 256, 384, 512)

V_MIX, V_MLP, V_PRE, V_MNORM, V_CONV, V_BGATE, V_POSK, V_POSV, V_QN, V_KN, V_ROWS = (
    0, 8, 16, 24, 32, 64, 80, 96, 112, 113, 114)

C_ID, C_TRI, C_NEG, C_MIN, C_STRIP, C_VALID, C_ALL = 0, 128, 256, 384, 512, 592, 596
REV = S + P
OH_REV, OH_W = 1024, 1024 + REV

VEC_PARTS = (("mix_g", (V_MIX, 8)), ("mlp_g", (V_MLP, 8)), ("pre_g", (V_PRE, 8)),
             ("mnorm_g", (V_MNORM, 8)), ("conv_w", (V_CONV, 32)), ("b_gate", (V_BGATE, 16)),
             ("pos_k", (V_POSK, 16)), ("pos_v", (V_POSV, 16)), ("qn_g", (V_QN, 1)), ("kn_g", (V_KN, 1)))
N_VEC = len(VEC_PARTS) + 1


def constants():
    j = np.arange(P)[:, None]
    s = np.arange(P)[None, :]
    c = np.zeros((P, C_ALL), np.float32)
    c[:, C_ID:C_ID + P] = j == s
    c[:, C_TRI:C_TRI + P] = np.where(j >= s, -1.0, 0.0)
    c[:, C_NEG:C_NEG + P] = -1.0
    c[:, C_MIN:C_MIN + P] = np.where(j < s, -NEG, NEG)
    c[:, C_STRIP + 39] = 1.0
    t = np.arange(TB)[None, :] * P + j
    c[:, C_VALID:C_VALID + TB] = t >= CLEN - 1
    return c


def bucket_table():
    dist = np.concatenate([np.arange(OH_REV) - 511, 511 - np.arange(OH_W - OH_REV)])
    n = np.maximum(dist, 0)
    half = BUCKETS // 2
    large = half + (np.log(np.maximum(n, 1) / half) / np.log(128 / half) * half + 1e-9).astype(int)
    bucket = np.where(n < half, n, np.minimum(large, BUCKETS - 1))
    t = (bucket[None, :] == np.arange(BUCKETS)[:, None]) & (dist >= 0)[None, :]
    return np.concatenate([t, (dist < 0)[None, :]]).astype(np.float32)


class Order:

    def __init__(self, eng, sem):
        self.eng, self.sem, self.n, self.shift = eng, sem, 0, 0

    def link(self, ins):
        ins.then_inc(self.sem, 1)
        self.n += 1
        self.eng.wait_ge(self.sem, self.n + self.shift)


def program(nc, a, out):
    with ExitStack() as ctx:
        def sem(name):
            return ctx.enter_context(nc.semaphore(name))

        base = -(-nc.sbuf_base // 64) * 64
        top = [base]

        def sb(name, shape, dt=F32, at=None):
            size = int(np.prod(shape[1:])) * 4
            if at is None:
                at = top[0]
                top[0] += -(-size // 32) * 32
                assert top[0] <= nc.sbuf_usable_end, (name, top[0])
            return nc.alloc_sbuf_tensor_at(name, shape, dt, offset=at)

        x_sb = sb("x_sb", [P, TB, D])
        act_hi = sb("act_hi", [P, KT, S], F32R)
        act_lo = sb("act_lo", [P, KT, S], F32R)
        w_raw = [sb(f"w_raw{i}", [P, KT, SLAB]) for i in range(2)]
        w_hi = [sb(f"w_hi{i}", [P, KT, SLAB], F32R) for i in range(2)]
        w_lo = [sb(f"w_lo{i}", [P, KT, SLAB], F32R) for i in range(2)]
        arena = top[0]
        K16 = 16384
        top[0] += 6 * K16

        xn = sb("xn", [P, TB, D], at=arena + 4 * K16)
        qk_a = sb("qk_a", [P, 8, S], at=arena)
        v_a = sb("v_a", [P, TB, D], at=arena + K16)
        y_f = sb("y_f", [P, 8, S], at=arena + 2 * K16)
        q_b = sb("q_b", [P, HB, S], at=arena + 3 * K16)
        k_b = sb("k_b", [P, HB, S], at=arena + 4 * K16)
        v_b = sb("v_b", [P, TB, D], at=arena + K16)
        y_hi = sb("y_hi", [P, KT, S], F32R, at=arena + 3 * K16)
        y_lo = sb("y_lo", [P, KT, S], F32R, at=arena + 4 * K16)
        yb_f = sb("yb_f", [P, HB, S], at=arena)
        t1 = arena + 5 * K16
        conv_t = sb("conv_t", [P, 2, S], at=t1)
        decay = sb("decay", [P, CAUSAL], at=t1)
        num_sq = sb("num_sq", [P, S], at=t1 + 5120)
        rows = [sb(f"rows{i}", [HA, S], at=t1 + 7168 + 2048 * i) for i in range(4)]
        sqs = sb("sqs", [P, 2, S], at=t1)
        sp_t = sb("sp_t", [P, CAUSAL], at=t1)
        later1 = sb("later1", [P, 256], at=t1 + 5120)
        later0 = sb("later0", [P, 384], at=t1 + 6144)
        attn_b = sb("attn_b", [P, CAUSAL], at=t1 + 7680)
        stat_row = sb("stat_row", [16, S], at=t1 + 5120)
        up_hi = sb("up_hi", [P, KT, S], F32R, at=arena)
        up_lo = sb("up_lo", [P, KT, S], F32R, at=arena + K16)
        xn2 = sb("xn2", [P, TB, D], at=arena + 2 * K16)
        relu_t = sb("relu_t", [P, 2, S], at=arena + 3 * K16)
        qn = sb("qn", [P, 8, S], at=arena)
        ks = sb("ks", [P, 2, S], at=arena + K16)
        kw = sb("kw", [P, 2, S], at=arena + K16 + 4096)
        vs = sb("vs", [P, TB, 256], at=arena + K16 + 8192)
        vw = sb("vw", [P, TB, 256], at=arena + K16 + 12288)
        o_a = sb("o_a", [P, TB, D], at=arena + 2 * K16)
        o_b = sb("o_b", [P, TB, D], at=arena + 3 * K16)
        o_c = sb("o_c", [P, TB, D], at=arena + 4 * K16)
        w1k = sb("w1k", [P, 16, 256], at=arena + 2 * K16)
        w1v = sb("w1v", [P, 16, 256], at=arena + 3 * K16)
        pairk = sb("pairk", [P, GN, S], at=arena + 4 * K16)
        pairv = sb("pairv", [P, GN, S], at=arena + 4 * K16 + 8192)
        cmp_in = sb("cmp_in", [P, 16, GN * NCMP], at=arena + 5 * K16)
        cbias = sb("cbias", [P, TB, NCMP, HN], at=arena + 3 * K16)
        clog = sb("clog", [P, HN, NCMP], at=arena + 3 * K16 + 8192)
        cpt = sb("cpt", [NCMP, HN, P], at=arena + 4 * K16)
        probs = [sb(f"probs{i}", [P, CAUSAL], at=arena + 5 * K16 + 5120 * i) for i in range(2)]
        probs_t = sb("probs_t", [P, CAUSAL], at=arena + 5 * K16 + 10240)
        y2 = sb("y2", [P, TB, D], at=arena)
        gain_bc = sb("gain_bc", [P, D], at=arena + K16)
        xo = sb("xo", [P, TB, D], at=arena + 3 * K16)

        cst = sb("cst", [P, C_ALL])
        vec_rows = sb("vec_rows", [V_ROWS, P])
        vec = sb("vec", [P, V_ROWS])
        bif_bc = sb("bif_bc", [P, 16])
        gate_pre = sb("gate_pre", [P, TB, 16])
        ones_row = sb("ones_row", [HA, S], at=arena + 3 * K16)
        u_col = sb("u_col", [P, TB, HA])
        ssq = sb("ssq", [P, 4, TB])
        rstd = sb("rstd", [P, 4, TB])
        ev_t = sb("ev_t", [P, 2, S])
        tile_t = [sb(f"tile_t{i}", [P, S]) for i in range(2)]
        gates_n = sb("gates_n", [P, TB, 48])
        table = sb("table", [BUCKETS + 1, HN])
        w2k = sb("w2k", [P, 2, DH], at=arena + 5 * K16 + 8192)
        w2v = sb("w2v", [P, 2, DH], at=arena + 5 * K16 + 8704)
        hid = sb("hid", [P, 2, GN * NCMP], at=arena + 5 * K16 + 9216)
        onehot = sb("onehot", [BUCKETS + 1, OH_W], at=t1 + 4096)
        bias_rev_sb = sb("bias_rev_sb", [HN, 640], at=t1 + 4096 + 4 * OH_W)
        bias_fwd_sb = sb("bias_fwd_sb", [P, 8, HN], at=t1 + 4096 + 4 * OH_W + 2560)
        gq_s = sb("gq_s", [P, 1])
        kc = sb("kc", [P, 2, NCMP])
        vc = sb("vc", [NCMP, GN, DH])
        cmax = sb("cmax", [P, HN])
        csum = sb("csum", [P, HN])
        rmax = sb("rmax", [P, 2, TB])
        rneg = sb("rneg", [P, 2, TB])
        rsum = sb("rsum", [P, 2, TB])
        rgate = sb("rgate", [P, TB])
        ps_g = ctx.enter_context(nc.psum_tensor("ps_g", [P, 2, 512], F32))
        ps_z = ctx.enter_context(nc.psum_tensor("ps_z", [P, 1536], F32))
        ps_t = ctx.enter_context(nc.psum_tensor("ps_t", [P, 1536], F32))

        ident = cst[:, C_ID:C_ID + P]

        def col(v, k):
            return vec[:, v + k:v + k + 1]

        def row_picker(i, rows_):
            at = C_STRIP + 39 - i
            return cst[:, at:at + rows_]

        def spread(i, k, m=P):
            return cst[0:k, C_ID + i:C_ID + i + 1].broadcast_to([k, m])

        const_in = sem("const_in")
        x_in = sem("x_in")
        vec_in = sem("vec_in")
        raw_landed = [sem(f"raw_landed{i}") for i in range(2)]
        hi_done = sem("hi_done")
        lo_done = sem("lo_done")
        tile_ready = sem("tile_ready")
        tile_free = [sem(f"tile_free{i}") for i in range(2)]
        ev_act = sem("ev_act")
        ev_dve = sem("ev_dve")
        act_order = sem("act_order")
        dve_order = sem("dve_order")
        pool_order = sem("pool_order")
        vec_t = sem("vec_t")
        vec_ready = sem("vec_ready")
        ones_ready = sem("ones_ready")
        sq_done = sem("sq_done")
        var_ready = sem("var_ready")
        std_ready = sem("std_ready")
        xn_ready = sem("xn_ready")
        gates_t = sem("gates_t")
        gate_act = sem("gate_act")
        gate_dve = sem("gate_dve")
        u_ready = sem("u_ready")
        u_t = sem("u_t")
        u_col_ready = sem("u_col_ready")
        a_scores = sem("a_scores")
        a_decay = sem("a_decay")
        a_masked = sem("a_masked")
        a_probs = sem("a_probs")
        a_pv = sem("a_pv")
        a_num = sem("a_num")
        a_ssq = sem("a_ssq")
        a_fin_d = sem("a_fin_d")
        a_fin_a = sem("a_fin_a")
        a_scale = sem("a_scale")
        a_bc = sem("a_bc")
        a_y = sem("a_y")
        b_sq = sem("b_sq")
        b_stat = sem("b_stat")
        b_var = sem("b_var")
        b_std = sem("b_std")
        b_rstd = sem("b_rstd")
        b_bc = sem("b_bc")
        b_normed = sem("b_normed")
        b_z = sem("b_z")
        b_ln = sem("b_ln")
        b_sp = sem("b_sp")
        b_later = sem("b_later")
        b_sfx = sem("b_sfx")
        b_min = sem("b_min")
        b_attn = sem("b_attn")
        b_pv = sem("b_pv")
        b_out = sem("b_out")
        nsa_in = sem("nsa_in")
        oh_mm = sem("oh_mm")
        oh_cp = sem("oh_cp")
        bias_out = sem("bias_out")
        w1_in = sem("w1_in")
        cmp_ready = sem("cmp_ready")
        hid_mm = sem("hid_mm")
        hid_ready = sem("hid_ready")
        kvc_mm = sem("kvc_mm")
        kvc_ready = sem("kvc_ready")
        cb_mm = sem("cb_mm")
        cb_ready = sem("cb_ready")
        c_scores = sem("c_scores")
        c_log = sem("c_log")
        c_exp = sem("c_exp")
        c_t = sem("c_t")
        c_tc = sem("c_tc")
        c_pv = sem("c_pv")
        c_gate = sem("c_gate")
        c_out = sem("c_out")
        bias_in = [sem(f"bias_in{i}") for i in range(2)]
        s_scores = sem("s_scores")
        s_max = sem("s_max")
        s_probs = sem("s_probs")
        s_t = sem("s_t")
        s_ta = sem("s_ta")
        s_td = sem("s_td")
        s_pv = sem("s_pv")
        s_out = sem("s_out")
        gain_in = sem("gain_in")
        out_ready = sem("out_ready")
        out_done = sem("out_done")

        W, NW = a["w_in"], a["nsa_w_in"]
        slabs = []

        def add(kind, mat, col0, n, row0=0, w=SLAB):
            first = len(slabs)
            for i in range(n):
                slabs.append((mat, row0, col0 + i * w, w, kind, i))
            return first

        N_QA = add("conv", W, QA, 4)
        N_IF = add("if", W, IF, 1, w=16)
        N_VA = add("va", W, VA, 4)
        N_QB = add("qb", W, QB, 8)
        N_VB = add("vb", W, VB, 4)
        N_OA = add("oa", W, OA, 4)
        N_GA = add("ga", W, GA, 4)
        N_GB = add("gb", W, GB, 4)
        N_WO = add("wo", a["w_out"], 0, 4)
        N_MLP = len(slabs)
        for quarter in range(4):
            add("up", a["w_up"], quarter * D, 4)
            add("down", a["w_down"], 0, 4, row0=quarter * D)
        N_NQ = add("nq", NW, NQ, 4)
        N_KC = add("nkc", NW, NKC, 1)
        N_VC = add("nvc", NW, NVC, 1)
        N_KS = add("nks", NW, NKS, 1)
        N_VS = add("nvs", NW, NVS, 1)
        N_KW = add("nkw", NW, NKW, 1)
        N_VW = add("nvw", NW, NVW, 1)
        N_NG = add("ng", NW, NG, 1, w=48)
        N_NZ = add("nz", NW, NZ, 12)
        N_NO = add("no", a["nsa_w_out"], 0, 4)
        N_ALL = len(slabs)
        MLP_SLABS = 8

        FEATURE = {"conv", "qb", "oa", "ga", "gb", "up", "nq", "nkc", "nvc", "nks", "nkw"}
        BY_ACT = {"norm": 1, "oa": 1, "ga": 1, "gb": 2, "up": 2, "nz": 1}
        BY_DVE = {"conv": 1, "gb": 1, "up": 1}
        norm_before = {N_QA, N_MLP, N_NQ, N_NO}
        tile_of, norm_tile_of, kinds = {}, {}, []
        for n in range(N_ALL):
            if n in norm_before:
                norm_tile_of[n] = len(kinds)
                kinds += ["norm"] * KT
            tile_of[n] = len(kinds)
            kinds += [slabs[n][4]] * (2 if slabs[n][4] in FEATURE else 4)
        tile_of[N_ALL] = len(kinds)
        act_count, dve_count = [0], [0]
        for kind in kinds:
            act_count.append(act_count[-1] + BY_ACT.get(kind, 0))
            dve_count.append(dve_count[-1] + BY_DVE.get(kind, 0))
        MLP_TILES = tile_of[N_MLP + MLP_SLABS] - tile_of[N_MLP]

        def tiles_of(n):
            return 2 if slabs[n][4] in FEATURE else 4

        def end_tile(n):
            return tile_of[n] + tiles_of(n)

        def wait_tile_free(eng, t, r=0):
            eng.wait_ge(tile_free[t % 2], t // 2 + 1 + MLP_TILES // 2 * r)

        def split_hi(act, n, r=0):
            if n >= N_ALL:
                return
            b, w = n % 2, slabs[n][3]
            act.wait_ge(raw_landed[b], 16 * (n // 2 + 1) + 16 * (MLP_SLABS // 2) * r)
            if n >= 2:
                act.wait_ge(tile_ready, tile_of[n - 1] + MLP_TILES * r)
            nc.scalar.activation(w_hi[b][:, :, 0:w], w_raw[b][:, :, 0:w], ACT.Copy).then_inc(hi_done, 1)

        def split_lo(dve, n, r=0):
            if n >= N_ALL:
                return
            b, w = n % 2, slabs[n][3]
            dve.wait_ge(hi_done, n + 1 + MLP_SLABS * r)
            nc.vector.tensor_tensor(w_lo[b][:, :, 0:w], w_raw[b][:, :, 0:w],
                                    w_hi[b][:, :, 0:w].bitcast(F32), ALU.subtract).then_inc(lo_done, 1)

        def mm_tile(pe, n, i, first_tile=None, hi=act_hi, lo=act_lo, r=0):
            t, kind = tile_of[n] + i, slabs[n][4]
            b, w = n % 2, slabs[n][3]
            pe.wait_ge(lo_done, n + 1 + MLP_SLABS * r)
            wait_tile_free(pe, t - 2, r)
            m = slice(i * P, (i + 1) * P)
            for k in range(KT):
                if first_tile is not None and i == 0:
                    wait_tile_free(pe, first_tile + k, r)
                if kind in FEATURE:
                    o = ps_g[:, t % 2, :]
                    three = ((w_hi[b][:, k, m], hi[:, k, :]), (w_hi[b][:, k, m], lo[:, k, :]),
                             (w_lo[b][:, k, m], hi[:, k, :]))
                else:
                    o = ps_g[:, t % 2, 0:w]
                    three = ((hi[:, k, m], w_hi[b][:, k, 0:w]), (hi[:, k, m], w_lo[b][:, k, 0:w]),
                             (lo[:, k, m], w_hi[b][:, k, 0:w]))
                for j, (stationary, moving) in enumerate(three):
                    mm = nc.tensor.matmul(o, stationary, moving, start=(k == 0 and j == 0),
                                          stop=(k == KT - 1 and j == 2))
            mm.then_inc(tile_ready, 1)

        def mm_slab(pe, n, first_tile=None, hi=act_hi, lo=act_lo, r=0):
            for i in range(tiles_of(n)):
                mm_tile(pe, n, i, first_tile, hi, lo, r)

        def transposed_tiles(pe, n, src):
            for k in range(KT):
                t = norm_tile_of[n] + k
                if t >= 2:
                    wait_tile_free(pe, t - 2)
                for b in range(TB):
                    mm = nc.tensor.transpose(ps_g[:, t % 2, b * P:(b + 1) * P],
                                             src[:, b, k * P:(k + 1) * P], ident)
                mm.then_inc(tile_ready, 1)

        def tile_done(eng, t, r=0):
            eng.wait_ge(tile_ready, t + 1 + MLP_TILES * r)

        def after_act(eng, t, k, r=0):
            eng.wait_ge(ev_act, act_count[t] + k + ACT_ROUND * r)

        def after_dve(eng, t, k, r=0):
            eng.wait_ge(ev_dve, dve_count[t] + k + DVE_ROUND * r)

        m0, m1 = tile_of[N_MLP], tile_of[N_MLP + MLP_SLABS]
        ACT_ROUND = act_count[m1] - act_count[m0]
        DVE_ROUND = dve_count[m1] - dve_count[m0]

        def act_norm_tile(act, n, k, gain):
            t = norm_tile_of[n] + k
            tile_done(act, t)
            scale = 1.0 if gain is None else col(gain, k)
            nc.scalar.activation(act_hi[:, k, :], ps_g[:, t % 2, :], ACT.Copy,
                                 scale=scale).then_inc(ev_act, 1)

        def dve_norm_tile(dve, n, k, gain):
            t = norm_tile_of[n] + k
            after_act(dve, t, 1)
            if gain is None:
                ins = nc.vector.tensor_tensor(act_lo[:, k, :], ps_g[:, t % 2, :],
                                              act_hi[:, k, :].bitcast(F32), ALU.subtract)
            else:
                ins = nc.vector.scalar_tensor_tensor(act_lo[:, k, :], ps_g[:, t % 2, :], col(gain, k),
                                                     act_hi[:, k, :].bitcast(F32), ALU.mult,
                                                     ALU.subtract)
            ins.then_inc(tile_free[t % 2], 1)

        def act_evacuate(act, n, i, r=0):
            kind, s = slabs[n][4], slabs[n][5]
            t = tile_of[n] + i
            g, free = t % 2, tile_free[t % 2]
            f = 2 * s + i
            cols = slice(s * SLAB, (s + 1) * SLAB)
            if kind == "conv":
                after_dve(act, t, 1)
                nc.scalar.activation(qk_a[:, f, :], conv_t[:, g, :], ACT.Silu).then_inc(free, 1)
                return
            if kind in ("if", "wo", "down", "no"):
                return
            tile_done(act, t, r)
            if kind in ("va", "vb"):
                dst = v_a if kind == "va" else v_b
                nc.scalar.copy(dst[:, i, cols], ps_g[:, g, 0:SLAB]).then_inc(free, 1)
            elif kind == "qb":
                dst = q_b[:, f, :] if f < HB else k_b[:, f - HB, :]
                nc.scalar.copy(dst, ps_g[:, g, :]).then_inc(free, 1)
            elif kind == "oa":
                nc.scalar.activation(ev_t[:, g, :], ps_g[:, g, :], ACT.Sigmoid).then_inc(ev_act, 1)
            elif kind in ("ga", "gb"):
                bias = col(V_BGATE, f + (8 if kind == "gb" else 0))
                nc.scalar.activation(ev_t[:, g, :], ps_g[:, g, :], ACT.Sigmoid,
                                     bias=bias).then_inc(ev_act, 1)
                if kind == "gb":
                    after_dve(act, t, 1)
                    nc.scalar.copy(y_hi[:, f, :], ev_t[:, g, :]).then_inc(ev_act, 1)
            elif kind == "up":
                nc.scalar.activation(ev_t[:, g, :], ps_g[:, g, :], ACT.Relu).then_inc(ev_act, 1)
                after_dve(act, t, 1, r)
                nc.scalar.copy(up_hi[:, f, :], relu_t[:, g, :]).then_inc(ev_act, 1)
            elif kind == "nq":
                half = f // 2 % 2
                for e in range(2):
                    dst = qn[64 * half:64 * half + 64, 4 * (f // 4) + (2 * f + e) % 4, :]
                    ins = nc.scalar.mul(dst, ps_g[64 * e:64 * e + 64, g, :], DH ** -0.5)
                ins.then_inc(free, 1)
            elif kind in ("nkc", "nvc"):
                pair = pairk if kind == "nkc" else pairv
                for e in range(2):
                    src = ps_g[64 * e:64 * e + 64, g, :]
                    nc.scalar.copy(pair[0:64, 2 * i + e, :], src)
                    ins = nc.scalar.copy(pair[64:128, 2 * i + e, 0:S - 1], src[:, 1:S])
                ins.then_inc(free, 1)
            elif kind in ("nks", "nkw"):
                dst = ks if kind == "nks" else kw
                nc.scalar.copy(dst[:, i, :], ps_g[:, g, :]).then_inc(free, 1)
            elif kind in ("nvs", "nvw"):
                dst = vs if kind == "nvs" else vw
                nc.scalar.copy(dst[:, i, :], ps_g[:, g, 0:SLAB]).then_inc(free, 1)
            elif kind == "ng":
                nc.scalar.activation(gates_n[:, i, :], ps_g[:, g, 0:48], ACT.Sigmoid).then_inc(free, 1)
            elif kind == "nz":
                nc.scalar.activation(ev_t[:, g, 0:SLAB], ps_g[:, g, 0:SLAB],
                                     ACT.Silu).then_inc(ev_act, 1)

        def dve_evacuate(dve, order, n, i, r=0):
            kind, s = slabs[n][4], slabs[n][5]
            t = tile_of[n] + i
            g, free = t % 2, tile_free[t % 2]
            f = 2 * s + i
            cols = slice(s * SLAB, (s + 1) * SLAB)
            ps = ps_g[:, g, :]
            if kind == "conv":
                tile_done(dve, t)
                y = conv_t[:, g, :]
                order.link(nc.vector.tensor_scalar(y, ps, col(V_CONV, 24 + f), None, ALU.mult))
                for back in (1, 2, 3):
                    w = col(V_CONV, 8 * (3 - back) + f)
                    ins = nc.vector.scalar_tensor_tensor(y[:, back:S], ps[:, 0:S - back], w,
                                                         y[:, back:S], ALU.mult, ALU.add)
                    if back < 3:
                        order.link(ins)
                ins.then_inc(ev_dve, 1)
            elif kind == "if":
                tile_done(dve, t)
                nc.vector.tensor_tensor(gate_pre[:, i, :], ps[:, 0:16], bif_bc[:], ALU.add)\
                    .then_inc(free, 1)
            elif kind in ("oa", "ga"):
                after_act(dve, t, 1)
                nc.vector.tensor_tensor(y_f[:, f, :], y_f[:, f, :], ev_t[:, g, :], ALU.mult)\
                    .then_inc(free, 1)
            elif kind == "gb":
                after_act(dve, t, 1)
                order.link(nc.vector.tensor_tensor(ev_t[:, g, :], ev_t[:, g, :], yb_f[:, f, :], ALU.mult))
                nc.vector.tensor_tensor(ev_t[:, g, :], ev_t[:, g, :], y_f[:, f, :], ALU.add)\
                    .then_inc(ev_dve, 1)
                after_act(dve, t, 2)
                nc.vector.tensor_tensor(y_lo[:, f, :], ev_t[:, g, :], y_hi[:, f, :].bitcast(F32),
                                        ALU.subtract).then_inc(free, 1)
            elif kind == "up":
                after_act(dve, t, 1, r)
                nc.vector.tensor_tensor(relu_t[:, g, :], ev_t[:, g, :], ps, ALU.mult)\
                    .then_inc(ev_dve, 1)
                after_act(dve, t, 2, r)
                nc.vector.tensor_tensor(up_lo[:, f, :], relu_t[:, g, :], up_hi[:, f, :].bitcast(F32),
                                        ALU.subtract).then_inc(free, 1)
            elif kind in ("wo", "down"):
                tile_done(dve, t, r)
                nc.vector.tensor_tensor(x_sb[:, i, cols], x_sb[:, i, cols], ps[:, 0:SLAB], ALU.add)\
                    .then_inc(free, 1)
            elif kind == "nz":
                after_act(dve, t, 1)
                branch, c = s // 4, slice(s % 4 * SLAB, (s % 4 + 1) * SLAB)
                e = ev_t[:, g, 0:SLAB]
                if branch == 0:
                    nc.vector.tensor_tensor(o_a[:, i, c], o_a[:, i, c], e, ALU.mult).then_inc(free, 1)
                else:
                    o = o_b if branch == 1 else o_c
                    order.link(nc.vector.tensor_tensor(e, e, o[:, i, c], ALU.mult))
                    nc.vector.tensor_tensor(o_a[:, i, c], o_a[:, i, c], e, ALU.add).then_inc(free, 1)
            elif kind == "no":
                tile_done(dve, t)
                nc.vector.tensor_copy(y2[:, i, cols], ps[:, 0:SLAB]).then_inc(free, 1)

        def act_norm(act, which, src, scratch, before):
            before()
            for b in range(TB):
                nc.scalar.activation(scratch[:, b, :], src[:, b, :], ACT.Square,
                                     accum_out=ssq[:, which, b:b + 1]).then_inc(sq_done, 1)
            act.wait_ge(var_ready, which + 1)
            nc.scalar.activation(rstd[:, which, :], ssq[:, which, :], ACT.Sqrt).then_inc(std_ready, 1)

        def dve_norm(dve, order, which, src, scratch):
            dve.wait_ge(sq_done, TB * (which + 1))
            nc.vector.tensor_scalar(ssq[:, which, :], ssq[:, which, :], 1.0 / D, EPS, ALU.mult,
                                    ALU.add).then_inc(var_ready, 1)
            dve.wait_ge(std_ready, which + 1)
            order.link(nc.vector.reciprocal(rstd[:, which, :], rstd[:, which, :]))
            if src is not None:
                for b in range(TB):
                    nc.vector.tensor_scalar(scratch[:, b, :], src[:, b, :], rstd[:, which, b:b + 1],
                                            None, ALU.mult).then_inc(xn_ready, 1)

        block = ctx.enter_context(nc.Block())

        @block.sync
        def _(sp):
            def load_slab(n):
                mat, row0, col0, w, _, _ = slabs[n]
                if n >= 2:
                    sp.wait_ge(lo_done, n - 1)
                sp.dma_start(w_raw[n % 2][:, :, 0:w],
                             mat[row0:row0 + D, col0:col0 + w].rearrange("(k p) n -> p k n", p=P))\
                    .then_inc(raw_landed[n % 2], 16)

            sp.dma_start(cst[:], a["cst"]).then_inc(const_in, 16)
            x_rows = a["x"].rearrange("(b p) n -> p b n", p=P)
            for b in range(TB):
                sp.dma_start(x_sb[:, b, :], x_rows[:, b, :]).then_inc(x_in, 16)
            for n in range(N_MLP):
                load_slab(n)
            down_rows = a["w_down"].rearrange("(q k p) n -> p q k n", k=KT, p=P)
            up_cols = a["w_up"].rearrange("(k p) n -> p k n", p=P)
            with sp.Fori(0, 4) as r:
                for j in range(MLP_SLABS):
                    n = N_MLP + j
                    sp.wait_ge(lo_done, MLP_SLABS * r + (n - 1))
                    if j < 4:
                        src = up_cols[:, :, bass.ds(r * D + j * SLAB, SLAB)]
                    else:
                        src = down_rows[:, bass.ds(r, 1), :, (j - 4) * SLAB:(j - 3) * SLAB]
                        src = src.rearrange("p q k n -> p (q k) n")
                    sp.dma_start(w_raw[n % 2][:], src).then_inc(raw_landed[n % 2], 16)
            for n in range(N_NQ, N_ALL):
                if n == N_KC:
                    wait_tile_free(sp, tile_of[N_NQ] - 1)
                    for dst, name in ((w1k, "nsa_cmp_k_w1"), (w1v, "nsa_cmp_v_w1")):
                        sp.dma_start(dst[:], a[name].rearrange("(k p) n -> p k n", p=P))\
                            .then_inc(w1_in, 16)
                    for dst, name in ((w2k, "nsa_cmp_k_w2"), (w2v, "nsa_cmp_v_w2")):
                        sp.dma_start(dst[:], a[name].rearrange("(k p) n -> p k n", p=P))\
                            .then_inc(w1_in, 16)
                load_slab(n)
            sp.wait_ge(s_pv, 32)
            sp.dma_start(gain_bc[:], a["post_gain"].partition_broadcast(P)).then_inc(gain_in, 16)
            out_rows = out.rearrange("(b p) n -> p b n", p=P)
            for b in range(TB):
                sp.wait_ge(out_ready, b + 1)
                sp.dma_start(out_rows[:, b, :], xo[:, b, :]).then_inc(out_done, 16)
            sp.wait_ge(out_done, 16 * TB)

        @block.tensor
        def _(pe):
            pe.wait_ge(const_in, 16)
            pe.wait_ge(vec_in, 16 * N_VEC)
            nc.tensor.transpose(ps_t[:, 0:V_ROWS], vec_rows[:], ident[0:V_ROWS, 0:V_ROWS]).then_inc(vec_t, 1)

            pe.wait_ge(nsa_in, 32)
            nc.tensor.matmul(ps_t[0:HN, 512:1024], table[:], onehot[:, OH_REV:OH_REV + 512],
                             start=True, stop=True)
            nc.tensor.matmul(ps_t[0:HN, 1024:1152], table[:], onehot[:, OH_REV + 512:OH_REV + 640],
                             start=True, stop=True)
            for c in range(8):
                mm = nc.tensor.matmul(ps_t[:, 1152 + HN * c:1152 + HN * (c + 1)],
                                      onehot[:, c * P:(c + 1) * P], table[:], start=True, stop=True)
            mm.then_inc(oh_mm, 1)

            pe.wait_ge(xn_ready, TB)
            transposed_tiles(pe, N_QA, xn)
            for n in range(N_QA, N_QA + 4):
                mm_slab(pe, n, norm_tile_of[N_QA] if n == N_QA else None)
            mm_slab(pe, N_IF)
            mm_slab(pe, N_VA)
            wait_tile_free(pe, end_tile(N_IF) - 2)
            wait_tile_free(pe, end_tile(N_IF) - 1)
            pe.wait_ge(oh_cp, 2)
            for c in range(2):
                for b in range(TB):
                    mm = nc.tensor.transpose(ps_t[0:HA, c * 512 + b * P:c * 512 + (b + 1) * P],
                                             gate_pre[:, b, c * HA:(c + 1) * HA], ident)
            mm.then_inc(gates_t, 1)
            mm_slab(pe, N_VA + 1)
            mm_slab(pe, N_VA + 2)
            pe.wait_ge(u_ready, 1)
            for b in range(TB):
                mm = nc.tensor.transpose(ps_t[:, 1024 + b * HA:1024 + (b + 1) * HA],
                                         rows[3][:, b * P:(b + 1) * P], ident[0:HA, 0:HA])
            mm.then_inc(u_t, 1)
            mm_slab(pe, N_VA + 3)

            for h in range(HA):
                n, half, ft = N_QB + h, 64 * (h % 2), h // 2
                if h == 0:
                    pe.wait_ge(gate_dve, 2)
                    pe.wait_ge(u_col_ready, 1)
                    pe.wait_ge(gate_act, 2)
                    wait_tile_free(pe, end_tile(N_QA + 3) - 2)
                    wait_tile_free(pe, end_tile(N_QA + 3) - 1)
                else:
                    pe.wait_ge(a_probs, h)
                nc.tensor.matmul(ps_t[:, 0:512], spread(h, HA), rows[0][:], start=True, stop=True)
                for b in range(TB):
                    at, w = CAUSAL_AT[b], CAUSAL_W[b]
                    mm = nc.tensor.matmul(ps_z[:, at:at + w], qk_a[half:half + 64, 4 + ft, b * P:(b + 1) * P],
                                          qk_a[half:half + 64, ft, b * P:S], start=True, stop=True)
                mm.then_inc(a_scores, 1)
                mm_tile(pe, n, 0)
                pe.wait_ge(a_probs, h + 1)
                if h == 0:
                    wait_tile_free(pe, end_tile(N_VA + 3) - 2)
                    wait_tile_free(pe, end_tile(N_VA + 3) - 1)
                else:
                    pe.wait_ge(a_num, h)
                for b in range(TB):
                    at, w = CAUSAL_AT[b], CAUSAL_W[b]
                    nc.tensor.matmul(ps_t[:, 512 + b * P:1024], v_a[:, b, h * P:(h + 1) * P],
                                     decay[:, at:at + w], start=(b == 0), stop=(b == TB - 1))
                for b in range(TB):
                    at, w = CAUSAL_AT[b], CAUSAL_W[b]
                    mm = nc.tensor.matmul(ps_t[0:40, 1024 + b * P:1536], row_picker(h, 40),
                                          decay[:, at:at + w], start=(h == 0 and b == 0), stop=False)
                mm.then_inc(a_pv, 1)
                mm_tile(pe, n, 1)
                pe.wait_ge(a_num, h + 1)
                nc.tensor.matmul(ps_t[0:40, 1024:1536], row_picker(32 + h, 40), num_sq[:],
                                 start=False, stop=(h == HA - 1)).then_inc(a_ssq, 1)

            for j in range(16):
                n = N_VB + j // 4
                mm_tile(pe, n, j % 4)
                for i in (2 * j, 2 * j + 1):
                    if j >= 8:
                        break
                    pe.wait_ge(b_sq, i + 1)
                    nc.tensor.matmul(ps_z[0:16, 0:512], row_picker(i, 16), sqs[:, i % 2, :],
                                     start=(i == 0), stop=(i == 15)).then_inc(b_stat, 1)
                if j >= 8:
                    if j == 8:
                        pe.wait_ge(b_rstd, 1)
                        pe.wait_ge(a_scale, 1)
                    for i in (2 * (j - 8), 2 * (j - 8) + 1):
                        if i >= 2:
                            pe.wait_ge(b_normed, i - 1)
                        at = 512 * (1 + i % 2)
                        nc.tensor.matmul(ps_z[:, at:at + 512], spread(i, 16), stat_row[:],
                                         start=True, stop=True).then_inc(b_bc, 1)
                    h = j - 8
                    if h >= 2:
                        pe.wait_ge(a_y, h - 1)
                    nc.tensor.matmul(ps_t[:, 512 * (h % 2):512 * (h % 2) + 512], spread(h, HA),
                                     rows[2][:], start=True, stop=True).then_inc(a_bc, 1)

            for h in range(HB):
                n = N_OA + h
                if h == 0:
                    pe.wait_ge(b_normed, 16)
                else:
                    pe.wait_ge(b_attn, h)
                for b in (0, 1, 3, 2):
                    at, w = CAUSAL_AT[b], CAUSAL_W[b]
                    mm = nc.tensor.matmul(ps_z[:, at:at + w], k_b[:, h, b * P:(b + 1) * P],
                                          q_b[:, h, b * P:S], start=(b != 3), stop=True,
                                          skip_group_check=True)
                mm.then_inc(b_z, 1)
                mm_tile(pe, n, 0)
                pe.wait_ge(b_later, h + 1)
                for b in range(TB):
                    at, w = CAUSAL_AT[b], CAUSAL_W[b]
                    mm = nc.tensor.matmul(ps_z[:, at:at + w], cst[:, C_TRI:C_TRI + P], sp_t[:, at:at + w],
                                          start=False, stop=True, skip_group_check=True)
                    if b < 3:
                        later = (later0[:], later1[:], sp_t[:, CAUSAL_AT[3]:CAUSAL_AT[3] + P])[b]
                        mm = nc.tensor.matmul(ps_z[:, at + P:at + w], cst[:, C_NEG:C_NEG + P], later,
                                              start=False, stop=True, skip_group_check=True)
                mm.then_inc(b_sfx, 1)
                mm_tile(pe, n, 1)
                pe.wait_ge(b_attn, h + 1)
                if h >= 2:
                    pe.wait_ge(b_out, h - 1)
                if h == 0:
                    wait_tile_free(pe, end_tile(N_VB + 3) - 2)
                    wait_tile_free(pe, end_tile(N_VB + 3) - 1)
                    pe.wait_ge(a_y, HA)
                o = 512 * (h % 2)
                for b in range(TB):
                    at, w = CAUSAL_AT[b], CAUSAL_W[b]
                    mm = nc.tensor.matmul(ps_t[:, o + b * P:o + 512], v_b[:, b, h * P:(h + 1) * P],
                                          attn_b[:, at:at + w], start=(b == 0), stop=(b == TB - 1))
                mm.then_inc(b_pv, 1)
            for n in range(N_GB, N_GB + 4):
                mm_slab(pe, n)
            for n in range(N_WO, N_WO + 4):
                mm_slab(pe, n, tile_of[N_GB] if n == N_WO else None, y_hi, y_lo)

            pe.wait_ge(xn_ready, 2 * TB)
            transposed_tiles(pe, N_MLP, xn2)
            for k in range(KT):
                wait_tile_free(pe, norm_tile_of[N_MLP] + k)
            with pe.Fori(0, 4) as r:
                for j in range(4):
                    mm_slab(pe, N_MLP + j, r=r)
                for j in range(4, MLP_SLABS):
                    mm_slab(pe, N_MLP + j, tile_of[N_MLP] if j == 4 else None, up_hi, up_lo, r=r)

            pe.wait_ge(xn_ready, 3 * TB)
            transposed_tiles(pe, N_NQ, xn2)
            for n in range(N_NQ, N_VS + 1):
                mm_slab(pe, n, norm_tile_of[N_NQ] if n == N_NQ else None)

            def compress(which, w1, at):
                pe.wait_ge(cmp_ready, which + 1)
                pe.wait_ge(w1_in, 64)
                if which == 0:
                    pe.wait_ge(b_out, HB)
                    pe.wait_ge(b_attn, HB)
                else:
                    pe.wait_ge(hid_ready, 1)
                for m in range(2):
                    for k in range(16):
                        mm = nc.tensor.matmul(ps_t[:, m * 512:m * 512 + GN * NCMP],
                                              w1[:, k, m * P:(m + 1) * P], cmp_in[:, k, :],
                                              start=(k == 0), stop=(k == 15))
                mm.then_inc(hid_mm, 1)

            compress(0, w1k, 0)
            mm_slab(pe, N_KW)
            pe.wait_ge(hid_ready, 1)
            for g in range(GN):
                half = 64 * (g % 2)
                for m in range(2):
                    mm = nc.tensor.matmul(ps_z[half:half + 64, g // 2 * NCMP:(g // 2 + 1) * NCMP],
                                          w2k[:, m, :], hid[:, m, g * NCMP:(g + 1) * NCMP],
                                          start=(m == 0), stop=(m == 1))
            mm.then_inc(kvc_mm, 1)
            mm_slab(pe, N_VW)
            compress(1, w1v, 0)
            mm_slab(pe, N_NG)
            pe.wait_ge(hid_ready, 2)
            for g in range(GN):
                for m in range(2):
                    mm = nc.tensor.matmul(ps_z[0:NCMP, 512 + g * DH:512 + (g + 1) * DH],
                                          hid[:, m, g * NCMP:(g + 1) * NCMP], w2v[:, m, :],
                                          start=(m == 0), stop=(m == 1))
            mm.then_inc(kvc_mm, 1)

            pe.wait_ge(kvc_ready, 2)
            for b in range(TB):
                if b:
                    pe.wait_ge(c_log, b)
                for h in range(HN):
                    g, half = h // 4, 64 * (h // 4 % 2)
                    at = 512 * (g % 2) + (4 * (g // 2) + h % 4) * NCMP
                    mm = nc.tensor.matmul(ps_z[:, at:at + NCMP],
                                          qn[half:half + 64, 4 * (g // 2) + h % 4, b * P:(b + 1) * P],
                                          kc[half:half + 64, g // 2, :], start=True, stop=True)
                mm.then_inc(c_scores, 1)
                pe.wait_ge(c_exp, b + 1)
                for e in range(2):
                    if 2 * b + e >= 1:
                        pe.wait_ge(c_tc, 2 * b + e)
                    for h in range(8):
                        mm = nc.tensor.transpose(ps_t[0:NCMP, h * P:(h + 1) * P], clog[:, 8 * e + h, :],
                                                 ident)
                    mm.then_inc(c_t, 1)
                pe.wait_ge(c_tc, 2 * b + 2)
                if b:
                    pe.wait_ge(c_out, b)
                for h in range(HN):
                    o = (ps_z if h < 8 else ps_t)[:, 1024 + h % 8 * DH:1024 + (h % 8 + 1) * DH]
                    mm = nc.tensor.matmul(o, cpt[:, h, :], vc[:, h // 4, :], start=True, stop=True)
                mm.then_inc(c_pv, 1)

            def unit(u):
                h = u % HN
                g = h // 4
                half = 64 * (g % 2)
                return h, g, half, (ks, kw)[u // HN], (vs, vw)[u // HN]

            def scores(u):
                h, g, half, keys, _ = unit(u)
                if u == 0:
                    pe.wait_ge(c_out, TB)
                else:
                    pe.wait_ge(s_max, u)
                for b in range(TB):
                    at, w = ROWS_AT[b], ROWS_W[b]
                    mm = nc.tensor.matmul(ps_z[:, at:at + w],
                                          qn[half:half + 64, 4 * (g // 2) + h % 4, b * P:(b + 1) * P],
                                          keys[half:half + 64, g // 2, 0:w], start=True, stop=True)
                mm.then_inc(s_scores, 1)

            scores(0)
            for u in range(32):
                h, g, half, _, values = unit(u)
                if u < 31:
                    scores(u + 1)
                pe.wait_ge(s_probs, u + 1)
                if u:
                    pe.wait_ge(s_ta, u)
                    pe.wait_ge(s_td, u)
                for b in range(TB):
                    for s in range(b + 1):
                        at = (b * (b + 1) // 2 + s) * P
                        if u and at == 1024:
                            pe.wait_ge(s_out, u)
                        mm = nc.tensor.transpose(ps_t[:, at:at + P],
                                                 probs[u % 2][:, ROWS_AT[b] + s * P:ROWS_AT[b] + (s + 1) * P],
                                                 ident)
                mm.then_inc(s_t, 1)
                mm_tile(pe, N_NZ + u // 4, u % 4)
                pe.wait_ge(s_ta, u + 1)
                pe.wait_ge(s_td, u + 1)
                if u:
                    pe.wait_ge(s_out, u)
                for b in range(TB):
                    for s in range(b + 1):
                        at = (b * (b + 1) // 2 + s) * P
                        mm = nc.tensor.matmul(ps_t[:, CAUSAL + b * DH:CAUSAL + (b + 1) * DH],
                                              probs_t[:, at:at + P], values[:, s, g * DH:(g + 1) * DH],
                                              start=(s == 0), stop=(s == b))
                mm.then_inc(s_pv, 1)
            for n in range(N_NZ + 8, N_NZ + 12):
                mm_slab(pe, n)
            wait_tile_free(pe, end_tile(N_NZ + 11) - 2)
            wait_tile_free(pe, end_tile(N_NZ + 11) - 1)
            transposed_tiles(pe, N_NO, o_a)
            for n in range(N_NO, N_NO + 4):
                mm_slab(pe, n, norm_tile_of[N_NO] if n == N_NO else None)

        @block.scalar
        def _(act):
            order = Order(act, act_order)
            for name, row0 in VEC_PARTS:
                r0, k = row0
                act.dma_start(vec_rows[r0:r0 + k, :], a[name]).then_inc(vec_in, 16)
            act.dma_start(bif_bc[:], a["b_if"].partition_broadcast(P)).then_inc(vec_in, 16)
            act.dma_start(table[:], a["table"]).then_inc(nsa_in, 16)
            act.dma_start(onehot[:], a["onehot"]).then_inc(nsa_in, 16)
            split_hi(act, 0)
            act_norm(act, 0, x_sb, xn, lambda: act.wait_ge(x_in, 16 * TB))
            act.wait_ge(vec_ready, 1)
            for k in range(KT):
                act_norm_tile(act, N_QA, k, V_MIX)
            for n in range(N_QA, N_QB):
                split_hi(act, n + 1)
                for i in range(tiles_of(n)):
                    act_evacuate(act, n, i)
                if n == N_VA:
                    act.wait_ge(gates_t, 1)
                    order.link(nc.scalar.activation(rows[0][:], ps_t[0:HA, 512:1024], ACT.Abs))
                    order.link(nc.scalar.activation(rows[0][:], rows[0][:], ACT.Exp, scale=-1.0))
                    nc.scalar.activation(rows[0][:], rows[0][:], ACT.Ln, bias=1.0).then_inc(gate_act, 1)
                if n == N_VA + 2:
                    act.wait_ge(gate_dve, 1)
                    nc.scalar.activation(rows[1][:], rows[1][:], ACT.Exp, scale=-1.0).then_inc(gate_act, 1)

            for h in range(HA):
                n = N_QB + h
                split_hi(act, n + 1)
                act.wait_ge(a_scores, h + 1)
                if h:
                    act.wait_ge(a_pv, h)
                for b in range(TB):
                    at, w = CAUSAL_AT[b], CAUSAL_W[b]
                    ins = nc.scalar.activation(decay[:, at:at + w], ps_t[:, b * P:512], ACT.Exp,
                                               bias=u_col[:, b, h:h + 1])
                ins.then_inc(a_decay, 1)
                act_evacuate(act, n, 0)
                act.wait_ge(a_pv, h + 1)
                nc.scalar.copy(y_f[:, h, :], ps_t[:, 512:1024])
                if h:
                    act.wait_ge(a_ssq, h)
                nc.scalar.activation(num_sq[:], ps_t[:, 512:1024], ACT.Square).then_inc(a_num, 1)
                act_evacuate(act, n, 1)

            for j in range(16):
                n = N_VB + j // 4
                if j % 4 == 0:
                    split_hi(act, n + 1)
                if j == 0:
                    act.wait_ge(a_ssq, HA)
                    nc.scalar.activation(rows[2][:], ps_t[0:HA, 1024:1536], ACT.Abs).then_inc(a_fin_a, 1)
                    nc.scalar.mul(rows[3][:], ps_t[32:32 + HA, 1024:1536], 1.0 / P).then_inc(a_fin_a, 1)
                    wait_tile_free(act, end_tile(N_QB + 7) - 1)
                if j < 8:
                    for i in (2 * j, 2 * j + 1):
                        if i >= 2:
                            act.wait_ge(b_stat, i - 1)
                        src = q_b[:, i, :] if i < HB else k_b[:, i - HB, :]
                        nc.scalar.activation(sqs[:, i % 2, :], src, ACT.Square).then_inc(b_sq, 1)
                if j == 6:
                    act.wait_ge(a_fin_d, 1)
                    nc.scalar.activation(rows[3][:], rows[3][:], ACT.Sqrt).then_inc(a_fin_a, 1)
                act_evacuate(act, n, j % 4)
                if j == 7:
                    act.wait_ge(b_var, 1)
                    nc.scalar.activation(stat_row[:], stat_row[:], ACT.Sqrt).then_inc(b_std, 1)

            for h in range(HB):
                n = N_OA + h
                split_hi(act, n + 1)
                act.wait_ge(b_z, h + 1)
                if h:
                    act.wait_ge(b_sfx, h)
                else:
                    act.wait_ge(b_normed, 16)
                z = ps_z[:, 0:CAUSAL]
                order.link(nc.scalar.activation(sp_t[:], z, ACT.Abs))
                order.link(nc.scalar.activation(sp_t[:], sp_t[:], ACT.Exp, scale=-1.0))
                nc.scalar.activation(sp_t[:], sp_t[:], ACT.Ln, bias=1.0).then_inc(b_ln, 1)
                act_evacuate(act, n, 0)
                act.wait_ge(b_min, h + 1)
                if h:
                    act.wait_ge(b_pv, h)
                nc.scalar.activation(attn_b[:], z, ACT.Exp).then_inc(b_attn, 1)
                act_evacuate(act, n, 1)
                act.wait_ge(b_pv, h + 1)
                nc.scalar.copy(yb_f[:, h, :], ps_t[:, 512 * (h % 2):512 * (h % 2) + 512]).then_inc(b_out, 1)
            for n in range(N_GB, N_MLP):
                split_hi(act, n + 1)
                for i in range(tiles_of(n)):
                    act_evacuate(act, n, i)

            def both_free(t):
                wait_tile_free(act, t - 2)
                wait_tile_free(act, t - 1)

            act_norm(act, 1, x_sb, xn2, lambda: both_free(end_tile(N_WO + 3)))
            for k in range(KT):
                act_norm_tile(act, N_MLP, k, V_MLP)
            with act.Fori(0, 4) as r:
                for j in range(MLP_SLABS):
                    split_hi(act, N_MLP + j + 1, r)
                    for i in range(tiles_of(N_MLP + j)):
                        act_evacuate(act, N_MLP + j, i, r)
            act_norm(act, 2, x_sb, xn2, lambda: both_free(end_tile(N_NQ - 1)))
            for k in range(KT):
                act_norm_tile(act, N_NQ, k, V_PRE)
            for n in range(N_NQ, N_NZ):
                split_hi(act, n + 1)
                if n == N_KC:
                    wait_tile_free(act, end_tile(N_NQ + 3) - 1)
                for i in range(tiles_of(n)):
                    act_evacuate(act, n, i)
                if n in (N_KW, N_NG):
                    pass
                if n in (N_VS, N_VW):
                    which = 0 if n == N_VS else 1
                    act.wait_ge(hid_mm, which + 1)
                    if which:
                        act.wait_ge(kvc_mm, 1)
                    for m in range(2):
                        ins = nc.scalar.activation(hid[:, m, :], ps_t[:, m * 512:m * 512 + GN * NCMP],
                                                   ACT.Silu)
                    ins.then_inc(hid_ready, 1)

            for b in range(TB):
                act.wait_ge(c_log, b + 1)
                nc.scalar.activation(clog[:], clog[:], ACT.Exp).then_inc(c_exp, 1)
                for e in range(2):
                    act.wait_ge(c_t, 2 * b + e + 1)
                    if b and e == 0:
                        act.wait_ge(c_pv, b)
                    nc.scalar.copy(cpt[:, 8 * e:8 * e + 8, :],
                                   ps_t[0:NCMP, 0:1024].rearrange("p (h t) -> p h t", t=P)).then_inc(c_tc, 1)

            def exps(u):
                act.wait_ge(s_max, u + 1)
                for b in range(TB):
                    p = probs[u % 2][:, ROWS_AT[b]:ROWS_AT[b] + ROWS_W[b]]
                    ins = nc.scalar.activation(p, p, ACT.Exp, bias=rneg[:, u % 2, b:b + 1],
                                               accum_out=rsum[:, u % 2, b:b + 1])
                ins.then_inc(s_probs, 1)

            exps(0)
            for u in range(32):
                if u % 4 == 0:
                    split_hi(act, N_NZ + u // 4 + 1)
                act.wait_ge(s_t, u + 1)
                if u:
                    act.wait_ge(s_pv, u)
                nc.scalar.copy(probs_t[:, 0:512], ps_t[:, 0:512]).then_inc(s_ta, 1)
                if u < 31:
                    exps(u + 1)
                act_evacuate(act, N_NZ + u // 4, u % 4)
            for n in range(N_NZ + 8, N_NO):
                split_hi(act, n + 1)
                for i in range(tiles_of(n)):
                    act_evacuate(act, n, i)
            for k in range(KT):
                act_norm_tile(act, N_NO, k, None)
            for n in range(N_NO, N_ALL):
                split_hi(act, n + 1)
            act_norm(act, 3, y2, xo, lambda: both_free(end_tile(N_ALL - 1)))

        @block.vector
        def _(dve):
            order = Order(dve, dve_order)
            order.link(nc.vector.memset(ones_row[:], 1.0))
            dve.wait_ge(vec_t, 1)
            nc.vector.tensor_copy(vec[:], ps_t[:, 0:V_ROWS]).then_inc(vec_ready, 1)
            dve.wait_ge(vec_ready, 1)
            order.link(nc.vector.tensor_scalar(gq_s[:], col(V_QN, 0), HD ** -0.5, None, ALU.mult))
            split_lo(dve, 0)
            dve_norm(dve, order, 0, x_sb, xn)
            dve.wait_ge(oh_mm, 1)
            nc.vector.tensor_copy(bias_rev_sb[:], ps_t[0:HN, 512:1152]).then_inc(oh_cp, 1)
            nc.vector.tensor_copy(bias_fwd_sb[:], ps_t[:, 1152:1152 + 8 * HN]
                                  .rearrange("p (c h) -> p c h", h=HN)).then_inc(oh_cp, 1)
            for k in range(KT):
                dve_norm_tile(dve, N_QA, k, V_MIX)
            for n in range(N_QA, N_QB):
                split_lo(dve, n + 1)
                for i in range(tiles_of(n)):
                    dve_evacuate(dve, order, n, i)
                if n == N_VA:
                    dve.wait_ge(gates_t, 1)
                    dve.wait_ge(bias_out, 32)
                    dve.wait_ge(gate_act, 1)
                    order.link(nc.vector.tensor_scalar(rows[1][:], ps_t[0:HA, 512:1024], 0.0, None, ALU.min))
                    order.link(nc.vector.tensor_tensor(rows[1][:], rows[1][:], rows[0][:], ALU.subtract))
                    order.link(nc.vector.tensor_tensor_scan(rows[2][:], ones_row[:], rows[1][:], 0.0,
                                                            ALU.mult, ALU.add))
                    nc.vector.tensor_tensor(rows[3][:], ps_t[0:HA, 0:512], rows[2][:], ALU.subtract)\
                        .then_inc(u_ready, 1)
                    dve.wait_ge(u_ready, 1)
                    order.link(nc.vector.tensor_tensor_scan(rows[0][:], rows[3][:], rows[3][:], 0.0,
                                                            ALU.max, ALU.max))
                    nc.vector.tensor_tensor(rows[1][:], rows[2][:], rows[0][:], ALU.add).then_inc(gate_dve, 1)
                    nc.vector.tensor_scalar(rows[0][:], rows[0][:], -1.0, None, ALU.mult).then_inc(gate_dve, 1)
                if n == N_VA + 2:
                    dve.wait_ge(u_t, 1)
                    nc.vector.tensor_copy(u_col[:], ps_t[:, 1024:1024 + TB * HA]
                                          .rearrange("p (b h) -> p b h", h=HA)).then_inc(u_col_ready, 1)

            for h in range(HA):
                split_lo(dve, N_QB + h + 1)
                dve.wait_ge(a_masked, h + 1)
                nc.vector.scalar_tensor_tensor(decay[:], ps_z[:, 0:CAUSAL], DQK ** -0.5, decay[:], ALU.mult,
                                               ALU.mult).then_inc(a_probs, 1)

            for j in range(16):
                n = N_VB + j // 4
                if j % 4 == 0:
                    split_lo(dve, n + 1)
                if j == 0:
                    dve.wait_ge(a_fin_a, 2)
                    order.link(nc.vector.tensor_tensor(rows[2][:], rows[2][:], rows[1][:], ALU.max))
                    order.link(nc.vector.reciprocal(rows[2][:], rows[2][:]))
                    order.link(nc.vector.tensor_tensor(rows[3][:], rows[3][:], rows[2][:], ALU.mult))
                    order.link(nc.vector.tensor_tensor(rows[3][:], rows[3][:], rows[2][:], ALU.mult))
                    nc.vector.tensor_scalar(rows[3][:], rows[3][:], EPS, None, ALU.add).then_inc(a_fin_d, 1)
                if j == 7:
                    dve.wait_ge(a_fin_a, 3)
                    order.link(nc.vector.reciprocal(rows[3][:], rows[3][:]))
                    nc.vector.tensor_tensor(rows[2][:], rows[2][:], rows[3][:], ALU.mult).then_inc(a_scale, 1)
                    dve.wait_ge(b_stat, 16)
                    nc.vector.tensor_scalar(stat_row[:], ps_z[0:16, 0:512], 1.0 / HD, EPS, ALU.mult,
                                            ALU.add).then_inc(b_var, 1)
                    dve.wait_ge(b_std, 1)
                    nc.vector.reciprocal(stat_row[:], stat_row[:]).then_inc(b_rstd, 1)
                if j >= 8:
                    for i in (2 * (j - 8), 2 * (j - 8) + 1):
                        dve.wait_ge(b_bc, i + 1)
                        q = q_b[:, i, :] if i < HB else k_b[:, i - HB, :]
                        gain = gq_s[:] if i < HB else col(V_KN, 0)
                        at = 512 * (1 + i % 2)
                        nc.vector.scalar_tensor_tensor(q, q, gain, ps_z[:, at:at + 512], ALU.mult,
                                                       ALU.mult).then_inc(b_normed, 1)
                    h = j - 8
                    dve.wait_ge(a_bc, h + 1)
                    at = 512 * (h % 2)
                    nc.vector.scalar_tensor_tensor(y_f[:, h, :], y_f[:, h, :], col(V_MNORM, h),
                                                   ps_t[:, at:at + 512], ALU.mult, ALU.mult).then_inc(a_y, 1)

            for h in range(HB):
                n = N_OA + h
                split_lo(dve, n + 1)
                dve.wait_ge(b_ln, h + 1)
                nc.vector.scalar_tensor_tensor(sp_t[:], ps_z[:, 0:CAUSAL], 0.0, sp_t[:], ALU.max,
                                               ALU.add).then_inc(b_sp, 1)
                if h == 0:
                    dve.wait_ge(a_y, HA)
                dve_evacuate(dve, order, n, 0)
                dve.wait_ge(b_sfx, h + 1)
                for b in range(TB):
                    zd = ps_z[:, CAUSAL_AT[b]:CAUSAL_AT[b] + P]
                    ins = nc.vector.tensor_tensor(zd, zd, cst[:, C_MIN:C_MIN + P], ALU.min)
                ins.then_inc(b_min, 1)
                dve_evacuate(dve, order, n, 1)
            dve.wait_ge(b_out, HB)
            for n in range(N_GB, N_MLP):
                split_lo(dve, n + 1)
                for i in range(tiles_of(n)):
                    dve_evacuate(dve, order, n, i)
            dve_norm(dve, order, 1, x_sb, xn2)
            for k in range(KT):
                dve_norm_tile(dve, N_MLP, k, V_MLP)
            with dve.Fori(0, 4) as r:
                for j in range(MLP_SLABS):
                    split_lo(dve, N_MLP + j + 1, r)
                    for i in range(tiles_of(N_MLP + j)):
                        dve_evacuate(dve, order, N_MLP + j, i, r)
            dve_norm(dve, order, 2, x_sb, xn2)
            for k in range(KT):
                dve_norm_tile(dve, N_NQ, k, V_PRE)
            for n in range(N_NQ, N_NZ):
                split_lo(dve, n + 1)
                if n == N_VW:
                    dve.wait_ge(kvc_mm, 1)
                    nc.vector.tensor_copy(kc[:], ps_z[:, 0:2 * NCMP].rearrange("p (t c) -> p t c", c=NCMP))\
                        .then_inc(kvc_ready, 1)
            dve.wait_ge(kvc_mm, 2)
            nc.vector.tensor_copy(vc[:], ps_z[0:NCMP, 512:512 + GN * DH]
                                  .rearrange("p (g d) -> p g d", d=DH)).then_inc(kvc_ready, 1)

            dve.wait_ge(cb_ready, 16 * TB)
            wait_tile_free(dve, end_tile(N_NG) - 1)
            wait_tile_free(dve, end_tile(N_NG) - 2)
            for b in range(TB):
                dve.wait_ge(c_scores, b + 1)
                for e in range(2):
                    for gg in range(2):
                        hs = slice(8 * gg + 4 * e, 8 * gg + 4 * e + 4)
                        at = 512 * e + 4 * gg * NCMP
                        ins = nc.vector.tensor_tensor(
                            clog[:, hs, :], ps_z[:, at:at + 4 * NCMP].rearrange("p (h c) -> p h c", c=NCMP),
                            cbias[:, b, :, hs].rearrange("p c h -> p h c"), ALU.add)
                order.link(ins)
                order.link(nc.vector.tensor_reduce(cmax[:], clog[:], AX_X, ALU.max))
                nc.vector.tensor_tensor(clog[:], clog[:], cmax[:].unsqueeze(2).broadcast_to([P, HN, NCMP]),
                                        ALU.subtract).then_inc(c_log, 1)
                dve.wait_ge(c_exp, b + 1)
                order.link(nc.vector.tensor_reduce(csum[:], clog[:], AX_X, ALU.add))
                order.link(nc.vector.reciprocal(csum[:], csum[:]))
                order.link(nc.vector.scalar_tensor_tensor(csum[:], csum[:], cst[:, C_VALID + b:C_VALID + b + 1],
                                                          gates_n[:, b, 0:HN], ALU.mult, ALU.mult))
                dve.wait_ge(c_pv, b + 1)
                for e, ps in enumerate((ps_z, ps_t)):
                    ins = nc.vector.tensor_tensor(
                        o_a[:, b, 512 * e:512 * e + 512].rearrange("p (h d) -> p h d", d=DH),
                        ps[:, 1024:1536].rearrange("p (h d) -> p h d", d=DH),
                        csum[:, 8 * e:8 * e + 8].unsqueeze(2).broadcast_to([P, 8, DH]), ALU.mult)
                ins.then_inc(c_out, 1)

            def row_max(u):
                dve.wait_ge(s_scores, u + 1)
                dve.wait_ge(bias_in[u % 2], 16 * (u // 2 + 1))
                if u >= 2:
                    dve.wait_ge(s_t, u - 1)
                elif u == 0:
                    dve.wait_ge(c_pv, TB)
                for b in range(TB):
                    at, w = ROWS_AT[b], ROWS_W[b]
                    ins = nc.vector.tensor_tensor_reduce(probs[u % 2][:, at:at + w], ps_z[:, at:at + w],
                                                         tile_t[u % 2][:, S - w:S], 1.0, -3.0e38, ALU.add,
                                                         ALU.max, rmax[:, u % 2, b:b + 1])
                order.link(ins)
                nc.vector.tensor_scalar(rneg[:, u % 2, :], rmax[:, u % 2, :], -1.0, None, ALU.mult)\
                    .then_inc(s_max, 1)

            row_max(0)
            for u in range(32):
                h, branch = u % HN, 1 + u // HN
                if u % 4 == 0:
                    split_lo(dve, N_NZ + u // 4 + 1)
                if u < 31:
                    row_max(u + 1)
                dve.wait_ge(s_t, u + 1)
                if u:
                    dve.wait_ge(s_pv, u)
                nc.vector.tensor_copy(probs_t[:, 512:CAUSAL], ps_t[:, 512:CAUSAL]).then_inc(s_td, 1)
                dve_evacuate(dve, order, N_NZ + u // 4, u % 4)
                dve.wait_ge(s_probs, u + 1)
                order.link(nc.vector.reciprocal(rgate[:], rsum[:, u % 2, :]))
                order.link(nc.vector.tensor_tensor(rgate[:], rgate[:],
                                                   gates_n[:, :, branch * HN + h], ALU.mult))
                dve.wait_ge(s_pv, u + 1)
                o = o_b if branch == 1 else o_c
                nc.vector.tensor_tensor(o[:, :, h * DH:(h + 1) * DH],
                                        ps_t[:, CAUSAL:CAUSAL + TB * DH].rearrange("p (b d) -> p b d", d=DH),
                                        rgate[:].unsqueeze(2).broadcast_to([P, TB, DH]),
                                        ALU.mult).then_inc(s_out, 1)
            dve.wait_ge(s_out, 32)
            for n in range(N_NZ + 8, N_NO):
                split_lo(dve, n + 1)
                for i in range(tiles_of(n)):
                    dve_evacuate(dve, order, n, i)
            for k in range(KT):
                dve_norm_tile(dve, N_NO, k, None)
            for n in range(N_NO, N_ALL):
                split_lo(dve, n + 1)
                for i in range(tiles_of(n)):
                    dve_evacuate(dve, order, n, i)
            dve_norm(dve, order, 3, None, None)
            dve.wait_ge(gain_in, 16)
            for b in range(TB):
                order.link(nc.vector.scalar_tensor_tensor(y2[:, b, :], y2[:, b, :], rstd[:, 3, b:b + 1],
                                                          gain_bc[:], ALU.mult, ALU.mult))
                nc.vector.tensor_tensor(xo[:, b, :], y2[:, b, :], x_sb[:, b, :], ALU.add).then_inc(out_ready, 1)

        @block.gpsimd
        def _(pool):
            order = Order(pool, pool_order)

            def mask_diagonals(t, keep):
                for b in range(TB):
                    d = t[:, CAUSAL_AT[b]:CAUSAL_AT[b] + P]
                    ins = nc.gpsimd.affine_select(out=d, in_=d, compare_op=keep, fill=0.0, base=0,
                                                  pattern=[[1, P]], channel_multiplier=-1)
                return ins

            pool.wait_ge(oh_cp, 2)
            pool.dma_start(a["bias_rev"], bias_rev_sb[:].unsqueeze(1).broadcast_to([HN, P, REV]))\
                .then_inc(bias_out, 16)
            pool.dma_start(a["bias_fwd"].rearrange("(c p) h -> p c h", p=P), bias_fwd_sb[:])\
                .then_inc(bias_out, 16)

            for h in range(HA):
                pool.wait_ge(a_decay, h + 1)
                mask_diagonals(decay, ALU.is_ge).then_inc(a_masked, 1)
            for h in range(HB):
                pool.wait_ge(b_sp, h + 1)
                if h:
                    pool.wait_ge(b_sfx, h)
                order.link(mask_diagonals(sp_t, ALU.is_gt))
                s1, s2, s3 = (sp_t[:, CAUSAL_AT[b]:CAUSAL_AT[b] + CAUSAL_W[b]] for b in (1, 2, 3))
                nc.gpsimd.tensor_copy(later1[:, 0:P], s2[:, 0:P])
                nc.gpsimd.tensor_copy(later0[:, 0:P], s1[:, 0:P])
                order.link(nc.gpsimd.tensor_tensor(later1[:, P:2 * P], s2[:, P:2 * P], s3, ALU.add))
                nc.gpsimd.tensor_tensor(later0[:, P:3 * P], s1[:, P:3 * P], later1[:], ALU.add)\
                    .then_inc(b_later, 1)

            for which, (pair, pos, n) in enumerate(((pairk, V_POSK, N_KC), (pairv, V_POSV, N_VC))):
                wait_tile_free(pool, end_tile(n) - 2)
                wait_tile_free(pool, end_tile(n) - 1)
                if which:
                    pool.wait_ge(hid_mm, 1)
                for k in range(16):
                    ins = nc.gpsimd.tensor_scalar(
                        cmp_in[:, k, :].rearrange("p (g c) -> p g c", c=NCMP),
                        pair[:, :, 2 * k:2 * k + CSTRIDE * (NCMP - 1) + 1:CSTRIDE], col(pos, k), None, ALU.add)
                ins.then_inc(cmp_ready, 1)

            pool.wait_ge(bias_out, 32)
            pool.wait_ge(hid_mm, 2)
            fwd = a["bias_fwd"]
            for b in range(TB):
                pool.dma_start(cbias[:, b], bass.AP(fwd.tensor, (S - 1 - (CLEN - 1) + b * P) * HN,
                                                    [[HN, P], [-CSTRIDE * HN, NCMP], [1, HN]]))\
                    .then_inc(cb_ready, 16)
            rev = a["bias_rev"]
            for u in range(32):
                if u >= 2:
                    pool.wait_ge(s_max, u - 1)
                pool.dma_start(tile_t[u % 2][:], bass.AP(rev.tensor, (u % HN) * P * REV + P - 1,
                                                         [[REV - 1, P], [1, S]])).then_inc(bias_in[u % 2], 16)


DRAM = dict(
    x=("x", (S, D)), w_in=("w_in", (D, 8208)), w_out=("w_out", (D, D)), w_up=("w_up", (D, DFF)),
    w_down=("w_down", (DFF, D)), nsa_w_in=("nsa_w_in_2", (D, 5680)), nsa_w_out=("nsa_w_out_2", (D, D)),
    nsa_cmp_k_w1=("nsa_cmp_k_w1_2", (2048, 256)), nsa_cmp_v_w1=("nsa_cmp_v_w1_2", (2048, 256)),
    nsa_cmp_k_w2=("nsa_cmp_k_w2_2", (256, DH)), nsa_cmp_v_w2=("nsa_cmp_v_w2_2", (256, DH)),
    mix_g=("norm_mix_g", (8, P)), mlp_g=("norm_mlp_g", (8, P)), pre_g=("pre_norm_gain_2", (8, P)),
    mnorm_g=("mlstm_norm_g", (8, P)), conv_w=("conv_w", (32, P)), b_gate=("b_gate", (16, P)),
    pos_k=("nsa_cmp_k_pos_2", (16, P)), pos_v=("nsa_cmp_v_pos_2", (16, P)),
    qn_g=("sb_q_norm_g", (1, P)), kn_g=("sb_k_norm_g", (1, P)), b_if=("b_if", (16,)),
    post_gain=("post_norm_gain_2", (D,)),
)


def build(nc, inputs):
    arrays, aps = {}, {}

    def bring(name, arr):
        arrays[f"in_{name}"] = arr
        aps[name] = nc.dram_tensor(f"in_{name}", arr.shape, F32, kind="ExternalInput").ap()

    for name, (key, shape) in DRAM.items():
        bring(name, np.ascontiguousarray(np.asarray(inputs[key]).reshape(shape)))
    bring("cst", constants())
    bring("onehot", bucket_table())
    table = np.asarray(inputs["rel_bias_table_2"])
    bring("table", np.ascontiguousarray(np.concatenate([table, np.full((1, HN), NEG, table.dtype)])))
    aps["bias_rev"] = nc.dram_tensor("bias_rev_dram", (HN, P, REV), F32, kind="Internal").ap()
    aps["bias_fwd"] = nc.dram_tensor("bias_fwd_dram", (1024, HN), F32, kind="Internal").ap()
    out = nc.dram_tensor("out_dram", (S, D), F32, kind="ExternalOutput").ap()
    program(nc, aps, out)
    return arrays


def kernel(**inputs):
    import concourse.bacc as bacc
    from concourse.bass_utils import run_bass_kernel_spmd
    nc = bacc.Bacc("TRN2", target_bir_lowering=False, num_devices=1)
    arrays = build(nc, inputs)
    r = run_bass_kernel_spmd(nc, [arrays], core_ids=[0])
    return r.results[0]["out_dram"].reshape(1, S, D)
```

```python
from contextlib import ExitStack

import numpy as np
import concourse.bass as bass
from concourse import mybir

ALU = mybir.AluOpType
ACT = mybir.ActivationFunctionType
AX_X = mybir.AxisListType.X
F32 = mybir.dt.float32
F32R = mybir.dt.float32r

P = 128
S = 512
D = 1024
TB = S // P
KT = D // P
SLAB = 256
EPS = 1e-6
HA = 8
DQK = 64
HB = 8
HD = 128
DFF = 4 * D
HN = 16
DH = 64
GN = 4
NCMP = 31
CPAD = 32
CSTRIDE = 16
CLEN = 32
BUCKETS = 32
NEG = -1e30

QA, KA, VA, OA, IF = 0, 512, 1024, 2048, 3072
QB, KB, VB, GA, GB = 3088, 4112, 5136, 6160, 7184
NQ, NKC, NVC, NKS, NVS, NKW, NVW, NG, NZ = 0, 1024, 1280, 1536, 1792, 2048, 2304, 2560, 2608

CAUSAL_AT = (0, 512, 1024, 896)
CAUSAL_W = (512, 384, 256, 128)
CAUSAL = 1280
ROWS_AT = (896, 1024, 512, 0)
ROWS_W = (128, 256, 384, 512)

V_MIX, V_MLP, V_PRE, V_MNORM, V_CONV, V_BGATE, V_POSK, V_POSV, V_QN, V_KN, V_ROWS = (
    0, 8, 16, 24, 32, 64, 80, 96, 112, 113, 114)

C_ID, C_TRI, C_NEG, C_MIN, C_STRIP, C_VALID, C_ALL = 0, 128, 256, 384, 512, 592, 596
REV = S + P
OH_REV, OH_W = 1024, 1024 + REV

VEC_PARTS = (("mix_g", (V_MIX, 8)), ("mlp_g", (V_MLP, 8)), ("pre_g", (V_PRE, 8)),
             ("mnorm_g", (V_MNORM, 8)), ("conv_w", (V_CONV, 32)), ("b_gate", (V_BGATE, 16)),
             ("pos_k", (V_POSK, 16)), ("pos_v", (V_POSV, 16)), ("qn_g", (V_QN, 1)), ("kn_g", (V_KN, 1)))
ACT_VECS = 5


def constants():
    j = np.arange(P)[:, None]
    s = np.arange(P)[None, :]
    c = np.zeros((P, C_ALL), np.float32)
    c[:, C_ID:C_ID + P] = j == s
    c[:, C_TRI:C_TRI + P] = np.where(j >= s, -1.0, 0.0)
    c[:, C_NEG:C_NEG + P] = -1.0
    c[:, C_MIN:C_MIN + P] = np.where(j < s, -NEG, NEG)
    c[:, C_STRIP + 39] = 1.0
    t = np.arange(TB)[None, :] * P + j
    c[:, C_VALID:C_VALID + TB] = t >= CLEN - 1
    return c


def bucket_table():
    dist = np.concatenate([np.arange(OH_REV) - 511, 511 - np.arange(OH_W - OH_REV)])
    n = np.maximum(dist, 0)
    half = BUCKETS // 2
    large = half + (np.log(np.maximum(n, 1) / half) / np.log(128 / half) * half + 1e-9).astype(int)
    bucket = np.where(n < half, n, np.minimum(large, BUCKETS - 1))
    t = (bucket[None, :] == np.arange(BUCKETS)[:, None]) & (dist >= 0)[None, :]
    return np.concatenate([t, (dist < 0)[None, :]]).astype(np.float32)


class Order:

    def __init__(self, eng, sem):
        self.eng, self.sem, self.n, self.shift = eng, sem, 0, 0

    def link(self, ins):
        ins.then_inc(self.sem, 1)
        self.n += 1
        self.eng.wait_ge(self.sem, self.n + self.shift)


def program(nc, a, out):
    with ExitStack() as ctx:
        def sem(name):
            return ctx.enter_context(nc.semaphore(name))

        base = -(-nc.sbuf_base // 64) * 64
        top = [base]

        def sb(name, shape, dt=F32, at=None):
            size = int(np.prod(shape[1:])) * 4
            if at is None:
                at = top[0]
                top[0] += -(-size // 32) * 32
                assert top[0] <= nc.sbuf_usable_end, (name, top[0])
            return nc.alloc_sbuf_tensor_at(name, shape, dt, offset=at)

        x_sb = sb("x_sb", [P, TB, D])
        act_hi = sb("act_hi", [P, KT, S], F32R)
        act_lo = sb("act_lo", [P, KT, S], F32R)
        w_raw = [sb(f"w_raw{i}", [P, KT, SLAB]) for i in range(2)]
        w_hi = [sb(f"w_hi{i}", [P, KT, SLAB], F32R) for i in range(2)]
        w_lo = [sb(f"w_lo{i}", [P, KT, SLAB], F32R) for i in range(2)]
        arena = top[0]
        K16 = 16384
        top[0] += 6 * K16

        diag = sb("diag", [P, TB, P], at=arena + 2 * K16)
        squares = [sb(f"squares{b}", [P, D], at=arena + 2 * K16 + 2048 + 4096 * b if b < 3
                      else arena + 5 * K16) for b in range(TB)]

        qk_a = sb("qk_a", [P, 8, S], at=arena)
        v_a = sb("v_a", [P, TB, D], at=arena + K16)
        y_f = sb("y_f", [P, 8, S], at=arena + 2 * K16)
        q_b = sb("q_b", [P, HB, S], at=arena + 3 * K16)
        k_b = sb("k_b", [P, HB, S], at=arena + 4 * K16)
        v_b = sb("v_b", [P, TB, D], at=arena + K16)
        y_hi = sb("y_hi", [P, KT, S], F32R, at=arena + 3 * K16)
        y_lo = sb("y_lo", [P, KT, S], F32R, at=arena + 4 * K16)
        yb_f = sb("yb_f", [P, HB, S], at=arena)
        t1 = arena + 5 * K16
        conv_t = sb("conv_t", [P, 2, S], at=t1)
        decay = sb("decay", [P, CAUSAL], at=t1)
        num_sq = sb("num_sq", [P, S], at=t1 + 5120)
        rows = [sb(f"rows{i}", [HA, S], at=t1 + 7168 + 2048 * i) for i in range(4)]
        sqs = sb("sqs", [P, 2, S], at=t1)
        sp_t = sb("sp_t", [P, CAUSAL], at=t1)
        later1 = sb("later1", [P, 128], at=t1 + 5120)
        later0 = sb("later0", [P, 256], at=t1 + 6144)
        attn_b = sb("attn_b", [P, CAUSAL], at=t1 + 7680)
        stat_row = sb("stat_row", [16, S], at=t1 + 5120)
        up_hi = sb("up_hi", [P, KT, S], F32R, at=arena)
        up_lo = sb("up_lo", [P, KT, S], F32R, at=arena + K16)
        relu_t = sb("relu_t", [P, 2, S], at=arena + 3 * K16)
        qn = sb("qn", [P, 8, S], at=arena)
        ks = sb("ks", [P, 2, S], at=arena + K16)
        kw = sb("kw", [P, 2, S], at=arena + K16 + 4096)
        vs = sb("vs", [P, TB, 256], at=arena + K16 + 8192)
        vw = sb("vw", [P, TB, 256], at=arena + K16 + 12288)
        o_a = sb("o_a", [P, TB, D], at=arena + 2 * K16)
        o_b = sb("o_b", [P, TB, D], at=arena + 3 * K16)
        o_c = sb("o_c", [P, TB, D], at=arena + 4 * K16)
        w1k = sb("w1k", [P, 16, 256], at=arena + 2 * K16)
        w1v = sb("w1v", [P, 16, 256], at=arena + 3 * K16)
        pairk = sb("pairk", [P, GN, S], at=arena + 4 * K16)
        pairv = sb("pairv", [P, GN, S], at=arena + 4 * K16 + 8192)
        cmp_in = [sb("cmp_in_k", [P, 16, GN * NCMP], at=arena + 5 * K16),
                  sb("cmp_in_v", [P, 16, GN * NCMP], at=arena + 4 * K16)]
        cbias = sb("cbias", [P, TB, NCMP, HN], at=arena + 4 * K16 + 8192)
        clog = [sb(f"clog{i}", [P, HN, CPAD], at=arena + 3 * K16 + 8192 * i) for i in range(2)]
        cpt = [sb(f"cpt{i}", [P, GN, P], at=arena + 4 * K16 + 2048 * i) for i in range(2)]
        v_diag = sb("v_diag", [P, GN, 4, DH], at=arena + 4 * K16 + 4096)
        probs = [sb(f"probs{i}", [P, CAUSAL], at=arena + 5 * K16 + 5120 * i) for i in range(2)]
        probs_t = sb("probs_t", [P, CAUSAL], at=arena + 5 * K16 + 10240)
        y2 = sb("y2", [P, TB, D], at=arena)
        gain_bc = sb("gain_bc", [P, D], at=arena + K16)
        xo = sb("xo", [P, TB, D], at=arena + 3 * K16)

        cst = sb("cst", [P, C_ALL])
        vec_rows = sb("vec_rows", [V_ROWS, P])
        vec = sb("vec", [P, V_ROWS])
        bif = sb("bif", [32 + HA, 1])
        ones_row = sb("ones_row", [HA, S], at=arena + 3 * K16)
        u_col = sb("u_col", [P, TB, HA])
        ssq = sb("ssq", [P, 4, TB])
        rstd = sb("rstd", [P, 4, TB])
        ssq_y = sb("ssq_y", [P, TB, 4])
        ev_t = sb("ev_t", [P, 2, S])
        tile_t_at = top[0]
        tile_t = [sb(f"tile_t{i}", [P, S]) for i in range(2)]
        gates_n = sb("gates_n", [P, TB, 48])
        gate_f = sb("gate_f", [48, S], at=tile_t_at)
        den_sum = sb("den_sum", [P, S - P], at=tile_t_at)
        table = sb("table", [BUCKETS + 1, HN])
        w2k = sb("w2k", [P, 2, DH], at=arena + 5 * K16 + 8192)
        w2v = sb("w2v", [P, 2, DH], at=arena + 5 * K16 + 8704)
        hid_v = sb("hid_v", [P, 2, GN, 4, CPAD], at=arena + 5 * K16 + 10240)
        hid = sb("hid", [P, 2, GN * NCMP], at=arena + 5 * K16 + 9216)
        onehot = sb("onehot", [BUCKETS + 1, OH_W], at=t1 + 4096)
        bias_rev_sb = sb("bias_rev_sb", [HN, 640], at=t1 + 4096 + 4 * OH_W)
        bias_fwd_sb = sb("bias_fwd_sb", [P, 8, HN], at=t1 + 4096 + 4 * OH_W + 2560)
        gq_s = sb("gq_s", [P, 1])
        mn_q = sb("mn_q", [P, HA])
        half_bg = sb("half_bg", [P, HA])
        k_diag = sb("k_diag", [P, 2, 2, CPAD])
        cmax = sb("cmax", [P, HN])
        csum = sb("csum", [P, 2, HN])
        rmax = sb("rmax", [P, 2, TB])
        rneg = sb("rneg", [P, 2, TB])
        rsum = sb("rsum", [P, 2, TB])
        rgate = sb("rgate", [P, TB])
        ps_g = ctx.enter_context(nc.psum_tensor("ps_g", [P, 2, 512], F32))
        ps_z = ctx.enter_context(nc.psum_tensor("ps_z", [P, 1536], F32))
        ps_t = ctx.enter_context(nc.psum_tensor("ps_t", [P, 1536], F32))

        ident = cst[:, C_ID:C_ID + P]

        def col(v, k):
            return vec[:, v + k:v + k + 1]

        def row_picker(i, rows_):
            at = C_STRIP + 39 - i
            return cst[:, at:at + rows_]

        def spread(i, k, m=P):
            return cst[0:k, C_ID + i:C_ID + i + 1].broadcast_to([k, m])

        const_in = sem("const_in")
        x_in = [sem(f"x_in{b}") for b in range(TB)]
        vec_in = sem("vec_in")
        vec_in_pool = sem("vec_in_pool")
        raw_landed = [sem(f"raw_landed{i}") for i in range(2)]
        hi_done = sem("hi_done")
        lo_done = sem("lo_done")
        tile_ready = sem("tile_ready")
        tile_free = [sem(f"tile_free{i}") for i in range(2)]
        ev_act = sem("ev_act")
        ev_dve = sem("ev_dve")
        act_order = sem("act_order")
        dve_order = sem("dve_order")
        pool_order = sem("pool_order")
        vec_t = sem("vec_t")
        vec_ready = sem("vec_ready")
        ones_ready = sem("ones_ready")
        sq_done = sem("sq_done")
        var_ready = sem("var_ready")
        std_ready = sem("std_ready")
        diag_ready = sem("diag_ready")
        norm_done = sem("norm_done")
        norm_hi = sem("norm_hi")
        norm_lo = sem("norm_lo")
        gates_mm = sem("gates_mm")
        gates_ready = sem("gates_ready")
        gate_act = sem("gate_act")
        gate_dve = sem("gate_dve")
        u_ready = sem("u_ready")
        u_t = sem("u_t")
        u_col_ready = sem("u_col_ready")
        a_scores = sem("a_scores")
        a_decay = sem("a_decay")
        a_masked = sem("a_masked")
        a_probs = sem("a_probs")
        a_pv = sem("a_pv")
        a_den = sem("a_den")
        a_num = sem("a_num")
        a_ssq = sem("a_ssq")
        a_fin_d = sem("a_fin_d")
        a_fin_a = sem("a_fin_a")
        a_scale = sem("a_scale")
        a_bc = sem("a_bc")
        a_y = sem("a_y")
        b_sq = sem("b_sq")
        b_stat = sem("b_stat")
        b_var = sem("b_var")
        b_std = sem("b_std")
        b_rstd = sem("b_rstd")
        b_bc = sem("b_bc")
        b_normed = sem("b_normed")
        b_z = sem("b_z")
        b_ln = sem("b_ln")
        b_sp = sem("b_sp")
        b_later = sem("b_later")
        b_sfx = sem("b_sfx")
        b_min = sem("b_min")
        b_attn = sem("b_attn")
        b_pv = sem("b_pv")
        b_out = sem("b_out")
        nsa_in = sem("nsa_in")
        oh_mm = sem("oh_mm")
        oh_cp = sem("oh_cp")
        bias_out = sem("bias_out")
        w1_in = sem("w1_in")
        cmp_ready = sem("cmp_ready")
        hid_mm = sem("hid_mm")
        hid_ready = sem("hid_ready")
        hid_pad = sem("hid_pad")
        kvc_mm = sem("kvc_mm")
        kvc_ready = sem("kvc_ready")
        cb_mm = sem("cb_mm")
        cb_ready = sem("cb_ready")
        c_scores = sem("c_scores")
        c_log = sem("c_log")
        c_exp = sem("c_exp")
        c_t = sem("c_t")
        c_tc = sem("c_tc")
        c_pv = sem("c_pv")
        c_gate = sem("c_gate")
        c_out = sem("c_out")
        bias_in = [sem(f"bias_in{i}") for i in range(2)]
        s_scores = sem("s_scores")
        s_max = sem("s_max")
        s_probs = sem("s_probs")
        s_t = sem("s_t")
        s_ta = sem("s_ta")
        s_td = sem("s_td")
        s_pv = sem("s_pv")
        s_out = sem("s_out")
        gain_in = sem("gain_in")
        out_ready = sem("out_ready")
        out_done = sem("out_done")

        W, NW = a["w_in"], a["nsa_w_in"]
        slabs = []

        def add(kind, mat, col0, n, row0=0, w=SLAB):
            first = len(slabs)
            for i in range(n):
                slabs.append((mat, row0, col0 + i * w, w, kind, i))
            return first

        N_QA = add("conv", W, QA, 4)
        N_IF = add("if", W, IF, 1, w=P)
        N_VA = add("va", W, VA, 4)
        N_QB = add("qb", W, QB, 8)
        N_VB = add("vb", W, VB, 4)
        N_OA = add("oa", W, OA, 4)
        N_GA = add("ga", W, GA, 4)
        N_GB = add("gb", W, GB, 4)
        N_WO = add("wo", a["w_out"], 0, 4)
        N_MLP = len(slabs)
        for quarter in range(4):
            add("up", a["w_up"], quarter * D, 4)
            add("down", a["w_down"], 0, 4, row0=quarter * D)
        N_NQ = add("nq", NW, NQ, 4)
        N_KC = add("nkc", NW, NKC, 1)
        N_VC = add("nvc", NW, NVC, 1)
        N_NG = add("ng", NW, NG, 1, w=P)
        N_KS = add("nks", NW, NKS, 1)
        N_KW = add("nkw", NW, NKW, 1)
        N_VS = add("nvs", NW, NVS, 1)
        N_VW = add("nvw", NW, NVW, 1)
        N_NZ = add("nz", NW, NZ, 12)
        N_NO = add("no", a["nsa_w_out"], 0, 4)
        N_ALL = len(slabs)
        MLP_SLABS = 8
        SB_CUT = 4

        FEATURE = {"conv", "if", "ng", "qb", "oa", "ga", "gb", "up", "nq", "nkc", "nvc", "nks", "nkw"}
        BY_ACT = {"norm": 1, "conv": 1, "no": 1, "oa": 1, "ga": 1, "gb": 2, "up": 2, "nz": 1}
        BY_DVE = {"gb": 1, "up": 1}
        norm_before = {N_QA, N_MLP, N_NQ, N_NO}
        tile_of, norm_tile_of, kinds = {}, {}, []

        def tiles_of(n):
            return slabs[n][3] // P if slabs[n][4] in FEATURE else TB

        for n in range(N_ALL):
            if n in norm_before:
                norm_tile_of[n] = len(kinds)
                kinds += ["norm"] * 2
            tile_of[n] = len(kinds)
            kinds += [slabs[n][4]] * tiles_of(n)
        tile_of[N_ALL] = len(kinds)
        act_count, dve_count = [0], [0]
        for kind in kinds:
            act_count.append(act_count[-1] + BY_ACT.get(kind, 0))
            dve_count.append(dve_count[-1] + BY_DVE.get(kind, 0))
        MLP_TILES = tile_of[N_MLP + MLP_SLABS] - tile_of[N_MLP]

        CMP_TILES = (((N_VS, 2),), ((N_VS, 3), (N_VW, 0)), ((N_VW, 1),), ((N_VW, 2), (N_VW, 3)))

        def end_tile(n):
            return tile_of[n] + tiles_of(n)

        def wait_tile_free(eng, t, r=0):
            eng.wait_ge(tile_free[t % 2], t // 2 + 1 + MLP_TILES // 2 * r)

        def split_hi(act, n, r=0):
            if n >= N_ALL:
                return
            b, w = n % 2, slabs[n][3]
            extra = n >= N_IF and b == N_IF % 2
            act.wait_ge(raw_landed[b], 16 * (n // 2 + 1 + extra) + 16 * (MLP_SLABS // 2) * r)
            if n >= 2:
                act.wait_ge(tile_ready, tile_of[n - 1] + MLP_TILES * r)
            nc.scalar.activation(w_hi[b][:, :, 0:w], w_raw[b][:, :, 0:w], ACT.Copy).then_inc(hi_done, 1)

        def split_lo(dve, n, r=0):
            if n >= N_ALL:
                return
            b, w = n % 2, slabs[n][3]
            dve.wait_ge(hi_done, n + 1 + MLP_SLABS * r)
            nc.vector.tensor_tensor(w_lo[b][:, :, 0:w], w_raw[b][:, :, 0:w],
                                    w_hi[b][:, :, 0:w].bitcast(F32), ALU.subtract).then_inc(lo_done, 1)

        def mm_tile(pe, n, i, first_tile=None, hi=act_hi, lo=act_lo, r=0, ks=range(KT),
                    activation_ready=None):
            t, kind = tile_of[n] + i, slabs[n][4]
            b, w = n % 2, slabs[n][3]
            pe.wait_ge(lo_done, n + 1 + MLP_SLABS * r)
            wait_tile_free(pe, t - 2, r)
            m = slice(i * P, (i + 1) * P)
            for k in ks:
                if activation_ready is not None and i == 0:
                    activation_ready(k)
                if first_tile is not None and i == 0 and (t - first_tile - k) % 2:
                    wait_tile_free(pe, first_tile + k, r)
                if kind in FEATURE:
                    o = ps_g[:, t % 2, :]
                    three = ((w_hi[b][:, k, m], hi[:, k, :]), (w_hi[b][:, k, m], lo[:, k, :]),
                             (w_lo[b][:, k, m], hi[:, k, :]))
                else:
                    o = ps_g[:, t % 2, 0:w]
                    three = ((hi[:, k, m], w_hi[b][:, k, 0:w]), (hi[:, k, m], w_lo[b][:, k, 0:w]),
                             (lo[:, k, m], w_hi[b][:, k, 0:w]))
                for j, (stationary, moving) in enumerate(three):
                    mm = nc.tensor.matmul(o, stationary, moving, start=(k == 0 and j == 0),
                                          stop=(k == KT - 1 and j == 2))
            if ks[-1] == KT - 1:
                mm.then_inc(tile_ready, 1)

        def mm_slab(pe, n, first_tile=None, hi=act_hi, lo=act_lo, r=0, activation_ready=None):
            for i in range(tiles_of(n)):
                mm_tile(pe, n, i, first_tile, hi, lo, r, activation_ready=activation_ready)

        def feature_bank(n, k):
            if k < 2:
                return ps_g[:, (norm_tile_of[n] + k) % 2, :]
            k -= 2
            return (ps_z, ps_t)[k // 3][:, k % 3 * 512:(k % 3 + 1) * 512]

        def feature_tiles(pe, n, src, scaled, block_ready, between=None):
            t0 = norm_tile_of[n]

            def turn(b, ks):
                for k in ks:
                    moving = diag[:, b, :] if scaled else ident
                    mm = nc.tensor.matmul(feature_bank(n, k)[:, b * P:(b + 1) * P],
                                          src[:, b, k * P:(k + 1) * P], moving, start=True, stop=True)
                    if b == TB - 1:
                        mm.then_inc(tile_ready if k < 2 else norm_done, 1)

            for b in range(TB - 1):
                block_ready(b)
                turn(b, range(2, KT))
            if between is not None:
                between()
            for k in (0, 1):
                if t0 >= 2:
                    wait_tile_free(pe, t0 + k - 2)
                for b in range(TB - 1):
                    turn(b, (k,))
            block_ready(TB - 1)
            turn(TB - 1, range(KT))

        def features_ready(pe, n, which):
            def wait(k):
                if k >= 2:
                    pe.wait_ge(norm_lo, 6 * which + k - 1)
                elif k == 1:
                    wait_tile_free(pe, norm_tile_of[n] + 1)
            return wait

        def tile_done(eng, t, r=0):
            eng.wait_ge(tile_ready, t + 1 + MLP_TILES * r)

        def after_act(eng, t, k, r=0):
            eng.wait_ge(ev_act, act_count[t] + k + ACT_ROUND * r)

        def after_dve(eng, t, k, r=0):
            eng.wait_ge(ev_dve, dve_count[t] + k + DVE_ROUND * r)

        m0, m1 = tile_of[N_MLP], tile_of[N_MLP + MLP_SLABS]
        ACT_ROUND = act_count[m1] - act_count[m0]
        DVE_ROUND = dve_count[m1] - dve_count[m0]

        def act_feature_tile(act, n, k, which, gain):
            if k < 2:
                tile_done(act, norm_tile_of[n] + k)
            else:
                act.wait_ge(norm_done, 6 * which + k - 1)
            scale = 1.0 if gain is None else col(gain, k)
            nc.scalar.activation(act_hi[:, k, :], feature_bank(n, k), ACT.Copy,
                                 scale=scale).then_inc(ev_act if k < 2 else norm_hi, 1)

        def dve_feature_tile(dve, n, k, which, gain):
            t = norm_tile_of[n] + k
            if k < 2:
                after_act(dve, t, 1)
            else:
                dve.wait_ge(norm_hi, 6 * which + k - 1)
            src, hi = feature_bank(n, k), act_hi[:, k, :].bitcast(F32)
            if gain is None:
                ins = nc.vector.tensor_tensor(act_lo[:, k, :], src, hi, ALU.subtract)
            else:
                ins = nc.vector.scalar_tensor_tensor(act_lo[:, k, :], src, col(gain, k), hi, ALU.mult,
                                                     ALU.subtract)
            ins.then_inc(tile_free[t % 2] if k < 2 else norm_lo, 1)

        def act_evacuate(act, n, i, r=0):
            kind, s = slabs[n][4], slabs[n][5]
            t = tile_of[n] + i
            g, free = t % 2, tile_free[t % 2]
            f = 2 * s + i
            cols = slice(s * SLAB, (s + 1) * SLAB)
            if kind == "conv":
                wait_tile_free(act, t)
                nc.scalar.activation(qk_a[:, f, :], conv_t[:, g, :], ACT.Silu).then_inc(ev_act, 1)
                return
            if kind in ("if", "wo", "down"):
                return
            tile_done(act, t, r)
            if kind in ("va", "vb"):
                dst = v_a if kind == "va" else v_b
                nc.scalar.copy(dst[:, i, cols], ps_g[:, g, 0:SLAB]).then_inc(free, 1)
            elif kind == "qb":
                dst = q_b[:, f, :] if f < HB else k_b[:, f - HB, :]
                nc.scalar.copy(dst, ps_g[:, g, :]).then_inc(free, 1)
            elif kind in ("oa", "ga"):
                bias = 0.0 if kind == "oa" else half_bg[:, f:f + 1]
                nc.scalar.activation(ev_t[:, g, :], ps_g[:, g, :], ACT.Tanh, bias=bias,
                                     scale=0.5).then_inc(ev_act, 1)
            elif kind == "gb":
                nc.scalar.activation(ev_t[:, g, :], ps_g[:, g, :], ACT.Sigmoid,
                                     bias=col(V_BGATE, 8 + f)).then_inc(ev_act, 1)
                after_dve(act, t, 1)
                nc.scalar.copy(y_hi[:, f, :], ev_t[:, g, :]).then_inc(ev_act, 1)
            elif kind == "up":
                nc.scalar.activation(ev_t[:, g, :], ps_g[:, g, :], ACT.Relu).then_inc(ev_act, 1)
                after_dve(act, t, 1, r)
                nc.scalar.copy(up_hi[:, f, :], relu_t[:, g, :]).then_inc(ev_act, 1)
            elif kind == "nq":
                half = f // 2 % 2
                for e in range(2):
                    dst = qn[64 * half:64 * half + 64, 4 * (f // 4) + (2 * f + e) % 4, :]
                    ins = nc.scalar.mul(dst, ps_g[64 * e:64 * e + 64, g, :], DH ** -0.5)
                ins.then_inc(free, 1)
            elif kind in ("nkc", "nvc"):
                pair = pairk if kind == "nkc" else pairv
                for e in range(2):
                    src = ps_g[64 * e:64 * e + 64, g, :]
                    nc.scalar.copy(pair[0:64, 2 * i + e, :], src)
                    ins = nc.scalar.copy(pair[64:128, 2 * i + e, 0:S - 1], src[:, 1:S])
                ins.then_inc(free, 1)
            elif kind in ("nks", "nkw"):
                dst = ks if kind == "nks" else kw
                nc.scalar.copy(dst[:, i, :], ps_g[:, g, :]).then_inc(free, 1)
            elif kind in ("nvs", "nvw"):
                dst = vs if kind == "nvs" else vw
                nc.scalar.copy(dst[:, i, :], ps_g[:, g, 0:SLAB]).then_inc(free, 1)
            elif kind == "ng":
                nc.scalar.activation(gate_f[:], ps_g[0:48, g, :], ACT.Tanh, scale=0.5).then_inc(free, 1)
            elif kind == "no":
                nc.scalar.activation(ev_t[:, g, 0:SLAB], ps_g[:, g, 0:SLAB], ACT.Square,
                                     accum_out=ssq_y[:, i, s:s + 1]).then_inc(ev_act, 1)
            elif kind == "nz":
                nc.scalar.activation(ev_t[:, g, 0:SLAB], ps_g[:, g, 0:SLAB], ACT.Tanh,
                                     scale=0.5).then_inc(ev_act, 1)

        def dve_evacuate(dve, order, n, i, r=0):
            kind, s = slabs[n][4], slabs[n][5]
            t = tile_of[n] + i
            g, free = t % 2, tile_free[t % 2]
            f = 2 * s + i
            cols = slice(s * SLAB, (s + 1) * SLAB)
            ps = ps_g[:, g, :]
            if kind == "conv":
                tile_done(dve, t)
                if f >= 2:
                    after_act(dve, t - 2, 1)
                y = conv_t[:, g, :]
                order.link(nc.vector.tensor_scalar(y, ps, col(V_CONV, 24 + f), None, ALU.mult))
                for back in (1, 2, 3):
                    w = col(V_CONV, 8 * (3 - back) + f)
                    ins = nc.vector.scalar_tensor_tensor(y[:, back:S], ps[:, 0:S - back], w,
                                                         y[:, back:S], ALU.mult, ALU.add)
                    if back < 3:
                        order.link(ins)
                ins.then_inc(free, 1)
            elif kind == "if":
                dve.wait_ge(bias_out, 32)
                tile_done(dve, t)
                nc.vector.tensor_scalar(rows[3][:], ps[0:HA, :], bif[0:HA, :], None, ALU.add)
                nc.vector.tensor_scalar(rows[2][:], ps[32:32 + HA, :], bif[32:32 + HA, :], None, ALU.add)\
                    .then_inc(free, 1)
            elif kind in ("oa", "ga"):
                after_act(dve, t, 1)
                nc.vector.scalar_tensor_tensor(y_f[:, f, :], ev_t[:, g, :], 1.0, y_f[:, f, :],
                                               ALU.add, ALU.mult).then_inc(free, 1)
            elif kind == "gb":
                after_act(dve, t, 1)
                order.link(nc.vector.tensor_tensor(ev_t[:, g, :], ev_t[:, g, :], yb_f[:, f, :], ALU.mult))
                nc.vector.tensor_tensor(ev_t[:, g, :], ev_t[:, g, :], y_f[:, f, :], ALU.add)\
                    .then_inc(ev_dve, 1)
                after_act(dve, t, 2)
                nc.vector.tensor_tensor(y_lo[:, f, :], ev_t[:, g, :], y_hi[:, f, :].bitcast(F32),
                                        ALU.subtract).then_inc(free, 1)
            elif kind == "up":
                after_act(dve, t, 1, r)
                nc.vector.tensor_tensor(relu_t[:, g, :], ev_t[:, g, :], ps, ALU.mult)\
                    .then_inc(ev_dve, 1)
                after_act(dve, t, 2, r)
                nc.vector.tensor_tensor(up_lo[:, f, :], relu_t[:, g, :], up_hi[:, f, :].bitcast(F32),
                                        ALU.subtract).then_inc(free, 1)
            elif kind in ("wo", "down"):
                tile_done(dve, t, r)
                nc.vector.tensor_tensor(x_sb[:, i, cols], x_sb[:, i, cols], ps[:, 0:SLAB], ALU.add)\
                    .then_inc(free, 1)
            elif kind == "nz":
                after_act(dve, t, 1)
                branch, c = s // 4, slice(s % 4 * SLAB, (s % 4 + 1) * SLAB)
                e = ev_t[:, g, 0:SLAB]
                order.link(nc.vector.scalar_tensor_tensor(e, e, 1.0, ps[:, 0:SLAB], ALU.add, ALU.mult))
                if branch == 0:
                    nc.vector.tensor_tensor(o_a[:, i, c], o_a[:, i, c], e, ALU.mult).then_inc(free, 1)
                else:
                    o = o_b if branch == 1 else o_c
                    order.link(nc.vector.tensor_tensor(e, e, o[:, i, c], ALU.mult))
                    nc.vector.tensor_tensor(o_a[:, i, c], o_a[:, i, c], e, ALU.add).then_inc(free, 1)
            elif kind == "no":
                after_act(dve, t, 1)
                nc.vector.tensor_tensor(y2[:, i, cols], ps[:, 0:SLAB], gain_bc[:, cols], ALU.mult)\
                    .then_inc(free, 1)

        NORM_PARTS = ((0, TB - 1), (TB - 1, TB))

        def act_rms(act, which, block_there):
            for p, (b0, b1) in enumerate(NORM_PARTS):
                for b in range(b0, b1):
                    block_there(b)
                    ins = nc.scalar.activation(squares[b][:], x_sb[:, b, :], ACT.Square,
                                               accum_out=ssq[:, which, b:b + 1])
                ins.then_inc(sq_done, 1)
                act.wait_ge(var_ready, 2 * which + p + 1)
                nc.scalar.activation(rstd[:, which, b0:b1], ssq[:, which, b0:b1],
                                     ACT.Sqrt).then_inc(std_ready, 1)

        def dve_rms(dve, order, which):
            for p, (b0, b1) in enumerate(NORM_PARTS):
                dve.wait_ge(sq_done, 2 * which + p + 1)
                v = ssq[:, which, b0:b1]
                nc.vector.tensor_scalar(v, v, 1.0 / D, EPS, ALU.mult, ALU.add).then_inc(var_ready, 1)
                dve.wait_ge(std_ready, 2 * which + p + 1)
                r = rstd[:, which, b0:b1]
                order.link(nc.vector.reciprocal(r, r))
                for b in range(b0, b1):
                    nc.vector.tensor_scalar(diag[:, b, :], ident, rstd[:, which, b:b + 1], None,
                                            ALU.mult).then_inc(diag_ready, 1)

        block = ctx.enter_context(nc.Block())

        @block.sync
        def _(sp):
            def load_slab(n):
                mat, row0, col0, w, _, _ = slabs[n]
                if n >= 2:
                    sp.wait_ge(lo_done, n - 1)
                parts = ((0, 0, 32), (32, HA, w - 32)) if n == N_IF else ((0, 0, w),)
                for at, skip, m in parts:
                    src = mat[row0:row0 + D, col0 + skip:col0 + skip + m]
                    sp.dma_start(w_raw[n % 2][:, :, at:at + m], src.rearrange("(k p) n -> p k n", p=P))\
                        .then_inc(raw_landed[n % 2], 16)

            x_rows = a["x"].rearrange("(b p) n -> p b n", p=P)
            for b in range(TB):
                sp.dma_start(x_sb[:, b, :], x_rows[:, b, :]).then_inc(x_in[b], 16)
            for n in range(N_MLP):
                if n < 2:
                    sp.wait_ge(x_in[TB - 1 if n == 0 else 0], 16)
                load_slab(n)
            down_rows = a["w_down"].rearrange("(q k p) n -> p q k n", k=KT, p=P)
            up_cols = a["w_up"].rearrange("(k p) n -> p k n", p=P)
            with sp.Fori(0, 4) as r:
                for j in range(MLP_SLABS):
                    n = N_MLP + j
                    sp.wait_ge(lo_done, MLP_SLABS * r + (n - 1))
                    if j < 4:
                        src = up_cols[:, :, bass.ds(r * D + j * SLAB, SLAB)]
                    else:
                        src = down_rows[:, bass.ds(r, 1), :, (j - 4) * SLAB:(j - 3) * SLAB]
                        src = src.rearrange("p q k n -> p (q k) n")
                    sp.dma_start(w_raw[n % 2][:], src).then_inc(raw_landed[n % 2], 16)
            for n in range(N_NQ, N_ALL):
                if n == N_KC:
                    wait_tile_free(sp, tile_of[N_NQ] - 1)
                    for dst, name in ((w1k, "nsa_cmp_k_w1"), (w1v, "nsa_cmp_v_w1")):
                        sp.dma_start(dst[:], a[name].rearrange("(k p) n -> p k n", p=P))\
                            .then_inc(w1_in, 16)
                    for dst, name in ((w2k, "nsa_cmp_k_w2"), (w2v, "nsa_cmp_v_w2")):
                        sp.dma_start(dst[:], a[name].rearrange("(k p) n -> p k n", p=P))\
                            .then_inc(w1_in, 16)
                if n == N_NO:
                    sp.wait_ge(s_pv, 32)
                    sp.dma_start(gain_bc[:], a["post_gain"].partition_broadcast(P)).then_inc(gain_in, 16)
                load_slab(n)
            out_rows = out.rearrange("(b p) n -> p b n", p=P)
            for b in range(TB):
                sp.wait_ge(out_ready, b + 1)
                sp.dma_start(out_rows[:, b, :], xo[:, b, :]).then_inc(out_done, 16)
            sp.wait_ge(out_done, 16 * TB)

        @block.tensor
        def _(pe):
            def turn_vectors():
                pe.wait_ge(vec_in, 16 * ACT_VECS)
                pe.wait_ge(vec_in_pool, 16 * (len(VEC_PARTS) - ACT_VECS + 2))
                nc.tensor.transpose(ps_g[:, 0, 0:V_ROWS], vec_rows[:], ident[0:V_ROWS, 0:V_ROWS])\
                    .then_inc(vec_t, 1)
                pe.wait_ge(vec_ready, 1)

            feature_tiles(pe, N_QA, x_sb, True, lambda b: pe.wait_ge(diag_ready, b + 1), turn_vectors)
            for n in range(N_QA, N_QA + 4):
                mm_slab(pe, n, activation_ready=features_ready(pe, n, 0) if n == N_QA else None)
                if n == N_QA:
                    pe.wait_ge(nsa_in, 32)
                    nc.tensor.matmul(ps_t[0:HN, 512:1024], table[:], onehot[:, OH_REV:OH_REV + 512],
                                     start=True, stop=True)
                    nc.tensor.matmul(ps_t[0:HN, 1024:1152], table[:],
                                     onehot[:, OH_REV + 512:OH_REV + 640], start=True, stop=True)
                    for c in range(8):
                        mm = nc.tensor.matmul(ps_t[:, 1152 + HN * c:1152 + HN * (c + 1)],
                                              onehot[:, c * P:(c + 1) * P], table[:], start=True,
                                              stop=True)
                    mm.then_inc(oh_mm, 1)
            mm_slab(pe, N_IF)
            mm_slab(pe, N_VA)
            mm_slab(pe, N_VA + 1)
            mm_slab(pe, N_VA + 2)
            pe.wait_ge(u_ready, 1)
            pe.wait_ge(oh_cp, 2)
            for b in range(TB):
                mm = nc.tensor.transpose(ps_t[:, 1024 + b * HA:1024 + (b + 1) * HA],
                                         rows[3][:, b * P:(b + 1) * P], ident[0:HA, 0:HA])
            mm.then_inc(u_t, 1)
            mm_slab(pe, N_VA + 3)

            for h in range(HA):
                n, half, ft = N_QB + h, 64 * (h % 2), h // 2
                if h == 0:
                    pe.wait_ge(gate_dve, 2)
                    pe.wait_ge(u_col_ready, 1)
                    pe.wait_ge(gate_act, 2)
                    pe.wait_ge(ev_act, act_count[end_tile(N_QA + 3)])
                else:
                    pe.wait_ge(a_probs, h)
                nc.tensor.matmul(ps_t[:, 0:512], spread(h, HA), rows[0][:], start=True, stop=True)
                for b in range(TB):
                    at, w = CAUSAL_AT[b], CAUSAL_W[b]
                    mm = nc.tensor.matmul(ps_z[:, at:at + w], qk_a[half:half + 64, 4 + ft, b * P:(b + 1) * P],
                                          qk_a[half:half + 64, ft, b * P:S], start=True, stop=True)
                mm.then_inc(a_scores, 1)
                mm_tile(pe, n, 0)
                pe.wait_ge(a_probs, h + 1)
                if h == 0:
                    wait_tile_free(pe, end_tile(N_VA + 3) - 2)
                    wait_tile_free(pe, end_tile(N_VA + 3) - 1)
                else:
                    pe.wait_ge(a_num, h)
                for b in range(TB):
                    at, w = CAUSAL_AT[b], CAUSAL_W[b]
                    mm = nc.tensor.matmul(ps_t[:, 512 + b * P:1024], v_a[:, b, h * P:(h + 1) * P],
                                          decay[:, at:at + w], start=(b == 0), stop=(b == TB - 1))
                nc.tensor.matmul(ps_t[0:40, 1024:1024 + P], row_picker(h, 40), decay[:, 0:P],
                                 start=(h == 0), stop=False, skip_group_check=True).then_inc(a_pv, 1)
                mm_tile(pe, n, 1)
                pe.wait_ge(a_den, h + 1)
                nc.tensor.matmul(ps_t[0:40, 1024 + P:1536], row_picker(h, 40), den_sum[:],
                                 start=False, stop=False, skip_group_check=True)
                pe.wait_ge(a_num, h + 1)
                nc.tensor.matmul(ps_t[0:40, 1024:1536], row_picker(32 + h, 40), num_sq[:],
                                 start=False, stop=(h == HA - 1), skip_group_check=True)\
                    .then_inc(a_ssq, 1)

            for j in range(16):
                n = N_VB + j // 4
                mm_tile(pe, n, j % 4)
                for i in (2 * j, 2 * j + 1):
                    if j >= 8:
                        break
                    pe.wait_ge(b_sq, i + 1)
                    nc.tensor.matmul(ps_z[0:16, 0:512], row_picker(i, 16), sqs[:, i % 2, :],
                                     start=(i == 0), stop=(i == 15)).then_inc(b_stat, 1)
                if j >= 8:
                    if j == 8:
                        pe.wait_ge(b_rstd, 1)
                        pe.wait_ge(a_scale, 1)
                    for i in (2 * (j - 8), 2 * (j - 8) + 1):
                        if i >= 2:
                            pe.wait_ge(b_normed, i - 1)
                        at = 512 * (1 + i % 2)
                        nc.tensor.matmul(ps_z[:, at:at + 512], spread(i, 16), stat_row[:],
                                         start=True, stop=True).then_inc(b_bc, 1)
                    h = j - 8
                    if h >= 2:
                        pe.wait_ge(a_y, h - 1)
                    nc.tensor.matmul(ps_t[:, 512 * (h % 2):512 * (h % 2) + 512], spread(h, HA),
                                     rows[2][:], start=True, stop=True).then_inc(a_bc, 1)

            def sb_values(h):
                pe.wait_ge(b_attn, h + 1)
                if h >= 2:
                    pe.wait_ge(b_out, h - 1)
                if h == 0:
                    wait_tile_free(pe, end_tile(N_VB + 3) - 2)
                    wait_tile_free(pe, end_tile(N_VB + 3) - 1)
                    pe.wait_ge(a_y, HA)
                o = 512 * (h % 2)
                for b in range(TB):
                    at, w = CAUSAL_AT[b], CAUSAL_W[b]
                    mm = nc.tensor.matmul(ps_t[:, o + b * P:o + 512], v_b[:, b, h * P:(h + 1) * P],
                                          attn_b[:, at:at + w], start=(b == 0), stop=(b == TB - 1))
                mm.then_inc(b_pv, 1)

            for h in range(HB):
                n = N_OA + h
                if h == 0:
                    pe.wait_ge(b_normed, 16)
                else:
                    pe.wait_ge(b_attn, h)
                for b in (0, 1, 3, 2):
                    at, w = CAUSAL_AT[b], CAUSAL_W[b]
                    mm = nc.tensor.matmul(ps_z[:, at:at + w], k_b[:, h, b * P:(b + 1) * P],
                                          q_b[:, h, b * P:S], start=(b != 3), stop=True,
                                          skip_group_check=True)
                mm.then_inc(b_z, 1)
                if h:
                    sb_values(h - 1)
                mm_tile(pe, n, 0)
                mm_tile(pe, n, 1, ks=range(0, SB_CUT))
                pe.wait_ge(b_later, h + 1)
                for b in range(TB):
                    at, w = CAUSAL_AT[b], CAUSAL_W[b]
                    mm = nc.tensor.matmul(ps_z[:, at:at + w], cst[:, C_TRI:C_TRI + P], sp_t[:, at:at + w],
                                          start=False, stop=True, skip_group_check=True)
                    if b < 3:
                        nxt = sp_t[:, CAUSAL_AT[b + 1]:CAUSAL_AT[b + 1] + P]
                        mm = nc.tensor.matmul(ps_z[:, at + P:at + 2 * P], cst[:, C_NEG:C_NEG + P], nxt,
                                              start=False, stop=True, skip_group_check=True)
                    if b < 2:
                        mm = nc.tensor.matmul(ps_z[:, at + 2 * P:at + w], cst[:, C_NEG:C_NEG + P],
                                              (later0, later1)[b][:], start=False, stop=True,
                                              skip_group_check=True)
                mm.then_inc(b_sfx, 1)
                mm_tile(pe, n, 1, ks=range(SB_CUT, KT))
            sb_values(HB - 1)
            for n in range(N_GB, N_GB + 4):
                mm_slab(pe, n)
            for n in range(N_WO, N_WO + 4):
                mm_slab(pe, n, tile_of[N_GB] if n == N_WO else None, y_hi, y_lo)

            feature_tiles(pe, N_MLP, x_sb, True, lambda b: pe.wait_ge(diag_ready, TB + b + 1))
            with pe.Fori(0, 4) as r:
                for j in range(4):
                    mm_slab(pe, N_MLP + j, r=r,
                            activation_ready=features_ready(pe, N_MLP, 1) if j == 0 else None)
                for j in range(4, MLP_SLABS):
                    mm_slab(pe, N_MLP + j, tile_of[N_MLP] if j == 4 else None, up_hi, up_lo, r=r)

            feature_tiles(pe, N_NQ, x_sb, True, lambda b: pe.wait_ge(diag_ready, 2 * TB + b + 1))
            for n in range(N_NQ, N_KS + 1):
                mm_slab(pe, n, activation_ready=features_ready(pe, n, 2) if n == N_NQ else None)

            def compress(which, w1):
                pe.wait_ge(cmp_ready, which + 1)
                if which == 0:
                    pe.wait_ge(w1_in, 64)
                    pe.wait_ge(b_out, HB)
                    pe.wait_ge(b_attn, HB)
                else:
                    pe.wait_ge(hid_ready, 1)
                for m in range(2):
                    for k in range(16):
                        mm = nc.tensor.matmul(ps_t[:, m * 512:m * 512 + GN * NCMP],
                                              w1[:, k, m * P:(m + 1) * P], cmp_in[which][:, k, :],
                                              start=(k == 0), stop=(k == 15))
                mm.then_inc(hid_mm, 1)

            compress(0, w1k)
            wait_tile_free(pe, tile_of[N_NG])
            for b in range(TB):
                mm = nc.tensor.transpose(ps_t[:, 1024 + 48 * b:1024 + 48 * (b + 1)],
                                         gate_f[:, b * P:(b + 1) * P], ident[0:48, 0:48])
            mm.then_inc(gates_mm, 1)
            mm_tile(pe, N_KW, 0)
            pe.wait_ge(hid_ready, 1)
            for g in range(GN):
                half = 64 * (g % 2)
                for m in range(2):
                    mm = nc.tensor.matmul(ps_z[half:half + 64, g // 2 * NCMP:(g // 2 + 1) * NCMP],
                                          w2k[:, m, :], hid[:, m, g * NCMP:(g + 1) * NCMP],
                                          start=(m == 0), stop=(m == 1))
            mm.then_inc(kvc_mm, 1)
            compress(1, w1v)
            mm_tile(pe, N_KW, 1)

            def cmp_scores(b):
                if b == 0:
                    pe.wait_ge(kvc_ready, 1)
                    wait_tile_free(pe, end_tile(N_NQ + 3) - 1)
                    wait_tile_free(pe, end_tile(N_NQ + 3) - 2)
                elif b >= 2:
                    pe.wait_ge(c_log, b - 1)
                for f in range(8):
                    at = 512 * (b % 2) + f * 2 * CPAD
                    mm = nc.tensor.matmul(ps_z[:, at:at + 2 * CPAD], qn[:, f, b * P:(b + 1) * P],
                                          k_diag[:, f // 4, :, :], start=True, stop=True)
                mm.then_inc(c_scores, 1)

            def cmp_transposes(b):
                pe.wait_ge(c_exp, b + 1)
                if b >= 2:
                    pe.wait_ge(c_tc, b - 1)
                for g in range(GN):
                    at = 512 * (b % 2) + g * P
                    mm = nc.tensor.transpose(ps_t[:, at:at + P],
                                             clog[b % 2][:, 4 * g:4 * g + 4, :]
                                             .rearrange("p h c -> p (h c)"), ident)
                mm.then_inc(c_t, 1)

            def cmp_values(b):
                pe.wait_ge(c_tc, b + 1)
                if b == 0:
                    pe.wait_ge(kvc_ready, 2)
                else:
                    pe.wait_ge(c_out, b)
                for g in range(GN):
                    o = (ps_z if g < 2 else ps_t)[:, 1024 + g % 2 * 256:1024 + (g % 2 + 1) * 256]
                    mm = nc.tensor.matmul(o, cpt[b % 2][:, g, :],
                                          v_diag[:, g, :, :].rearrange("p h d -> p (h d)"),
                                          start=True, stop=True)
                mm.then_inc(c_pv, 1)

            cmp_scores(0)
            pe.wait_ge(hid_ready, 2)
            pe.wait_ge(hid_pad, 1)
            for g in range(GN):
                for m in range(2):
                    mm = nc.tensor.matmul(ps_z[:, 1024 + g * DH:1024 + (g + 1) * DH],
                                          hid_v[:, m, g, :, :].rearrange("p r c -> p (r c)"),
                                          w2v[:, m, :],
                                          start=(m == 0), stop=(m == 1))
            mm.then_inc(kvc_mm, 1)
            mm_tile(pe, N_VS, 0)
            mm_tile(pe, N_VS, 1)
            for b in range(TB):
                cmp_transposes(b)
                if b < TB - 1:
                    cmp_scores(b + 1)
                for n, i in CMP_TILES[b]:
                    mm_tile(pe, n, i)
                cmp_values(b)

            def unit(u):
                h = u % HN
                g = h // 4
                half = 64 * (g % 2)
                return h, g, half, (ks, kw)[u // HN], (vs, vw)[u // HN]

            def scores(u):
                h, g, half, keys, _ = unit(u)
                if u == 0:
                    pe.wait_ge(c_out, TB)
                else:
                    pe.wait_ge(s_max, u)
                for b in range(TB):
                    at, w = ROWS_AT[b], ROWS_W[b]
                    mm = nc.tensor.matmul(ps_z[:, at:at + w],
                                          qn[half:half + 64, 4 * (g // 2) + h % 4, b * P:(b + 1) * P],
                                          keys[half:half + 64, g // 2, 0:w], start=True, stop=True)
                mm.then_inc(s_scores, 1)

            scores(0)
            for u in range(32):
                h, g, half, _, values = unit(u)
                if u < 31:
                    scores(u + 1)
                pe.wait_ge(s_probs, u + 1)
                if u:
                    pe.wait_ge(s_ta, u)
                    pe.wait_ge(s_td, u)
                for b in range(TB):
                    for s in range(b + 1):
                        at = (b * (b + 1) // 2 + s) * P
                        if u and at == 1024:
                            pe.wait_ge(s_out, u)
                        mm = nc.tensor.transpose(ps_t[:, at:at + P],
                                                 probs[u % 2][:, ROWS_AT[b] + s * P:ROWS_AT[b] + (s + 1) * P],
                                                 ident)
                mm.then_inc(s_t, 1)
                mm_tile(pe, N_NZ + u // 4, u % 4)
                pe.wait_ge(s_ta, u + 1)
                pe.wait_ge(s_td, u + 1)
                if u:
                    pe.wait_ge(s_out, u)
                for b in range(TB):
                    for s in range(b + 1):
                        at = (b * (b + 1) // 2 + s) * P
                        mm = nc.tensor.matmul(ps_t[:, CAUSAL + b * DH:CAUSAL + (b + 1) * DH],
                                              probs_t[:, at:at + P], values[:, s, g * DH:(g + 1) * DH],
                                              start=(s == 0), stop=(s == b))
                mm.then_inc(s_pv, 1)
            for n in range(N_NZ + 8, N_NZ + 12):
                mm_slab(pe, n)
            feature_tiles(pe, N_NO, o_a, False,
                          lambda b: wait_tile_free(pe, tile_of[N_NZ + 11] + b))
            for n in range(N_NO, N_NO + 4):
                mm_slab(pe, n, activation_ready=features_ready(pe, n, 3) if n == N_NO else None)

        @block.scalar
        def _(act):
            order = Order(act, act_order)
            act.dma_start(cst[:], a["cst"]).then_inc(const_in, 16)
            for name, row0 in VEC_PARTS[:ACT_VECS]:
                r0, k = row0
                act.dma_start(vec_rows[r0:r0 + k, :], a[name]).then_inc(vec_in, 16)
            act_rms(act, 0, lambda b: act.wait_ge(x_in[b], 16))
            split_hi(act, 0)
            act.wait_ge(vec_ready, 1)
            for k in range(KT):
                act_feature_tile(act, N_QA, k, 0, V_MIX)
            for n in range(N_QA, N_QB):
                split_hi(act, n + 1)
                for i in range(tiles_of(n)):
                    act_evacuate(act, n, i)
                if n == N_VA:
                    wait_tile_free(act, tile_of[N_IF])
                    order.link(nc.scalar.activation(rows[0][:], rows[2][:], ACT.Abs))
                    order.link(nc.scalar.activation(rows[0][:], rows[0][:], ACT.Exp, scale=-1.0))
                    nc.scalar.activation(rows[0][:], rows[0][:], ACT.Ln, bias=1.0).then_inc(gate_act, 1)
                if n == N_VA + 2:
                    act.wait_ge(gate_dve, 1)
                    nc.scalar.activation(rows[1][:], rows[1][:], ACT.Exp, scale=-1.0).then_inc(gate_act, 1)

            for h in range(HA):
                n = N_QB + h
                split_hi(act, n + 1)
                act.wait_ge(a_scores, h + 1)
                if h:
                    act.wait_ge(a_pv, h)
                for b in range(TB):
                    at, w = CAUSAL_AT[b], CAUSAL_W[b]
                    ins = nc.scalar.activation(decay[:, at:at + w], ps_t[:, b * P:512], ACT.Exp,
                                               bias=u_col[:, b, h:h + 1])
                ins.then_inc(a_decay, 1)
                act_evacuate(act, n, 0)
                act.wait_ge(a_pv, h + 1)
                nc.scalar.copy(y_f[:, h, :], ps_t[:, 512:1024])
                if h:
                    act.wait_ge(a_ssq, h)
                nc.scalar.activation(num_sq[:], ps_t[:, 512:1024], ACT.Square).then_inc(a_num, 1)
                act_evacuate(act, n, 1)

            for j in range(16):
                n = N_VB + j // 4
                if j % 4 == 0:
                    split_hi(act, n + 1)
                if j == 0:
                    act.wait_ge(a_ssq, HA)
                    nc.scalar.activation(rows[2][:], ps_t[0:HA, 1024:1536], ACT.Abs).then_inc(a_fin_a, 1)
                    nc.scalar.mul(rows[3][:], ps_t[32:32 + HA, 1024:1536], 1.0 / P).then_inc(a_fin_a, 1)
                    wait_tile_free(act, end_tile(N_QB + 7) - 1)
                if j < 8:
                    for i in (2 * j, 2 * j + 1):
                        if i >= 2:
                            act.wait_ge(b_stat, i - 1)
                        src = q_b[:, i, :] if i < HB else k_b[:, i - HB, :]
                        nc.scalar.activation(sqs[:, i % 2, :], src, ACT.Square).then_inc(b_sq, 1)
                if j == 6:
                    act.wait_ge(a_fin_d, 1)
                    nc.scalar.activation(rows[3][:], rows[3][:], ACT.Sqrt).then_inc(a_fin_a, 1)
                act_evacuate(act, n, j % 4)
                if j == 7:
                    act.wait_ge(b_var, 1)
                    nc.scalar.activation(stat_row[:], stat_row[:], ACT.Sqrt).then_inc(b_std, 1)

            def sb_out(h):
                act.wait_ge(b_pv, h + 1)
                nc.scalar.copy(yb_f[:, h, :], ps_t[:, 512 * (h % 2):512 * (h % 2) + 512]).then_inc(b_out, 1)

            for h in range(HB):
                n = N_OA + h
                split_hi(act, n + 1)
                act.wait_ge(b_z, h + 1)
                if h:
                    act.wait_ge(b_sfx, h)
                else:
                    act.wait_ge(b_normed, 16)
                z = ps_z[:, 0:CAUSAL]
                order.link(nc.scalar.activation(sp_t[:], z, ACT.Abs))
                order.link(nc.scalar.activation(sp_t[:], sp_t[:], ACT.Exp, scale=-1.0))
                nc.scalar.activation(sp_t[:], sp_t[:], ACT.Ln, bias=1.0).then_inc(b_ln, 1)
                if h:
                    sb_out(h - 1)
                act_evacuate(act, n, 0)
                act.wait_ge(b_min, h + 1)
                if h:
                    act.wait_ge(b_pv, h)
                nc.scalar.activation(attn_b[:], z, ACT.Exp).then_inc(b_attn, 1)
                act_evacuate(act, n, 1)
            sb_out(HB - 1)
            for n in range(N_GB, N_MLP):
                split_hi(act, n + 1)
                for i in range(tiles_of(n)):
                    act_evacuate(act, n, i)

            act_rms(act, 1, lambda b: wait_tile_free(act, tile_of[N_WO + 3] + b))
            for k in range(KT):
                act_feature_tile(act, N_MLP, k, 1, V_MLP)
            with act.Fori(0, 4) as r:
                for j in range(MLP_SLABS):
                    split_hi(act, N_MLP + j + 1, r)
                    for i in range(tiles_of(N_MLP + j)):
                        act_evacuate(act, N_MLP + j, i, r)
            act_rms(act, 2, lambda b: wait_tile_free(act, tile_of[N_NQ - 1] + b))
            for k in range(KT):
                act_feature_tile(act, N_NQ, k, 2, V_PRE)
            def hidden(which):
                act.wait_ge(hid_mm, which + 1)
                for m in range(2):
                    src, dst = ps_t[:, m * 512:m * 512 + GN * NCMP], hid[:, m, :]
                    if which:
                        src = src.rearrange("p (g c) -> p g c", c=NCMP).unsqueeze(2)\
                            .broadcast_to([P, GN, 4, NCMP])
                        dst = hid_v[:, m, :, :, 0:NCMP]
                    ins = nc.scalar.activation(dst, src, ACT.Silu)
                ins.then_inc(hid_ready, 1)

            for n in range(N_NQ, N_KS + 1):
                split_hi(act, n + 1)
                if n == N_KC:
                    wait_tile_free(act, norm_tile_of[N_NQ] + 1)
                for i in range(tiles_of(n)):
                    act_evacuate(act, n, i)
            split_hi(act, N_KW + 1)
            hidden(0)
            act_evacuate(act, N_KW, 0)
            hidden(1)
            act_evacuate(act, N_KW, 1)

            def cmp_exp(b):
                act.wait_ge(c_log, b + 1)
                log = clog[b % 2][:, :, 0:NCMP]
                nc.scalar.activation(log, log, ACT.Exp).then_inc(c_exp, 1)

            split_hi(act, N_VS + 1)
            cmp_exp(0)
            act_evacuate(act, N_VS, 0)
            act_evacuate(act, N_VS, 1)
            for b in range(TB):
                act.wait_ge(c_t, b + 1)
                if b >= 2:
                    act.wait_ge(c_pv, b - 1)
                nc.scalar.copy(cpt[b % 2][:], ps_t[:, 512 * (b % 2):512 * (b % 2) + 512]
                               .rearrange("p (g t) -> p g t", t=P)).then_inc(c_tc, 1)
                if b < TB - 1:
                    cmp_exp(b + 1)
                for n, i in CMP_TILES[b]:
                    act_evacuate(act, n, i)
                    if (n, i) == (N_VS, 3):
                        split_hi(act, N_VW + 1)

            def exps(u):
                act.wait_ge(s_max, u + 1)
                for b in range(TB):
                    p = probs[u % 2][:, ROWS_AT[b]:ROWS_AT[b] + ROWS_W[b]]
                    ins = nc.scalar.activation(p, p, ACT.Exp, bias=rneg[:, u % 2, b:b + 1],
                                               accum_out=rsum[:, u % 2, b:b + 1])
                ins.then_inc(s_probs, 1)

            exps(0)
            for u in range(32):
                if u % 4 == 0:
                    split_hi(act, N_NZ + u // 4 + 1)
                act.wait_ge(s_t, u + 1)
                if u:
                    act.wait_ge(s_pv, u)
                nc.scalar.copy(probs_t[:, 0:512], ps_t[:, 0:512]).then_inc(s_ta, 1)
                if u < 31:
                    exps(u + 1)
                act_evacuate(act, N_NZ + u // 4, u % 4)
            for n in range(N_NZ + 8, N_NO):
                split_hi(act, n + 1)
                for i in range(tiles_of(n)):
                    act_evacuate(act, n, i)
            for k in range(KT):
                act_feature_tile(act, N_NO, k, 3, None)
            for n in range(N_NO, N_ALL):
                split_hi(act, n + 1)
                for i in range(tiles_of(n)):
                    act_evacuate(act, n, i)
                    if n == N_ALL - 1:
                        act.wait_ge(var_ready, 6 + i + 1)
                        r = rstd[:, 3, i:i + 1]
                        nc.scalar.activation(r, r, ACT.Sqrt).then_inc(std_ready, 1)

        @block.vector
        def _(dve):
            order = Order(dve, dve_order)
            order.link(nc.vector.memset(ones_row[:], 1.0))
            dve.wait_ge(const_in, 16)
            dve_rms(dve, order, 0)
            dve.wait_ge(vec_t, 1)
            nc.vector.tensor_copy(vec[:], ps_g[:, 0, 0:V_ROWS]).then_inc(vec_ready, 1)
            dve.wait_ge(vec_ready, 1)
            order.link(nc.vector.tensor_scalar(gq_s[:], col(V_QN, 0), HD ** -0.5, None, ALU.mult))
            order.link(nc.vector.memset(k_diag[:], 0.0))
            nc.vector.tensor_scalar(mn_q[:], vec[:, V_MNORM:V_MNORM + HA], 0.25, None, ALU.mult)
            order.link(nc.vector.tensor_scalar(half_bg[:], vec[:, V_BGATE:V_BGATE + HA], 0.5, None, ALU.mult))
            split_lo(dve, 0)
            for k in range(KT):
                dve_feature_tile(dve, N_QA, k, 0, V_MIX)
            for n in range(N_QA, N_QB):
                for i in range(tiles_of(n)):
                    if i == (1 if n < N_IF else 0):
                        split_lo(dve, n + 1)
                    dve_evacuate(dve, order, n, i)
                if n == N_QA:
                    dve.wait_ge(oh_mm, 1)
                    nc.vector.tensor_copy(bias_rev_sb[:], ps_t[0:HN, 512:1152]).then_inc(oh_cp, 1)
                    nc.vector.tensor_copy(bias_fwd_sb[:], ps_t[:, 1152:1152 + 8 * HN]
                                          .rearrange("p (c h) -> p c h", h=HN)).then_inc(oh_cp, 1)
                if n == N_VA:
                    wait_tile_free(dve, tile_of[N_IF])
                    dve.wait_ge(gate_act, 1)
                    order.link(nc.vector.tensor_scalar(rows[1][:], rows[2][:], 0.0, None, ALU.min))
                    order.link(nc.vector.tensor_tensor(rows[1][:], rows[1][:], rows[0][:], ALU.subtract))
                    order.link(nc.vector.tensor_tensor_scan(rows[2][:], ones_row[:], rows[1][:], 0.0,
                                                            ALU.mult, ALU.add))
                    nc.vector.tensor_tensor(rows[3][:], rows[3][:], rows[2][:], ALU.subtract)\
                        .then_inc(u_ready, 1)
                    dve.wait_ge(u_ready, 1)
                    order.link(nc.vector.tensor_tensor_scan(rows[0][:], rows[3][:], rows[3][:], 0.0,
                                                            ALU.max, ALU.max))
                    nc.vector.tensor_tensor(rows[1][:], rows[2][:], rows[0][:], ALU.add).then_inc(gate_dve, 1)
                    nc.vector.tensor_scalar(rows[0][:], rows[0][:], -1.0, None, ALU.mult).then_inc(gate_dve, 1)
                if n == N_VA + 2:
                    dve.wait_ge(u_t, 1)
                    nc.vector.tensor_copy(u_col[:], ps_t[:, 1024:1024 + TB * HA]
                                          .rearrange("p (b h) -> p b h", h=HA)).then_inc(u_col_ready, 1)

            for h in range(HA):
                split_lo(dve, N_QB + h + 1)
                dve.wait_ge(a_masked, h + 1)
                nc.vector.scalar_tensor_tensor(decay[:], ps_z[:, 0:CAUSAL], DQK ** -0.5, decay[:], ALU.mult,
                                               ALU.mult).then_inc(a_probs, 1)

            for j in range(16):
                n = N_VB + j // 4
                if j % 4 == 0:
                    split_lo(dve, n + 1)
                if j == 0:
                    dve.wait_ge(a_fin_a, 2)
                    order.link(nc.vector.tensor_tensor(rows[2][:], rows[2][:], rows[1][:], ALU.max))
                    order.link(nc.vector.reciprocal(rows[2][:], rows[2][:]))
                    order.link(nc.vector.tensor_tensor(rows[3][:], rows[3][:], rows[2][:], ALU.mult))
                    order.link(nc.vector.tensor_tensor(rows[3][:], rows[3][:], rows[2][:], ALU.mult))
                    nc.vector.tensor_scalar(rows[3][:], rows[3][:], EPS, None, ALU.add).then_inc(a_fin_d, 1)
                if j == 7:
                    dve.wait_ge(a_fin_a, 3)
                    order.link(nc.vector.reciprocal(rows[3][:], rows[3][:]))
                    nc.vector.tensor_tensor(rows[2][:], rows[2][:], rows[3][:], ALU.mult).then_inc(a_scale, 1)
                    dve.wait_ge(b_stat, 16)
                    nc.vector.tensor_scalar(stat_row[:], ps_z[0:16, 0:512], 1.0 / HD, EPS, ALU.mult,
                                            ALU.add).then_inc(b_var, 1)
                    dve.wait_ge(b_std, 1)
                    nc.vector.reciprocal(stat_row[:], stat_row[:]).then_inc(b_rstd, 1)
                if j >= 8:
                    for i in (2 * (j - 8), 2 * (j - 8) + 1):
                        dve.wait_ge(b_bc, i + 1)
                        q = q_b[:, i, :] if i < HB else k_b[:, i - HB, :]
                        gain = gq_s[:] if i < HB else col(V_KN, 0)
                        at = 512 * (1 + i % 2)
                        nc.vector.scalar_tensor_tensor(q, q, gain, ps_z[:, at:at + 512], ALU.mult,
                                                       ALU.mult).then_inc(b_normed, 1)
                    h = j - 8
                    dve.wait_ge(a_bc, h + 1)
                    at = 512 * (h % 2)
                    nc.vector.scalar_tensor_tensor(y_f[:, h, :], y_f[:, h, :], mn_q[:, h:h + 1],
                                                   ps_t[:, at:at + 512], ALU.mult, ALU.mult).then_inc(a_y, 1)

            for h in range(HB):
                n = N_OA + h
                split_lo(dve, n + 1)
                dve.wait_ge(b_ln, h + 1)
                nc.vector.scalar_tensor_tensor(sp_t[:], ps_z[:, 0:CAUSAL], 0.0, sp_t[:], ALU.max,
                                               ALU.add).then_inc(b_sp, 1)
                if h == 0:
                    dve.wait_ge(a_y, HA)
                dve_evacuate(dve, order, n, 0)
                dve.wait_ge(b_sfx, h + 1)
                for b in range(TB):
                    zd = ps_z[:, CAUSAL_AT[b]:CAUSAL_AT[b] + P]
                    ins = nc.vector.tensor_tensor(zd, zd, cst[:, C_MIN:C_MIN + P], ALU.min)
                ins.then_inc(b_min, 1)
                dve_evacuate(dve, order, n, 1)
            dve.wait_ge(b_out, HB)
            for n in range(N_GB, N_MLP):
                split_lo(dve, n + 1)
                for i in range(tiles_of(n)):
                    dve_evacuate(dve, order, n, i)
            dve_rms(dve, order, 1)
            for k in range(KT):
                dve_feature_tile(dve, N_MLP, k, 1, V_MLP)
            with dve.Fori(0, 4) as r:
                for j in range(MLP_SLABS):
                    split_lo(dve, N_MLP + j + 1, r)
                    for i in range(tiles_of(N_MLP + j)):
                        dve_evacuate(dve, order, N_MLP + j, i, r)
            dve_rms(dve, order, 2)
            for k in range(KT):
                dve_feature_tile(dve, N_NQ, k, 2, V_PRE)
            for n in range(N_NQ, N_KS + 1):
                split_lo(dve, n + 1)
            nc.vector.memset(hid_v[:, :, :, :, NCMP:CPAD], 0.0).then_inc(hid_pad, 1)
            dve.wait_ge(gates_mm, 1)
            nc.vector.tensor_scalar(gates_n[:], ps_t[:, 1024:1024 + TB * 48]
                                    .rearrange("p (b c) -> p b c", c=48), 1.0, 0.25, ALU.add,
                                    ALU.mult).then_inc(gates_ready, 1)
            split_lo(dve, N_KW + 1)
            dve.wait_ge(kvc_mm, 1)
            for e in range(2):
                half = slice(64 * e, 64 * e + 64)
                ins = nc.vector.tensor_copy(k_diag[half, :, e, 0:NCMP],
                                            ps_z[half, 0:2 * NCMP].rearrange("p (t c) -> p t c", c=NCMP))
            ins.then_inc(kvc_ready, 1)
            dve.wait_ge(hid_mm, 2)
            order.link(nc.vector.memset(v_diag[:], 0.0))
            for i in range(2):
                order.link(nc.vector.memset(clog[i][:, :, NCMP:CPAD], 0.0))

            def cmp_logits(b):
                dve.wait_ge(c_scores, b + 1)
                if b == 0:
                    dve.wait_ge(cb_ready, 16 * TB)
                if b >= 2:
                    dve.wait_ge(c_t, b - 1)
                log = clog[b % 2][:, :, 0:NCMP]
                for gg in range(2):
                    at = 512 * (b % 2) + 4 * gg * 2 * CPAD
                    ins = nc.vector.tensor_tensor(
                        log[:, 8 * gg:8 * gg + 8, :].rearrange("p (e r) c -> p e r c", e=2),
                        ps_z[:, at:at + 8 * CPAD].rearrange("p (r e c) -> p e r c", e=2, c=CPAD)[:, :, :, 0:NCMP],
                        cbias[:, b, :, 8 * gg:8 * gg + 8].rearrange("p c (e r) -> p e r c", e=2), ALU.add)
                order.link(ins)
                order.link(nc.vector.tensor_reduce(cmax[:], log, AX_X, ALU.max))
                nc.vector.tensor_tensor(log, log, cmax[:].unsqueeze(2).broadcast_to([P, HN, NCMP]),
                                        ALU.subtract).then_inc(c_log, 1)

            def cmp_sums(b):
                dve.wait_ge(c_exp, b + 1)
                cs = csum[:, b % 2, :]
                order.link(nc.vector.tensor_reduce(cs, clog[b % 2][:, :, 0:NCMP], AX_X, ALU.add))
                order.link(nc.vector.reciprocal(cs, cs))
                order.link(nc.vector.scalar_tensor_tensor(cs, cs, cst[:, C_VALID + b:C_VALID + b + 1],
                                                          gates_n[:, b, 0:HN], ALU.mult, ALU.mult))

            split_lo(dve, N_VS + 1)
            cmp_logits(0)
            dve.wait_ge(gates_ready, 1)
            dve.wait_ge(kvc_mm, 2)
            for r in range(4):
                rows_r = slice(CPAD * r, CPAD * (r + 1))
                ins = nc.vector.tensor_copy(v_diag[rows_r, :, r, :], ps_z[rows_r, 1024:1024 + GN * DH]
                                            .rearrange("p (g d) -> p g d", d=DH))
            ins.then_inc(kvc_ready, 1)
            cmp_sums(0)
            for b in range(TB):
                if b < TB - 1:
                    cmp_logits(b + 1)
                    cmp_sums(b + 1)
                if b == 1:
                    split_lo(dve, N_VW + 1)
                dve.wait_ge(c_pv, b + 1)
                for e, ps in enumerate((ps_z, ps_t)):
                    ins = nc.vector.tensor_tensor(
                        o_a[:, b, 512 * e:512 * e + 512].rearrange("p (h d) -> p h d", d=DH),
                        ps[:, 1024:1536].rearrange("p (h d) -> p h d", d=DH),
                        csum[:, b % 2, 8 * e:8 * e + 8].unsqueeze(2).broadcast_to([P, 8, DH]), ALU.mult)
                ins.then_inc(c_out, 1)

            def row_max(u):
                dve.wait_ge(s_scores, u + 1)
                dve.wait_ge(bias_in[u % 2], 16 * (u // 2 + 1))
                if u >= 2:
                    dve.wait_ge(s_t, u - 1)
                elif u == 0:
                    dve.wait_ge(c_pv, TB)
                for b in range(TB):
                    at, w = ROWS_AT[b], ROWS_W[b]
                    ins = nc.vector.tensor_tensor_reduce(probs[u % 2][:, at:at + w], ps_z[:, at:at + w],
                                                         tile_t[u % 2][:, S - w:S], 1.0, -3.0e38, ALU.add,
                                                         ALU.max, rmax[:, u % 2, b:b + 1])
                order.link(ins)
                nc.vector.tensor_scalar(rneg[:, u % 2, :], rmax[:, u % 2, :], -1.0, None, ALU.mult)\
                    .then_inc(s_max, 1)

            row_max(0)
            for u in range(32):
                h, branch = u % HN, 1 + u // HN
                if u % 4 == 0:
                    split_lo(dve, N_NZ + u // 4 + 1)
                if u < 31:
                    row_max(u + 1)
                dve.wait_ge(s_t, u + 1)
                if u:
                    dve.wait_ge(s_pv, u)
                nc.vector.tensor_copy(probs_t[:, 512:CAUSAL], ps_t[:, 512:CAUSAL]).then_inc(s_td, 1)
                dve_evacuate(dve, order, N_NZ + u // 4, u % 4)
                dve.wait_ge(s_probs, u + 1)
                order.link(nc.vector.reciprocal(rgate[:], rsum[:, u % 2, :]))
                order.link(nc.vector.tensor_tensor(rgate[:], rgate[:],
                                                   gates_n[:, :, branch * HN + h], ALU.mult))
                dve.wait_ge(s_pv, u + 1)
                o = o_b if branch == 1 else o_c
                nc.vector.tensor_tensor(o[:, :, h * DH:(h + 1) * DH],
                                        ps_t[:, CAUSAL:CAUSAL + TB * DH].rearrange("p (b d) -> p b d", d=DH),
                                        rgate[:].unsqueeze(2).broadcast_to([P, TB, DH]),
                                        ALU.mult).then_inc(s_out, 1)
            dve.wait_ge(s_out, 32)
            for n in range(N_NZ + 8, N_NO):
                split_lo(dve, n + 1)
                for i in range(tiles_of(n)):
                    dve_evacuate(dve, order, n, i)
            for k in range(KT):
                dve_feature_tile(dve, N_NO, k, 3, None)
            dve.wait_ge(gain_in, 16)
            for n in range(N_NO, N_ALL):
                split_lo(dve, n + 1)
                for i in range(tiles_of(n)):
                    dve_evacuate(dve, order, n, i)
                    if n == N_ALL - 1:
                        r = rstd[:, 3, i:i + 1]
                        order.link(nc.vector.tensor_reduce(r, ssq_y[:, i, :], AX_X, ALU.add))
                        nc.vector.tensor_scalar(r, r, 1.0 / D, EPS, ALU.mult, ALU.add)\
                            .then_inc(var_ready, 1)
                        dve.wait_ge(std_ready, 6 + i + 1)
                        order.link(nc.vector.reciprocal(r, r))
                        wait_tile_free(dve, tile_of[n] + i)
                        nc.vector.scalar_tensor_tensor(xo[:, i, :], y2[:, i, :], r, x_sb[:, i, :],
                                                       ALU.mult, ALU.add).then_inc(out_ready, 1)

        @block.gpsimd
        def _(pool):
            order = Order(pool, pool_order)

            def mask_diagonals(t, keep):
                for b in range(TB):
                    d = t[:, CAUSAL_AT[b]:CAUSAL_AT[b] + P]
                    ins = nc.gpsimd.affine_select(out=d, in_=d, compare_op=keep, fill=0.0, base=0,
                                                  pattern=[[1, P]], channel_multiplier=-1)
                return ins

            for name, row0 in VEC_PARTS[ACT_VECS:]:
                r0, k = row0
                pool.dma_start(vec_rows[r0:r0 + k, :], a[name]).then_inc(vec_in_pool, 16)
            for c in range(2):
                pool.dma_start(bif[32 * c:32 * c + HA, :], a["b_if"][HA * c:HA * (c + 1), :])\
                    .then_inc(vec_in_pool, 16)
            pool.dma_start(table[:], a["table"]).then_inc(nsa_in, 16)
            pool.dma_start(onehot[:], a["onehot"]).then_inc(nsa_in, 16)

            pool.wait_ge(oh_cp, 2)
            pool.dma_start(a["bias_rev"], bias_rev_sb[:].unsqueeze(1).broadcast_to([HN, P, REV]))\
                .then_inc(bias_out, 16)
            pool.dma_start(a["bias_fwd"].rearrange("(c p) h -> p c h", p=P), bias_fwd_sb[:])\
                .then_inc(bias_out, 16)

            for h in range(HA):
                pool.wait_ge(a_decay, h + 1)
                mask_diagonals(decay, ALU.is_ge).then_inc(a_masked, 1)
                pool.wait_ge(a_probs, h + 1)
                if h:
                    pool.wait_ge(a_ssq, h)
                s0, s1, s2, s3 = (decay[:, CAUSAL_AT[b]:CAUSAL_AT[b] + CAUSAL_W[b]] for b in range(TB))
                order.link(nc.gpsimd.tensor_tensor(den_sum[:], s0[:, P:S], s1, ALU.add))
                order.link(nc.gpsimd.tensor_tensor(den_sum[:, P:], den_sum[:, P:], s2, ALU.add))
                nc.gpsimd.tensor_tensor(den_sum[:, 2 * P:], den_sum[:, 2 * P:], s3, ALU.add)\
                    .then_inc(a_den, 1)
            for h in range(HB):
                pool.wait_ge(b_sp, h + 1)
                if h:
                    pool.wait_ge(b_sfx, h)
                order.link(mask_diagonals(sp_t, ALU.is_gt))
                s1, s2, s3 = (sp_t[:, CAUSAL_AT[b]:CAUSAL_AT[b] + CAUSAL_W[b]] for b in (1, 2, 3))
                order.link(nc.gpsimd.tensor_tensor(later1[:], s2[:, P:2 * P], s3, ALU.add))
                nc.gpsimd.tensor_tensor(later0[:, 0:P], s1[:, P:2 * P], s2[:, 0:P], ALU.add)
                nc.gpsimd.tensor_tensor(later0[:, P:2 * P], s1[:, 2 * P:3 * P], later1[:], ALU.add)\
                    .then_inc(b_later, 1)

            for which, (pair, pos, n) in enumerate(((pairk, V_POSK, N_KC), (pairv, V_POSV, N_VC))):
                wait_tile_free(pool, end_tile(n) - 2)
                wait_tile_free(pool, end_tile(n) - 1)
                if which:
                    pool.wait_ge(cmp_ready, 1)
                for k in range(16):
                    ins = nc.gpsimd.tensor_scalar(
                        cmp_in[which][:, k, :].rearrange("p (g c) -> p g c", c=NCMP),
                        pair[:, :, 2 * k:2 * k + CSTRIDE * (NCMP - 1) + 1:CSTRIDE], col(pos, k), None, ALU.add)
                ins.then_inc(cmp_ready, 1)

            pool.wait_ge(bias_out, 32)
            pool.wait_ge(cmp_ready, 2)
            fwd = a["bias_fwd"]
            for b in range(TB):
                pool.dma_start(cbias[:, b], bass.AP(fwd.tensor, (S - 1 - (CLEN - 1) + b * P) * HN,
                                                    [[HN, P], [-CSTRIDE * HN, NCMP], [1, HN]]))\
                    .then_inc(cb_ready, 16)
            pool.wait_ge(gates_mm, 1)
            rev = a["bias_rev"]
            for u in range(32):
                if u >= 2:
                    pool.wait_ge(s_max, u - 1)
                pool.dma_start(tile_t[u % 2][:], bass.AP(rev.tensor, (u % HN) * P * REV + P - 1,
                                                         [[REV - 1, P], [1, S]])).then_inc(bias_in[u % 2], 16)


DRAM = dict(
    x=("x", (S, D)), w_in=("w_in", (D, 8208)), w_out=("w_out", (D, D)), w_up=("w_up", (D, DFF)),
    w_down=("w_down", (DFF, D)), nsa_w_in=("nsa_w_in_2", (D, 5680)), nsa_w_out=("nsa_w_out_2", (D, D)),
    nsa_cmp_k_w1=("nsa_cmp_k_w1_2", (2048, 256)), nsa_cmp_v_w1=("nsa_cmp_v_w1_2", (2048, 256)),
    nsa_cmp_k_w2=("nsa_cmp_k_w2_2", (256, DH)), nsa_cmp_v_w2=("nsa_cmp_v_w2_2", (256, DH)),
    mix_g=("norm_mix_g", (8, P)), mlp_g=("norm_mlp_g", (8, P)), pre_g=("pre_norm_gain_2", (8, P)),
    mnorm_g=("mlstm_norm_g", (8, P)), conv_w=("conv_w", (32, P)), b_gate=("b_gate", (16, P)),
    pos_k=("nsa_cmp_k_pos_2", (16, P)), pos_v=("nsa_cmp_v_pos_2", (16, P)),
    qn_g=("sb_q_norm_g", (1, P)), kn_g=("sb_k_norm_g", (1, P)), b_if=("b_if", (16, 1)),
    post_gain=("post_norm_gain_2", (D,)),
)


def build(nc, inputs):
    arrays, aps = {}, {}

    def bring(name, arr):
        arrays[f"in_{name}"] = arr
        aps[name] = nc.dram_tensor(f"in_{name}", arr.shape, F32, kind="ExternalInput").ap()

    for name, (key, shape) in DRAM.items():
        bring(name, np.ascontiguousarray(np.asarray(inputs[key]).reshape(shape)))
    bring("cst", constants())
    bring("onehot", bucket_table())
    table = np.asarray(inputs["rel_bias_table_2"])
    bring("table", np.ascontiguousarray(np.concatenate([table, np.full((1, HN), NEG, table.dtype)])))
    aps["bias_rev"] = nc.dram_tensor("bias_rev_dram", (HN, P, REV), F32, kind="Internal").ap()
    aps["bias_fwd"] = nc.dram_tensor("bias_fwd_dram", (1024, HN), F32, kind="Internal").ap()
    out = nc.dram_tensor("out_dram", (S, D), F32, kind="ExternalOutput").ap()
    program(nc, aps, out)
    return arrays


def kernel(**inputs):
    import concourse.bacc as bacc
    from concourse.bass_utils import run_bass_kernel_spmd
    nc = bacc.Bacc("TRN2", target_bir_lowering=False, num_devices=1)
    arrays = build(nc, inputs)
    r = run_bass_kernel_spmd(nc, [arrays], core_ids=[0])
    return r.results[0]["out_dram"].reshape(1, S, D)
```

```python
from contextlib import ExitStack

import numpy as np
import concourse.bass as bass
from concourse import mybir

ALU = mybir.AluOpType
ACT = mybir.ActivationFunctionType
AX_X = mybir.AxisListType.X
F32 = mybir.dt.float32
F32R = mybir.dt.float32r

P = 128
S = 512
D = 1024
TB = S // P
KT = D // P
SLAB = 256
EPS = 1e-6
HA = 8
DQK = 64
HB = 8
HD = 128
DFF = 4 * D
HN = 16
DH = 64
GN = 4
NCMP = 31
CPAD = 32
CSTRIDE = 16
CLEN = 32
BUCKETS = 32
NEG = -1e30

QA, KA, VA, OA, IF = 0, 512, 1024, 2048, 3072
QB, KB, VB, GA, GB = 3088, 4112, 5136, 6160, 7184
NQ, NKC, NVC, NKS, NVS, NKW, NVW, NG, NZ = 0, 1024, 1280, 1536, 1792, 2048, 2304, 2560, 2608

CAUSAL_AT = (0, 512, 1024, 896)
CAUSAL_W = (512, 384, 256, 128)
CAUSAL = 1280
ROWS_AT = (896, 1024, 512, 0)
ROWS_W = (128, 256, 384, 512)

V_MIX, V_MLP, V_PRE, V_MNORM, V_CONV, V_BGATE, V_POSK, V_POSV, V_QN, V_KN, V_ROWS = (
    0, 8, 16, 24, 32, 64, 80, 96, 112, 113, 114)

C_ID, C_TRI, C_NEG, C_MIN, C_STRIP, C_VALID, C_ALL = 0, 128, 256, 384, 512, 592, 596
REV = S + P
OH_REV, OH_W = 1024, 1024 + REV

VEC_PARTS = (("mix_g", (V_MIX, 8)), ("mlp_g", (V_MLP, 8)), ("pre_g", (V_PRE, 8)),
             ("mnorm_g", (V_MNORM, 8)), ("conv_w", (V_CONV, 32)), ("b_gate", (V_BGATE, 16)),
             ("pos_k", (V_POSK, 16)), ("pos_v", (V_POSV, 16)), ("qn_g", (V_QN, 1)), ("kn_g", (V_KN, 1)))
SYNC_VECS = 5


def constants():
    j = np.arange(P)[:, None]
    s = np.arange(P)[None, :]
    c = np.zeros((P, C_ALL), np.float32)
    c[:, C_ID:C_ID + P] = j == s
    c[:, C_TRI:C_TRI + P] = np.where(j >= s, -1.0, 0.0)
    c[:, C_NEG:C_NEG + P] = -1.0
    c[:, C_MIN:C_MIN + P] = np.where(j < s, -NEG, NEG)
    c[:, C_STRIP + 39] = 1.0
    t = np.arange(TB)[None, :] * P + j
    c[:, C_VALID:C_VALID + TB] = t >= CLEN - 1
    return c


def bucket_table():
    dist = np.concatenate([np.arange(OH_REV) - 511, 511 - np.arange(OH_W - OH_REV)])
    n = np.maximum(dist, 0)
    half = BUCKETS // 2
    large = half + (np.log(np.maximum(n, 1) / half) / np.log(128 / half) * half + 1e-9).astype(int)
    bucket = np.where(n < half, n, np.minimum(large, BUCKETS - 1))
    t = (bucket[None, :] == np.arange(BUCKETS)[:, None]) & (dist >= 0)[None, :]
    return np.concatenate([t, (dist < 0)[None, :]]).astype(np.float32)


class Order:

    def __init__(self, eng, sem):
        self.eng, self.sem, self.n, self.shift = eng, sem, 0, 0

    def link(self, ins):
        ins.then_inc(self.sem, 1)
        self.n += 1
        self.eng.wait_ge(self.sem, self.n + self.shift)


def program(nc, a, out):
    with ExitStack() as ctx:
        def sem(name):
            return ctx.enter_context(nc.semaphore(name))

        base = -(-nc.sbuf_base // 64) * 64
        top = [base]

        def sb(name, shape, dt=F32, at=None):
            size = int(np.prod(shape[1:])) * 4
            if at is None:
                at = top[0]
                top[0] += -(-size // 32) * 32
                assert top[0] <= nc.sbuf_usable_end, (name, top[0])
            return nc.alloc_sbuf_tensor_at(name, shape, dt, offset=at)

        x_sb = sb("x_sb", [P, TB, D])
        act_hi = sb("act_hi", [P, KT, S], F32R)
        act_lo = sb("act_lo", [P, KT, S], F32R)
        w_raw = [sb(f"w_raw{i}", [P, KT, SLAB]) for i in range(2)]
        w_hi = [sb(f"w_hi{i}", [P, KT, SLAB], F32R) for i in range(2)]
        w_lo = [sb(f"w_lo{i}", [P, KT, SLAB], F32R) for i in range(2)]
        arena = top[0]
        K16 = 16384
        top[0] += 6 * K16

        xn = [sb(f"xn{b}", [P, D], at=arena + 2 * K16 + 4096 * b if b < 3
                 else arena + 5 * K16) for b in range(TB)]

        qk_a = sb("qk_a", [P, 8, S], at=arena)
        v_a = sb("v_a", [P, TB, D], at=arena + K16)
        y_f = sb("y_f", [P, 8, S], at=arena + 2 * K16)
        q_b = sb("q_b", [P, HB, S], at=arena + 3 * K16)
        k_b = sb("k_b", [P, HB, S], at=arena + 4 * K16)
        v_b = sb("v_b", [P, TB, D], at=arena + K16)
        y_hi = sb("y_hi", [P, KT, S], F32R, at=arena + 3 * K16)
        y_lo = sb("y_lo", [P, KT, S], F32R, at=arena + 4 * K16)
        yb_f = sb("yb_f", [P, HB, S], at=arena)
        a_keys = sb("a_keys", [P, S], F32R, at=arena + 2 * K16 + 7 * 2048)
        a_q_hi = sb("a_q_hi", [P, S], F32R, at=arena + 4 * K16 + 6 * 2048)
        a_q_lo = sb("a_q_lo", [P, S], F32R, at=arena + 4 * K16 + 7 * 2048)
        t1 = arena + 5 * K16
        conv_t = sb("conv_t", [P, 2, S], at=t1)
        decay = sb("decay", [P, CAUSAL], at=t1)
        num_sq = sb("num_sq", [P, S], at=t1 + 5120)
        rows = [sb(f"rows{i}", [HA, S], at=t1 + 7168 + 2048 * i) for i in range(4)]
        m_lo = sb("m_lo", [HA, S], F32R, at=t1 + 7168 + 2048 * 3)
        scale_parts = [sb(f"scale_part{i}", [HA, S], F32R, at=t1 + 7168 + 2048 * i) for i in range(2)]
        stat_parts = [sb(f"stat_part{i}", [64, S], F32R, at=t1 + 2048 * i) for i in range(2)]
        sp_t = sb("sp_t", [P, CAUSAL], at=t1)
        later1 = sb("later1", [P, 128], at=t1 + 5120)
        later0 = sb("later0", [P, 256], at=t1 + 6144)
        attn_b = sb("attn_b", [P, CAUSAL], at=t1 + 7680)
        stat_row = sb("stat_row", [64, S], at=t1 + 5120)
        up_hi = sb("up_hi", [P, KT, S], F32R, at=arena)
        up_lo = sb("up_lo", [P, KT, S], F32R, at=arena + K16)
        relu_t = sb("relu_t", [P, 2, S], at=arena + 3 * K16)
        qn = sb("qn", [P, 8, S], at=arena)
        ks = sb("ks", [P, 2, S], at=arena + K16)
        kw = sb("kw", [P, 2, S], at=arena + K16 + 4096)
        vs = sb("vs", [P, TB, 256], at=arena + K16 + 8192)
        vw = sb("vw", [P, TB, 256], at=arena + K16 + 12288)
        o_a = sb("o_a", [P, TB, D], at=arena + 2 * K16)
        o_b = sb("o_b", [P, TB, D], at=arena + 4 * K16)
        q_parts = [sb(f"q_parts{i}", [P, S], F32R, at=arena + 3 * K16 + 2048 * (1 + i)) for i in range(2)]
        o_w = [sb(f"o_w{i}", [P, 2, 256], at=arena + 3 * K16 + 8192 * i) for i in range(2)]
        k_hi = [sb(f"k_hi{i}", [P, S], F32R, at=arena + 3 * K16 + (10240, 14336)[i]) for i in range(2)]
        k_lo = [sb(f"k_lo{i}", [P, S], F32R, at=arena + 3 * K16 + (12288, 6144)[i]) for i in range(2)]
        w1k = sb("w1k", [P, 16, 256], at=arena + 2 * K16)
        w1v = sb("w1v", [P, 16, 256], at=arena + 3 * K16)
        pairk = sb("pairk", [P, GN, S], at=arena + 4 * K16)
        pairv = sb("pairv", [P, GN, S], at=arena + 4 * K16 + 8192)
        cmp_in = [sb("cmp_in_k", [P, 16, GN * NCMP], at=arena + 5 * K16),
                  sb("cmp_in_v", [P, 16, GN * NCMP], at=arena + 4 * K16)]
        cbias = sb("cbias", [P, TB, NCMP, HN], at=arena + 4 * K16 + 8192)
        clog = [sb(f"clog{i}", [P, HN, CPAD], at=arena + 3 * K16 + 8192 * i) for i in range(2)]
        cpt = [sb(f"cpt{i}", [P, GN, P], at=arena + 4 * K16 + 2048 * i) for i in range(2)]
        v_diag = sb("v_diag", [P, GN, 4, DH], at=arena + 4 * K16 + 4096)
        probs = [sb(f"probs{i}", [P, CAUSAL], at=arena + 5 * K16 + 5120 * i) for i in range(2)]
        probs_t = sb("probs_t", [P, CAUSAL], at=arena + 5 * K16 + 10240)
        out_f = sb("out_f", [P, 2, P], at=arena + 5 * K16 + 15360)
        y2 = sb("y2", [P, TB, D], at=arena)
        gain_bc = sb("gain_bc", [P, D], at=arena + K16)
        xo = sb("xo", [P, TB, D], at=arena + 3 * K16)

        cst = sb("cst", [P, C_ALL])
        vec_rows = sb("vec_rows", [V_ROWS, P])
        vec = sb("vec", [P, V_ROWS])
        bif = sb("bif", [32 + HA, 1])
        ones_row = sb("ones_row", [HA, S], at=arena + 3 * K16)
        u_col = sb("u_col", [P, TB, HA])
        ssq = sb("ssq", [P, 4, TB])
        rstd = sb("rstd", [P, 4, TB])
        ssq_y = sb("ssq_y", [P, TB, 4])
        ev_t = sb("ev_t", [P, 2, S])
        tile_t_at = top[0]
        tile_t = [sb(f"tile_t{i}", [P, S]) for i in range(2)]
        gates_n = sb("gates_n", [P, TB, 48])
        gate_f = sb("gate_f", [48, S], at=tile_t_at)
        sqs = [[sb("sq_q0", [P, S], at=t1), sb("sq_k0", [P, S], at=t1 + 2048)],
               [sb(f"sq_{n}1", [P, S], at=tile_t_at + 2048 * e) for e, n in enumerate("qk")]]
        m_hi = sb("m_hi", [HA, S], F32R, at=tile_t_at + 2048)
        den_sum = sb("den_sum", [P, S - P], at=tile_t_at)
        table = sb("table", [BUCKETS + 1, HN])
        w2k = sb("w2k", [P, 2, DH], at=arena + 5 * K16 + 8192)
        w2v = sb("w2v", [P, 2, DH], at=arena + 5 * K16 + 8704)
        hid_v = sb("hid_v", [P, 2, GN, 4, CPAD], at=arena + 5 * K16 + 10240)
        hid = sb("hid", [P, 2, GN * NCMP], at=arena + 5 * K16 + 9216)
        onehot = sb("onehot", [BUCKETS + 1, OH_W], at=t1 + 4096)
        bias_rev_sb = sb("bias_rev_sb", [HN, 640], at=t1 + 4096 + 4 * OH_W)
        bias_fwd_sb = sb("bias_fwd_sb", [P, 8, HN], at=t1 + 4096 + 4 * OH_W + 2560)
        picks = sb("picks", [64, 64], F32R)
        gq_s = sb("gq_s", [P, 1])
        mn_q = sb("mn_q", [P, HA])
        half_bg = sb("half_bg", [P, HA])
        k_diag = sb("k_diag", [P, 2, 2, CPAD])
        cmax = sb("cmax", [P, HN])
        csum = sb("csum", [P, 2, HN])
        rmax = sb("rmax", [P, 2, TB])
        rneg = sb("rneg", [P, 2, TB])
        rsum = sb("rsum", [P, 2, TB])
        rgate = sb("rgate", [P, TB])
        ps_g = ctx.enter_context(nc.psum_tensor("ps_g", [P, 2, 512], F32))
        ps_z = ctx.enter_context(nc.psum_tensor("ps_z", [P, 1536], F32))
        ps_t = ctx.enter_context(nc.psum_tensor("ps_t", [P, 1536], F32))

        ident = cst[:, C_ID:C_ID + P]

        def col(v, k):
            return vec[:, v + k:v + k + 1]

        def row_picker(i, rows_):
            at = C_STRIP + 39 - i
            return cst[:, at:at + rows_]

        def spread(out, i, k, parts):
            pick = picks[0:k, i:i + 1].broadcast_to([k, P])
            for j, part in enumerate(parts):
                mm = nc.tensor.matmul(out, pick, part[:], start=(j == 0), stop=(j == 1))
            return mm

        const_in = sem("const_in")
        x_in = [sem(f"x_in{b}") for b in range(TB)]
        vec_in = sem("vec_in")
        vec_in_pool = sem("vec_in_pool")
        raw_landed = [sem(f"raw_landed{i}") for i in range(2)]
        hi_done = sem("hi_done")
        lo_done = sem("lo_done")
        tile_ready = sem("tile_ready")
        tile_free = [sem(f"tile_free{i}") for i in range(2)]
        ev_act = sem("ev_act")
        ev_dve = sem("ev_dve")
        act_order = sem("act_order")
        dve_order = sem("dve_order")
        pool_order = sem("pool_order")
        vec_t = sem("vec_t")
        vec_ready = sem("vec_ready")
        sq_done = sem("sq_done")
        var_ready = sem("var_ready")
        std_ready = sem("std_ready")
        xn_ready = sem("xn_ready")
        norm_done = sem("norm_done")
        norm_hi = sem("norm_hi")
        norm_lo = sem("norm_lo")
        gates_mm = sem("gates_mm")
        gates_ready = sem("gates_ready")
        gate_act = sem("gate_act")
        gate_dve = sem("gate_dve")
        u_ready = sem("u_ready")
        u_t = sem("u_t")
        u_col_ready = sem("u_col_ready")
        a_scores = sem("a_scores")
        a_decay = sem("a_decay")
        a_masked = sem("a_masked")
        a_probs = sem("a_probs")
        a_pv = sem("a_pv")
        a_den = sem("a_den")
        a_num = sem("a_num")
        a_ssq = sem("a_ssq")
        a_fin_d = sem("a_fin_d")
        a_fin_a = sem("a_fin_a")
        a_scale = sem("a_scale")
        a_qk_hi = sem("a_qk_hi")
        a_qk = sem("a_qk")
        m_parts = sem("m_parts")
        scale_ready = sem("scale_ready")
        stat_ready = sem("stat_ready")
        a_bc = sem("a_bc")
        a_y = sem("a_y")
        b_sq = sem("b_sq")
        b_stat = sem("b_stat")
        b_var = sem("b_var")
        b_std = sem("b_std")
        b_rstd = sem("b_rstd")
        b_bc = sem("b_bc")
        b_normed = sem("b_normed")
        b_z = sem("b_z")
        b_ln = sem("b_ln")
        b_sp = sem("b_sp")
        b_later = sem("b_later")
        b_sfx = sem("b_sfx")
        b_min = sem("b_min")
        b_attn = sem("b_attn")
        b_pv = sem("b_pv")
        b_out = sem("b_out")
        nsa_in = sem("nsa_in")
        oh_mm = sem("oh_mm")
        oh_cp = sem("oh_cp")
        bias_out = sem("bias_out")
        w1_in = sem("w1_in")
        cmp_ready = sem("cmp_ready")
        hid_mm = sem("hid_mm")
        hid_ready = sem("hid_ready")
        hid_pad = sem("hid_pad")
        kvc_mm = sem("kvc_mm")
        kvc_ready = sem("kvc_ready")
        cb_ready = sem("cb_ready")
        c_scores = sem("c_scores")
        c_log = sem("c_log")
        c_exp = sem("c_exp")
        c_t = sem("c_t")
        c_tc = sem("c_tc")
        c_pv = sem("c_pv")
        c_out = sem("c_out")
        bias_in = [sem(f"bias_in{i}") for i in range(2)]
        s_q_hi = sem("s_q_hi")
        s_q = sem("s_q")
        s_k_hi = sem("s_k_hi")
        s_k = sem("s_k")
        s_scores = sem("s_scores")
        s_max = sem("s_max")
        s_probs = sem("s_probs")
        s_t = sem("s_t")
        s_ta = sem("s_ta")
        s_td = sem("s_td")
        s_pv = sem("s_pv")
        s_f = sem("s_f")
        s_back = sem("s_back")
        s_out = sem("s_out")
        gain_in = sem("gain_in")
        out_ready = sem("out_ready")
        out_done = sem("out_done")

        W, NW = a["w_in"], a["nsa_w_in"]
        slabs = []

        def add(kind, mat, col0, n, row0=0, w=SLAB):
            first = len(slabs)
            for i in range(n):
                slabs.append((mat, row0, col0 + i * w, w, kind, i))
            return first

        N_QA = add("conv", W, QA, 4)
        N_IF = add("if", W, IF, 1, w=P)
        N_VA = add("va", W, VA, 4)
        N_QB = add("qb", W, QB, 8)
        N_VB = add("vb", W, VB, 4)
        N_OA = add("oa", W, OA, 4)
        N_GA = add("ga", W, GA, 4)
        N_GB = add("gb", W, GB, 4)
        N_WO = add("wo", a["w_out"], 0, 4)
        N_MLP = len(slabs)
        for quarter in range(4):
            add("up", a["w_up"], quarter * D, 4)
            add("down", a["w_down"], 0, 4, row0=quarter * D)
        N_NQ = add("nq", NW, NQ, 4)
        N_KC = add("nkc", NW, NKC, 1)
        N_VC = add("nvc", NW, NVC, 1)
        N_NG = add("ng", NW, NG, 1, w=P)
        N_KS = add("nks", NW, NKS, 1)
        N_KW = add("nkw", NW, NKW, 1)
        N_VS = add("nvs", NW, NVS, 1)
        N_VW = add("nvw", NW, NVW, 1)
        N_NZ = len(slabs)
        for z in (0, 1, 2, 4, 5, 6, 3, 7, 8, 9, 10, 11):
            slabs.append((NW, 0, NZ + z * SLAB, SLAB, "nz", z))
        N_NO = add("no", a["nsa_w_out"], 0, 4)
        N_ALL = len(slabs)
        MLP_SLABS = 8
        SB_CUT = 4

        FEATURE = {"conv", "if", "ng", "qb", "oa", "ga", "gb", "up", "nq", "nkc", "nvc", "nks", "nkw"}
        BY_ACT = {"norm": 1, "conv": 1, "no": 1, "oa": 1, "ga": 1, "gb": 2, "up": 2, "nz": 1}
        BY_DVE = {"gb": 1, "up": 1}
        norm_before = {N_QA, N_MLP, N_NQ, N_NO}
        tile_of, norm_tile_of, kinds = {}, {}, []

        def tiles_of(n):
            return slabs[n][3] // P if slabs[n][4] in FEATURE else TB

        for n in range(N_ALL):
            if n in norm_before:
                norm_tile_of[n] = len(kinds)
                kinds += ["norm"] * 2
            tile_of[n] = len(kinds)
            kinds += [slabs[n][4]] * tiles_of(n)
        tile_of[N_ALL] = len(kinds)
        act_count, dve_count = [0], [0]
        for kind in kinds:
            act_count.append(act_count[-1] + BY_ACT.get(kind, 0))
            dve_count.append(dve_count[-1] + BY_DVE.get(kind, 0))
        MLP_TILES = tile_of[N_MLP + MLP_SLABS] - tile_of[N_MLP]

        def cmp_outputs(b):
            return (ps_t[:, 0:512] if b == TB - 1 else ps_z[:, 1024:1536]), ps_t[:, 1024:1536]

        CMP_TILES = (((N_VS, 2),), ((N_VS, 3), (N_VW, 0)), ((N_VW, 1),), ((N_VW, 2), (N_VW, 3)))

        def end_tile(n):
            return tile_of[n] + tiles_of(n)

        def wait_tile_free(eng, t, r=0):
            eng.wait_ge(tile_free[t % 2], t // 2 + 1 + MLP_TILES // 2 * r)

        def split_hi(act, n, r=0):
            if n >= N_ALL:
                return
            b, w = n % 2, slabs[n][3]
            extra = n >= N_IF and b == N_IF % 2
            act.wait_ge(raw_landed[b], 16 * (n // 2 + 1 + extra) + 16 * (MLP_SLABS // 2) * r)
            if n >= 2:
                act.wait_ge(tile_ready, tile_of[n - 1] + MLP_TILES * r)
            nc.scalar.activation(w_hi[b][:, :, 0:w], w_raw[b][:, :, 0:w], ACT.Copy).then_inc(hi_done, 1)

        def split_lo(dve, n, r=0):
            if n >= N_ALL:
                return
            b, w = n % 2, slabs[n][3]
            dve.wait_ge(hi_done, n + 1 + MLP_SLABS * r)
            nc.vector.tensor_tensor(w_lo[b][:, :, 0:w], w_raw[b][:, :, 0:w],
                                    w_hi[b][:, :, 0:w].bitcast(F32), ALU.subtract).then_inc(lo_done, 1)

        def mm_tile(pe, n, i, first_tile=None, hi=act_hi, lo=act_lo, r=0, ks=range(KT),
                    activation_ready=None):
            t, kind = tile_of[n] + i, slabs[n][4]
            b, w = n % 2, slabs[n][3]
            pe.wait_ge(lo_done, n + 1 + MLP_SLABS * r)
            wait_tile_free(pe, t - 2, r)
            m = slice(i * P, (i + 1) * P)
            for k in ks:
                if activation_ready is not None and i == 0:
                    activation_ready(k)
                if first_tile is not None and i == 0 and (t - first_tile - k) % 2:
                    wait_tile_free(pe, first_tile + k, r)
                if kind in FEATURE:
                    o = ps_g[:, t % 2, :]
                    three = ((w_hi[b][:, k, m], hi[:, k, :]), (w_hi[b][:, k, m], lo[:, k, :]),
                             (w_lo[b][:, k, m], hi[:, k, :]))
                else:
                    o = ps_g[:, t % 2, 0:w]
                    three = ((hi[:, k, m], w_hi[b][:, k, 0:w]), (hi[:, k, m], w_lo[b][:, k, 0:w]),
                             (lo[:, k, m], w_hi[b][:, k, 0:w]))
                for j, (stationary, moving) in enumerate(three):
                    mm = nc.tensor.matmul(o, stationary, moving, start=(k == 0 and j == 0),
                                          stop=(k == KT - 1 and j == 2))
            if ks[-1] == KT - 1:
                mm.then_inc(tile_ready, 1)

        def mm_slab(pe, n, first_tile=None, hi=act_hi, lo=act_lo, r=0, activation_ready=None):
            for i in range(tiles_of(n)):
                mm_tile(pe, n, i, first_tile, hi, lo, r, activation_ready=activation_ready)

        def feature_bank(n, k):
            if k < 2:
                return ps_g[:, (norm_tile_of[n] + k) % 2, :]
            k -= 2
            return (ps_z, ps_t)[k // 3][:, k % 3 * 512:(k % 3 + 1) * 512]

        def feature_tiles(pe, n, src, block_ready, between=None):
            t0 = norm_tile_of[n]

            def turn(b, ks):
                for k in ks:
                    mm = nc.tensor.transpose(feature_bank(n, k)[:, b * P:(b + 1) * P],
                                             src(b)[:, k * P:(k + 1) * P], ident)
                    if b == TB - 1:
                        mm.then_inc(tile_ready if k < 2 else norm_done, 1)

            for b in range(TB - 1):
                block_ready(b)
                turn(b, range(2, KT))
            if between is not None:
                between()
            for k in (0, 1):
                if t0 >= 2:
                    wait_tile_free(pe, t0 + k - 2)
                for b in range(TB - 1):
                    turn(b, (k,))
            block_ready(TB - 1)
            turn(TB - 1, range(KT))

        def features_ready(pe, n, which):
            def wait(k):
                if k >= 2:
                    pe.wait_ge(norm_lo, 6 * which + k - 1)
                elif k == 1:
                    wait_tile_free(pe, norm_tile_of[n] + 1)
            return wait

        def tile_done(eng, t, r=0):
            eng.wait_ge(tile_ready, t + 1 + MLP_TILES * r)

        def after_act(eng, t, k, r=0):
            eng.wait_ge(ev_act, act_count[t] + k + ACT_ROUND * r)

        def after_dve(eng, t, k, r=0):
            eng.wait_ge(ev_dve, dve_count[t] + k + DVE_ROUND * r)

        m0, m1 = tile_of[N_MLP], tile_of[N_MLP + MLP_SLABS]
        ACT_ROUND = act_count[m1] - act_count[m0]
        DVE_ROUND = dve_count[m1] - dve_count[m0]

        def act_feature_tile(act, n, k, which, gain):
            if k < 2:
                tile_done(act, norm_tile_of[n] + k)
            else:
                act.wait_ge(norm_done, 6 * which + k - 1)
            scale = 1.0 if gain is None else col(gain, k)
            nc.scalar.activation(act_hi[:, k, :], feature_bank(n, k), ACT.Copy,
                                 scale=scale).then_inc(ev_act if k < 2 else norm_hi, 1)

        def dve_feature_tile(dve, n, k, which, gain):
            t = norm_tile_of[n] + k
            if k < 2:
                after_act(dve, t, 1)
            else:
                dve.wait_ge(norm_hi, 6 * which + k - 1)
            src, hi = feature_bank(n, k), act_hi[:, k, :].bitcast(F32)
            if gain is None:
                ins = nc.vector.tensor_tensor(act_lo[:, k, :], src, hi, ALU.subtract)
            else:
                ins = nc.vector.scalar_tensor_tensor(act_lo[:, k, :], src, col(gain, k), hi, ALU.mult,
                                                     ALU.subtract)
            ins.then_inc(tile_free[t % 2] if k < 2 else norm_lo, 1)

        def act_evacuate(act, n, i, r=0):
            kind, s = slabs[n][4], slabs[n][5]
            t = tile_of[n] + i
            g, free = t % 2, tile_free[t % 2]
            f = 2 * s + i
            cols = slice(s * SLAB, (s + 1) * SLAB)
            if kind == "conv":
                wait_tile_free(act, t)
                nc.scalar.activation(qk_a[:, f, :], conv_t[:, g, :], ACT.Silu).then_inc(ev_act, 1)
                return
            if kind in ("if", "wo", "down"):
                return
            tile_done(act, t, r)
            if kind in ("va", "vb"):
                dst = v_a if kind == "va" else v_b
                nc.scalar.copy(dst[:, i, cols], ps_g[:, g, 0:SLAB]).then_inc(free, 1)
            elif kind == "qb":
                dst = q_b[:, f, :] if f < HB else k_b[:, f - HB, :]
                nc.scalar.copy(dst, ps_g[:, g, :]).then_inc(free, 1)
            elif kind in ("oa", "ga"):
                bias = 0.0 if kind == "oa" else half_bg[:, f:f + 1]
                nc.scalar.activation(ev_t[:, g, :], ps_g[:, g, :], ACT.Tanh, bias=bias,
                                     scale=0.5).then_inc(ev_act, 1)
            elif kind == "gb":
                nc.scalar.activation(ev_t[:, g, :], ps_g[:, g, :], ACT.Sigmoid,
                                     bias=col(V_BGATE, 8 + f)).then_inc(ev_act, 1)
                after_dve(act, t, 1)
                nc.scalar.copy(y_hi[:, f, :], ev_t[:, g, :]).then_inc(ev_act, 1)
            elif kind == "up":
                nc.scalar.activation(ev_t[:, g, :], ps_g[:, g, :], ACT.Relu).then_inc(ev_act, 1)
                after_dve(act, t, 1, r)
                nc.scalar.copy(up_hi[:, f, :], relu_t[:, g, :]).then_inc(ev_act, 1)
            elif kind == "nq":
                half = f // 2 % 2
                for e in range(2):
                    dst = qn[64 * half:64 * half + 64, 4 * (f // 4) + (2 * f + e) % 4, :]
                    ins = nc.scalar.mul(dst, ps_g[64 * e:64 * e + 64, g, :], DH ** -0.5)
                ins.then_inc(free, 1)
            elif kind in ("nkc", "nvc"):
                pair = pairk if kind == "nkc" else pairv
                for e in range(2):
                    src = ps_g[64 * e:64 * e + 64, g, :]
                    nc.scalar.copy(pair[0:64, 2 * i + e, :], src)
                    ins = nc.scalar.copy(pair[64:128, 2 * i + e, 0:S - 1], src[:, 1:S])
                ins.then_inc(free, 1)
            elif kind in ("nks", "nkw"):
                dst = ks if kind == "nks" else kw
                nc.scalar.copy(dst[:, i, :], ps_g[:, g, :]).then_inc(free, 1)
            elif kind in ("nvs", "nvw"):
                dst = vs if kind == "nvs" else vw
                nc.scalar.copy(dst[:, i, :], ps_g[:, g, 0:SLAB]).then_inc(free, 1)
            elif kind == "ng":
                nc.scalar.activation(gate_f[:], ps_g[0:48, g, :], ACT.Tanh, scale=0.5).then_inc(free, 1)
            elif kind == "no":
                nc.scalar.activation(ev_t[:, g, 0:SLAB], ps_g[:, g, 0:SLAB], ACT.Square,
                                     accum_out=ssq_y[:, i, s:s + 1]).then_inc(ev_act, 1)
            elif kind == "nz":
                nc.scalar.activation(ev_t[:, g, 0:SLAB], ps_g[:, g, 0:SLAB], ACT.Tanh,
                                     scale=0.5).then_inc(ev_act, 1)

        def dve_evacuate(dve, order, n, i, r=0):
            kind, s = slabs[n][4], slabs[n][5]
            t = tile_of[n] + i
            g, free = t % 2, tile_free[t % 2]
            f = 2 * s + i
            cols = slice(s * SLAB, (s + 1) * SLAB)
            ps = ps_g[:, g, :]
            if kind == "conv":
                tile_done(dve, t)
                if f >= 2:
                    after_act(dve, t - 2, 1)
                y = conv_t[:, g, :]
                order.link(nc.vector.tensor_scalar(y, ps, col(V_CONV, 24 + f), None, ALU.mult))
                for back in (1, 2, 3):
                    w = col(V_CONV, 8 * (3 - back) + f)
                    ins = nc.vector.scalar_tensor_tensor(y[:, back:S], ps[:, 0:S - back], w,
                                                         y[:, back:S], ALU.mult, ALU.add)
                    if back < 3:
                        order.link(ins)
                ins.then_inc(free, 1)
            elif kind == "if":
                dve.wait_ge(bias_out, 32)
                tile_done(dve, t)
                nc.vector.tensor_scalar(rows[3][:], ps[0:HA, :], bif[0:HA, :], None, ALU.add)
                nc.vector.tensor_scalar(rows[2][:], ps[32:32 + HA, :], bif[32:32 + HA, :], None, ALU.add)\
                    .then_inc(free, 1)
            elif kind in ("oa", "ga"):
                after_act(dve, t, 1)
                nc.vector.scalar_tensor_tensor(y_f[:, f, :], ev_t[:, g, :], 1.0, y_f[:, f, :],
                                               ALU.add, ALU.mult).then_inc(free, 1)
            elif kind == "gb":
                after_act(dve, t, 1)
                order.link(nc.vector.tensor_tensor(ev_t[:, g, :], ev_t[:, g, :], yb_f[:, f, :], ALU.mult))
                nc.vector.tensor_tensor(ev_t[:, g, :], ev_t[:, g, :], y_f[:, f, :], ALU.add)\
                    .then_inc(ev_dve, 1)
                after_act(dve, t, 2)
                nc.vector.tensor_tensor(y_lo[:, f, :], ev_t[:, g, :], y_hi[:, f, :].bitcast(F32),
                                        ALU.subtract).then_inc(free, 1)
            elif kind == "up":
                after_act(dve, t, 1, r)
                nc.vector.tensor_tensor(relu_t[:, g, :], ev_t[:, g, :], ps, ALU.mult)\
                    .then_inc(ev_dve, 1)
                after_act(dve, t, 2, r)
                nc.vector.tensor_tensor(up_lo[:, f, :], relu_t[:, g, :], up_hi[:, f, :].bitcast(F32),
                                        ALU.subtract).then_inc(free, 1)
            elif kind in ("wo", "down"):
                tile_done(dve, t, r)
                nc.vector.tensor_tensor(x_sb[:, i, cols], x_sb[:, i, cols], ps[:, 0:SLAB], ALU.add)\
                    .then_inc(free, 1)
            elif kind == "nz":
                after_act(dve, t, 1)
                branch, c = s // 4, slice(s % 4 * SLAB, (s % 4 + 1) * SLAB)
                e = ev_t[:, g, 0:SLAB]
                order.link(nc.vector.scalar_tensor_tensor(e, e, 1.0, ps[:, 0:SLAB], ALU.add, ALU.mult))
                if branch == 0:
                    nc.vector.tensor_tensor(o_a[:, i, c], o_a[:, i, c], e, ALU.mult).then_inc(free, 1)
                else:
                    o = o_w[i // 2][:, i % 2, :] if s == 11 else o_b[:, i, c]
                    order.link(nc.vector.tensor_tensor(e, e, o, ALU.mult))
                    nc.vector.tensor_tensor(o_a[:, i, c], o_a[:, i, c], e, ALU.add).then_inc(free, 1)
            elif kind == "no":
                after_act(dve, t, 1)
                nc.vector.tensor_tensor(y2[:, i, cols], ps[:, 0:SLAB], gain_bc[:, cols], ALU.mult)\
                    .then_inc(free, 1)

        def dve_slab(dve, order, n, r=0):
            token_major = slabs[n][4] not in FEATURE
            if not token_major:
                split_lo(dve, n + 1, r)
            for i in range(tiles_of(n)):
                dve_evacuate(dve, order, n, i, r)
                if i == 0 and token_major:
                    split_lo(dve, n + 1, r)

        NORM_PARTS = (((0, 1), (1, 3), (3, 4)), ((0, 3), (3, 4)), ((0, 3), (3, 4)))

        def parts_before(which):
            return sum(len(parts) for parts in NORM_PARTS[:which])

        def act_rms(act, which, block_there):
            for p, (b0, b1) in enumerate(NORM_PARTS[which], parts_before(which)):
                for b in range(b0, b1):
                    block_there(b)
                    ins = nc.scalar.activation(xn[b][:], x_sb[:, b, :], ACT.Square,
                                               accum_out=ssq[:, which, b:b + 1])
                ins.then_inc(sq_done, 1)
                act.wait_ge(var_ready, p + 1)
                nc.scalar.activation(rstd[:, which, b0:b1], ssq[:, which, b0:b1],
                                     ACT.Sqrt).then_inc(std_ready, 1)

        def dve_rms(dve, order, which):
            parts, first = NORM_PARTS[which], parts_before(which)

            def mean_square(p):
                if p < len(parts):
                    dve.wait_ge(sq_done, first + p + 1)
                    v = ssq[:, which, parts[p][0]:parts[p][1]]
                    nc.vector.tensor_scalar(v, v, 1.0 / D, EPS, ALU.mult, ALU.add).then_inc(var_ready, 1)

            mean_square(0)
            for p, (b0, b1) in enumerate(parts):
                dve.wait_ge(std_ready, first + p + 1)
                r = rstd[:, which, b0:b1]
                order.link(nc.vector.reciprocal(r, r))
                for b in range(b0, b1):
                    nc.vector.tensor_scalar(xn[b][:], x_sb[:, b, :], rstd[:, which, b:b + 1], None,
                                            ALU.mult).then_inc(xn_ready, 1)
                    if b == (b0 if which else b1 - 1):
                        mean_square(p + 1)

        block = ctx.enter_context(nc.Block())

        @block.sync
        def _(sp):
            def load_slab(n):
                mat, row0, col0, w, _, _ = slabs[n]
                if n >= 2:
                    sp.wait_ge(lo_done, n - 1)
                parts = ((0, 0, 32), (32, HA, w - 32)) if n == N_IF else ((0, 0, w),)
                for at, skip, m in parts:
                    src = mat[row0:row0 + D, col0 + skip:col0 + skip + m]
                    sp.dma_start(w_raw[n % 2][:, :, at:at + m], src.rearrange("(k p) n -> p k n", p=P))\
                        .then_inc(raw_landed[n % 2], 16)

            x_rows = a["x"].rearrange("(b p) n -> p b n", p=P)
            for b in range(TB):
                sp.dma_start(x_sb[:, b, :], x_rows[:, b, :]).then_inc(x_in[b], 16)
            for name, (r0, k) in VEC_PARTS[:SYNC_VECS]:
                sp.dma_start(vec_rows[r0:r0 + k, :], a[name]).then_inc(vec_in, 16)
            for n in range(N_MLP):
                if n == 1:
                    sp.wait_ge(raw_landed[0], 16)
                load_slab(n)
            down_rows = a["w_down"].rearrange("(q k p) n -> p q k n", k=KT, p=P)
            up_cols = a["w_up"].rearrange("(k p) n -> p k n", p=P)
            with sp.Fori(0, 4) as r:
                for j in range(MLP_SLABS):
                    n = N_MLP + j
                    sp.wait_ge(lo_done, MLP_SLABS * r + (n - 1))
                    if j < 4:
                        src = up_cols[:, :, bass.ds(r * D + j * SLAB, SLAB)]
                    else:
                        src = down_rows[:, bass.ds(r, 1), :, (j - 4) * SLAB:(j - 3) * SLAB]
                        src = src.rearrange("p q k n -> p (q k) n")
                    sp.dma_start(w_raw[n % 2][:], src).then_inc(raw_landed[n % 2], 16)
            for n in range(N_NQ, N_ALL):
                if n == N_KC:
                    wait_tile_free(sp, tile_of[N_NQ] - 1)
                    for dst, name in ((w1k, "nsa_cmp_k_w1"), (w1v, "nsa_cmp_v_w1")):
                        sp.dma_start(dst[:], a[name].rearrange("(k p) n -> p k n", p=P))\
                            .then_inc(w1_in, 16)
                    for dst, name in ((w2k, "nsa_cmp_k_w2"), (w2v, "nsa_cmp_v_w2")):
                        sp.dma_start(dst[:], a[name].rearrange("(k p) n -> p k n", p=P))\
                            .then_inc(w1_in, 16)
                if n == N_NO:
                    sp.wait_ge(s_pv, 32)
                    sp.dma_start(gain_bc[:], a["post_gain"].partition_broadcast(P)).then_inc(gain_in, 16)
                load_slab(n)
            out_rows = out.rearrange("(b p) n -> p b n", p=P)
            for b in range(TB):
                sp.wait_ge(out_ready, b + 1)
                sp.dma_start(out_rows[:, b, :], xo[:, b, :]).then_inc(out_done, 16)
            sp.wait_ge(out_done, 16 * TB)

        @block.tensor
        def _(pe):
            def turn_vectors():
                pe.wait_ge(vec_in, 16 * SYNC_VECS)
                pe.wait_ge(vec_in_pool, 16 * (len(VEC_PARTS) - SYNC_VECS + 2))
                nc.tensor.transpose(ps_g[:, 0, 0:V_ROWS], vec_rows[:], ident[0:V_ROWS, 0:V_ROWS])\
                    .then_inc(vec_t, 1)
                pe.wait_ge(vec_ready, 1)

            feature_tiles(pe, N_QA, lambda b: xn[b], lambda b: pe.wait_ge(xn_ready, b + 1), turn_vectors)
            for n in range(N_QA, N_QA + 4):
                mm_slab(pe, n, activation_ready=features_ready(pe, n, 0) if n == N_QA else None)
                if n == N_QA:
                    pe.wait_ge(nsa_in, 32)
                    nc.tensor.matmul(ps_t[0:HN, 512:1024], table[:], onehot[:, OH_REV:OH_REV + 512],
                                     start=True, stop=True)
                    nc.tensor.matmul(ps_t[0:HN, 1024:1152], table[:],
                                     onehot[:, OH_REV + 512:OH_REV + 640], start=True, stop=True)
                    for c in range(8):
                        mm = nc.tensor.matmul(ps_t[:, 1152 + HN * c:1152 + HN * (c + 1)],
                                              onehot[:, c * P:(c + 1) * P], table[:], start=True,
                                              stop=True)
                    mm.then_inc(oh_mm, 1)
            mm_slab(pe, N_IF)
            mm_slab(pe, N_VA)
            mm_slab(pe, N_VA + 1)
            mm_slab(pe, N_VA + 2)
            pe.wait_ge(u_ready, 1)
            pe.wait_ge(oh_cp, 2)
            for b in range(TB):
                mm = nc.tensor.transpose(ps_t[:, 1024 + b * HA:1024 + (b + 1) * HA],
                                         rows[3][:, b * P:(b + 1) * P], ident[0:HA, 0:HA])
            mm.then_inc(u_t, 1)
            mm_slab(pe, N_VA + 3)

            for h in range(HA):
                n = N_QB + h
                if h == 0:
                    pe.wait_ge(m_parts, 2)
                    pe.wait_ge(u_col_ready, 1)
                    pe.wait_ge(gate_act, 2)
                else:
                    pe.wait_ge(a_probs, h)
                spread(ps_t[:, 0:512], h, HA, (m_hi, m_lo))
                pe.wait_ge(a_qk, h + 1)
                for b in range(TB):
                    at, w = CAUSAL_AT[b], CAUSAL_W[b]
                    for j, q in enumerate((a_q_hi, a_q_lo)):
                        mm = nc.tensor.matmul(ps_z[:, at:at + w], a_keys[:, b * P:(b + 1) * P],
                                              q[:, b * P:S], start=(j == 0), stop=(j == 1))
                mm.then_inc(a_scores, 1)
                mm_tile(pe, n, 0)
                pe.wait_ge(a_probs, h + 1)
                if h == 0:
                    wait_tile_free(pe, end_tile(N_VA + 3) - 2)
                    wait_tile_free(pe, end_tile(N_VA + 3) - 1)
                else:
                    pe.wait_ge(a_num, h)
                for b in range(TB):
                    at, w = CAUSAL_AT[b], CAUSAL_W[b]
                    mm = nc.tensor.matmul(ps_t[:, 512 + b * P:1024], v_a[:, b, h * P:(h + 1) * P],
                                          decay[:, at:at + w], start=(b == 0), stop=(b == TB - 1))
                nc.tensor.matmul(ps_t[0:HA, 1024:1024 + P], row_picker(h, HA), decay[:, 0:P],
                                 start=(h == 0), stop=False, skip_group_check=True).then_inc(a_pv, 1)
                mm_tile(pe, n, 1)
                pe.wait_ge(a_den, h + 1)
                pe.wait_ge(a_num, h + 1)
                nc.tensor.matmul(ps_t[0:HA, 1024 + P:1536], row_picker(h, HA), den_sum[:],
                                 start=False, stop=(h == HA - 1), skip_group_check=True)
                nc.tensor.matmul(ps_t[32:32 + HA, 1024:1536], row_picker(h, HA), num_sq[:],
                                 start=(h == 0), stop=(h == HA - 1), skip_group_check=True)\
                    .then_inc(a_ssq, 1)

            for j in range(16):
                n = N_VB + j // 4
                mm_tile(pe, n, j % 4)
                for h in range(2 * j, min(2 * j + 2, HB)):
                    pe.wait_ge(b_sq, h + 1)
                    for e in range(2):
                        mm = nc.tensor.matmul(ps_z[32 * e:32 * e + 32, 0:512], row_picker(h, 32),
                                              sqs[h % 2][e][:], start=(h == 0), stop=(h == HB - 1))
                    mm.then_inc(b_stat, 1)
                if j >= 8:
                    if j == 8:
                        pe.wait_ge(stat_ready, 2)
                        pe.wait_ge(scale_ready, 2)
                    for i in (2 * (j - 8), 2 * (j - 8) + 1):
                        if i >= 2:
                            pe.wait_ge(b_normed, i - 1)
                        at = 512 * (1 + i % 2)
                        spread(ps_z[:, at:at + 512], i % HB + 32 * (i // HB), 64, stat_parts).then_inc(b_bc, 1)
                    h = j - 8
                    if h >= 2:
                        pe.wait_ge(a_y, h - 1)
                    spread(ps_t[:, 512 * (h % 2):512 * (h % 2) + 512], h, HA, scale_parts)\
                        .then_inc(a_bc, 1)

            def sb_values(h):
                pe.wait_ge(b_attn, h + 1)
                if h >= 2:
                    pe.wait_ge(b_out, h - 1)
                if h == 0:
                    wait_tile_free(pe, end_tile(N_VB + 3) - 2)
                    wait_tile_free(pe, end_tile(N_VB + 3) - 1)
                    pe.wait_ge(a_y, HA)
                o = 512 * (h % 2)
                for b in range(TB):
                    at, w = CAUSAL_AT[b], CAUSAL_W[b]
                    mm = nc.tensor.matmul(ps_t[:, o + b * P:o + 512], v_b[:, b, h * P:(h + 1) * P],
                                          attn_b[:, at:at + w], start=(b == 0), stop=(b == TB - 1))
                mm.then_inc(b_pv, 1)

            for h in range(HB):
                n = N_OA + h
                if h == 0:
                    pe.wait_ge(b_normed, 16)
                else:
                    pe.wait_ge(b_attn, h)
                for b in (0, 1, 3, 2):
                    at, w = CAUSAL_AT[b], CAUSAL_W[b]
                    mm = nc.tensor.matmul(ps_z[:, at:at + w], k_b[:, h, b * P:(b + 1) * P],
                                          q_b[:, h, b * P:S], start=(b != 3), stop=True,
                                          skip_group_check=True)
                mm.then_inc(b_z, 1)
                if h:
                    sb_values(h - 1)
                mm_tile(pe, n, 0)
                mm_tile(pe, n, 1, ks=range(0, SB_CUT))
                pe.wait_ge(b_later, h + 1)
                for b in range(TB):
                    at, w = CAUSAL_AT[b], CAUSAL_W[b]
                    mm = nc.tensor.matmul(ps_z[:, at:at + w], cst[:, C_TRI:C_TRI + P], sp_t[:, at:at + w],
                                          start=False, stop=True, skip_group_check=True)
                    if b < 3:
                        nxt = sp_t[:, CAUSAL_AT[b + 1]:CAUSAL_AT[b + 1] + P]
                        mm = nc.tensor.matmul(ps_z[:, at + P:at + 2 * P], cst[:, C_NEG:C_NEG + P], nxt,
                                              start=False, stop=True, skip_group_check=True)
                    if b < 2:
                        mm = nc.tensor.matmul(ps_z[:, at + 2 * P:at + w], cst[:, C_NEG:C_NEG + P],
                                              (later0, later1)[b][:], start=False, stop=True,
                                              skip_group_check=True)
                mm.then_inc(b_sfx, 1)
                mm_tile(pe, n, 1, ks=range(SB_CUT, KT))
            sb_values(HB - 1)
            for n in range(N_GB, N_GB + 4):
                mm_slab(pe, n)
            for n in range(N_WO, N_WO + 4):
                mm_slab(pe, n, tile_of[N_GB] if n == N_WO else None, y_hi, y_lo)

            feature_tiles(pe, N_MLP, lambda b: xn[b], lambda b: pe.wait_ge(xn_ready, TB + b + 1))
            with pe.Fori(0, 4) as r:
                for j in range(4):
                    mm_slab(pe, N_MLP + j, r=r,
                            activation_ready=features_ready(pe, N_MLP, 1) if j == 0 else None)
                for j in range(4, MLP_SLABS):
                    mm_slab(pe, N_MLP + j, tile_of[N_MLP] if j == 4 else None, up_hi, up_lo, r=r)

            feature_tiles(pe, N_NQ, lambda b: xn[b], lambda b: pe.wait_ge(xn_ready, 2 * TB + b + 1))
            for n in range(N_NQ, N_KS + 1):
                mm_slab(pe, n, activation_ready=features_ready(pe, n, 2) if n == N_NQ else None)

            def compress(which, w1):
                pe.wait_ge(cmp_ready, which + 1)
                if which == 0:
                    pe.wait_ge(w1_in, 64)
                    pe.wait_ge(b_out, HB)
                    pe.wait_ge(b_attn, HB)
                else:
                    pe.wait_ge(hid_ready, 1)
                for m in range(2):
                    for k in range(16):
                        mm = nc.tensor.matmul(ps_t[:, m * 512:m * 512 + GN * NCMP],
                                              w1[:, k, m * P:(m + 1) * P], cmp_in[which][:, k, :],
                                              start=(k == 0), stop=(k == 15))
                mm.then_inc(hid_mm, 1)

            compress(0, w1k)
            wait_tile_free(pe, tile_of[N_NG])
            for b in range(TB):
                mm = nc.tensor.transpose(ps_t[:, 1024 + 48 * b:1024 + 48 * (b + 1)],
                                         gate_f[:, b * P:(b + 1) * P], ident[0:48, 0:48])
            mm.then_inc(gates_mm, 1)
            mm_tile(pe, N_KW, 0)
            pe.wait_ge(hid_ready, 1)
            for g in range(GN):
                half = 64 * (g % 2)
                for m in range(2):
                    mm = nc.tensor.matmul(ps_z[half:half + 64, g // 2 * NCMP:(g // 2 + 1) * NCMP],
                                          w2k[:, m, :], hid[:, m, g * NCMP:(g + 1) * NCMP],
                                          start=(m == 0), stop=(m == 1))
            mm.then_inc(kvc_mm, 1)
            compress(1, w1v)
            mm_tile(pe, N_KW, 1)

            def cmp_scores(b):
                if b == 0:
                    pe.wait_ge(kvc_ready, 1)
                    wait_tile_free(pe, end_tile(N_NQ + 3) - 1)
                    wait_tile_free(pe, end_tile(N_NQ + 3) - 2)
                elif b >= 2:
                    pe.wait_ge(c_log, b - 1)
                for f in range(8):
                    at = 512 * (b % 2) + f * 2 * CPAD
                    mm = nc.tensor.matmul(ps_z[:, at:at + 2 * CPAD], qn[:, f, b * P:(b + 1) * P],
                                          k_diag[:, f // 4, :, :], start=True, stop=True)
                mm.then_inc(c_scores, 1)

            def cmp_transposes(b):
                pe.wait_ge(c_exp, b + 1)
                if b >= 2:
                    pe.wait_ge(c_tc, b - 1)
                for g in range(GN):
                    at = 512 * (b % 2) + g * P
                    mm = nc.tensor.transpose(ps_t[:, at:at + P],
                                             clog[b % 2][:, 4 * g:4 * g + 4, :]
                                             .rearrange("p h c -> p (h c)"), ident)
                mm.then_inc(c_t, 1)

            def cmp_values(b):
                pe.wait_ge(c_tc, b + 1)
                if b == 0:
                    pe.wait_ge(kvc_ready, 2)
                else:
                    pe.wait_ge(c_out, b)
                for g in range(GN):
                    first, second = cmp_outputs(b)
                    o = (first if g < 2 else second)[:, g % 2 * 256:(g % 2 + 1) * 256]
                    mm = nc.tensor.matmul(o, cpt[b % 2][:, g, :],
                                          v_diag[:, g, :, :].rearrange("p h d -> p (h d)"),
                                          start=True, stop=True)
                mm.then_inc(c_pv, 1)

            def scores(u):
                pe.wait_ge(s_q, u + 1)
                pe.wait_ge(s_k, u // 4 + 1)
                if u == 0:
                    pe.wait_ge(c_log, TB)
                    pe.wait_ge(c_out, TB - 1)
                else:
                    pe.wait_ge(s_max, u)
                for b in (3, 2, 0, 1):
                    at, w = ROWS_AT[b], ROWS_W[b]
                    if b == 1 and u >= 2:
                        pe.wait_ge(s_f, u - 1)
                    for j, keys in enumerate((k_hi, k_lo)):
                        mm = nc.tensor.matmul(ps_z[:, at:at + w], q_parts[u % 2][:, b * P:(b + 1) * P],
                                              keys[u // 4 % 2][:, 0:w], start=(j == 0), stop=(j == 1))
                mm.then_inc(s_scores, 1)

            cmp_scores(0)
            pe.wait_ge(hid_ready, 2)
            pe.wait_ge(hid_pad, 1)
            for g in range(GN):
                for m in range(2):
                    mm = nc.tensor.matmul(ps_z[:, 1024 + g * DH:1024 + (g + 1) * DH],
                                          hid_v[:, m, g, :, :].rearrange("p r c -> p (r c)"),
                                          w2v[:, m, :],
                                          start=(m == 0), stop=(m == 1))
            mm.then_inc(kvc_mm, 1)
            mm_tile(pe, N_VS, 0)
            mm_tile(pe, N_VS, 1)
            for b in range(TB):
                cmp_transposes(b)
                if b < TB - 1:
                    cmp_scores(b + 1)
                for n, i in CMP_TILES[b]:
                    if (n, i) == (N_VW, 3):
                        scores(0)
                    mm_tile(pe, n, i)
                cmp_values(b)

            def values_of(u):
                g, values = u % HN // 4, (vs, vw)[u // HN]
                if u < 31:
                    pe.wait_ge(s_max, u + 2)
                halves = [[(at, b, s) for at, b in enumerate(blocks) for s in range(b + 1)]
                          for blocks in ((0, 3), (1, 2))]
                for pair in zip(*halves):
                    for e, (at, b, s) in enumerate(pair):
                        block_at = (b * (b + 1) // 2 + s) * P
                        mm = nc.tensor.matmul(
                            ps_z[64 * e:64 * e + 64, CAUSAL + at * P:CAUSAL + (at + 1) * P],
                            values[:, s, g * DH:(g + 1) * DH], probs_t[:, block_at:block_at + P],
                            start=(s == 0), stop=(s == b))
                mm.then_inc(s_pv, 1)

            def turn_back(u):
                pe.wait_ge(s_f, u + 1)
                if u:
                    pe.wait_ge(s_out, u)
                for at in range(2):
                    mm = nc.tensor.transpose(ps_t[:, CAUSAL + at * P:CAUSAL + (at + 1) * P],
                                             out_f[:, at, :], ident)
                mm.then_inc(s_back, 1)

            for u in range(32):
                if u < 31:
                    scores(u + 1)
                else:
                    mm_tile(pe, N_NZ + 7, 3)
                if u:
                    turn_back(u - 1)
                pe.wait_ge(s_probs, u + 1)
                if u:
                    pe.wait_ge(s_ta, u)
                    pe.wait_ge(s_td, u)
                else:
                    pe.wait_ge(c_out, TB)
                for b in range(TB):
                    for s in range(b + 1):
                        at = (b * (b + 1) // 2 + s) * P
                        if u and at == 1024:
                            pe.wait_ge(s_out, u)
                        mm = nc.tensor.transpose(ps_t[:, at:at + P],
                                                 probs[u % 2][:, ROWS_AT[b] + s * P:ROWS_AT[b] + (s + 1) * P],
                                                 ident)
                mm.then_inc(s_t, 1)
                if u < 31:
                    mm_tile(pe, N_NZ + u // 4, u % 4)
                else:
                    mm_tile(pe, N_NZ + 8, 0)
                pe.wait_ge(s_ta, u + 1)
                pe.wait_ge(s_td, u + 1)
                values_of(u)
            turn_back(31)
            for i in (1, 2, 3):
                mm_tile(pe, N_NZ + 8, i)
            for n in range(N_NZ + 9, N_NZ + 12):
                mm_slab(pe, n)
            feature_tiles(pe, N_NO, lambda b: o_a[:, b, :],
                          lambda b: wait_tile_free(pe, tile_of[N_NZ + 11] + b))
            for n in range(N_NO, N_NO + 4):
                mm_slab(pe, n, activation_ready=features_ready(pe, n, 3) if n == N_NO else None)

        @block.scalar
        def _(act):
            order = Order(act, act_order)
            act.dma_start(cst[:], a["cst"]).then_inc(const_in, 16)
            act_rms(act, 0, lambda b: act.wait_ge(x_in[b], 16))
            split_hi(act, 0)
            act.wait_ge(vec_ready, 1)
            for k in range(KT):
                act_feature_tile(act, N_QA, k, 0, V_MIX)
            def a_hi(h):
                half, ft = 64 * (h % 2), h // 2
                if h == 0:
                    act.wait_ge(ev_act, act_count[end_tile(N_QA + 3)])
                else:
                    act.wait_ge(a_scores, h)
                nc.scalar.copy(a_keys[half:half + 64, :], qk_a[half:half + 64, 4 + ft, :])
                for to in (0, 64):
                    ins = nc.scalar.copy(a_q_hi[to:to + 64, :], qk_a[half:half + 64, ft, :])
                ins.then_inc(a_qk_hi, 1)

            for n in range(N_QA, N_QB):
                if n != N_IF:
                    split_hi(act, n + 1)
                for i in range(tiles_of(n)):
                    if n == N_IF - 1 and i == 1:
                        split_hi(act, N_IF + 1)
                    act_evacuate(act, n, i)
                    if n == N_VA and i == 1:
                        wait_tile_free(act, tile_of[N_IF])
                        order.link(nc.scalar.activation(rows[0][:], rows[2][:], ACT.Abs))
                        order.link(nc.scalar.activation(rows[0][:], rows[0][:], ACT.Exp, scale=-1.0))
                    if n == N_VA and i == 3:
                        nc.scalar.activation(rows[0][:], rows[0][:], ACT.Ln, bias=1.0).then_inc(gate_act, 1)
                if n == N_VA + 1:
                    a_hi(0)
                if n == N_VA + 2:
                    act.wait_ge(gate_dve, 1)
                    nc.scalar.activation(rows[1][:], rows[1][:], ACT.Exp, scale=-1.0).then_inc(gate_act, 1)
                    act.wait_ge(gate_dve, 2)
                    nc.scalar.copy(m_hi[:], rows[0][:]).then_inc(m_parts, 1)

            for h in range(HA):
                n = N_QB + h
                split_hi(act, n + 1)
                act.wait_ge(a_scores, h + 1)
                if h:
                    act.wait_ge(a_pv, h)
                for b in range(TB):
                    at, w = CAUSAL_AT[b], CAUSAL_W[b]
                    ins = nc.scalar.activation(decay[:, at:at + w], ps_t[:, b * P:512], ACT.Exp,
                                               bias=u_col[:, b, h:h + 1])
                ins.then_inc(a_decay, 1)
                if h < HA - 1:
                    a_hi(h + 1)
                act_evacuate(act, n, 0)
                act.wait_ge(a_pv, h + 1)
                nc.scalar.copy(y_f[:, h, :], ps_t[:, 512:1024])
                if h:
                    act.wait_ge(a_ssq, h)
                nc.scalar.activation(num_sq[:], ps_t[:, 512:1024], ACT.Square).then_inc(a_num, 1)
                act_evacuate(act, n, 1)

            for j in range(16):
                n = N_VB + j // 4
                if j % 4 == 0:
                    split_hi(act, n + 1)
                if j == 0:
                    act.wait_ge(a_ssq, HA)
                    nc.scalar.activation(rows[2][:], ps_t[0:HA, 1024:1536], ACT.Abs).then_inc(a_fin_a, 1)
                    nc.scalar.mul(rows[3][:], ps_t[32:32 + HA, 1024:1536], 1.0 / P).then_inc(a_fin_a, 1)
                    wait_tile_free(act, end_tile(N_QB + 7) - 1)
                for h in range(2 * j, min(2 * j + 2, HB)):
                    if h >= 2:
                        act.wait_ge(b_stat, h - 1)
                    for e, src in enumerate((q_b, k_b)):
                        ins = nc.scalar.activation(sqs[h % 2][e][:], src[:, h, :], ACT.Square)
                    ins.then_inc(b_sq, 1)
                if j == 4:
                    act.wait_ge(a_fin_d, 1)
                    nc.scalar.activation(rows[3][:], rows[3][:], ACT.Sqrt).then_inc(a_fin_a, 1)
                act_evacuate(act, n, j % 4)
                if j == 5:
                    act.wait_ge(b_var, 1)
                    nc.scalar.activation(stat_row[:], stat_row[:], ACT.Sqrt).then_inc(b_std, 1)
                    act.wait_ge(a_scale, 1)
                    nc.scalar.copy(scale_parts[0][:], rows[2][:]).then_inc(scale_ready, 1)
                if j == 7:
                    act.wait_ge(b_rstd, 1)
                    nc.scalar.copy(stat_parts[0][:], stat_row[:]).then_inc(stat_ready, 1)

            def sb_out(h):
                act.wait_ge(b_pv, h + 1)
                nc.scalar.copy(yb_f[:, h, :], ps_t[:, 512 * (h % 2):512 * (h % 2) + 512]).then_inc(b_out, 1)

            for h in range(HB):
                n = N_OA + h
                split_hi(act, n + 1)
                act.wait_ge(b_z, h + 1)
                if h:
                    act.wait_ge(b_sfx, h)
                else:
                    act.wait_ge(b_normed, 16)
                z = ps_z[:, 0:CAUSAL]
                order.link(nc.scalar.activation(sp_t[:], z, ACT.Abs))
                order.link(nc.scalar.activation(sp_t[:], sp_t[:], ACT.Exp, scale=-1.0))
                nc.scalar.activation(sp_t[:], sp_t[:], ACT.Ln, bias=1.0).then_inc(b_ln, 1)
                if h:
                    sb_out(h - 1)
                act_evacuate(act, n, 0)
                act.wait_ge(b_min, h + 1)
                if h:
                    act.wait_ge(b_pv, h)
                nc.scalar.activation(attn_b[:], z, ACT.Exp).then_inc(b_attn, 1)
                act_evacuate(act, n, 1)
            sb_out(HB - 1)
            for n in range(N_GB, N_MLP):
                split_hi(act, n + 1)
                for i in range(tiles_of(n)):
                    act_evacuate(act, n, i)

            act_rms(act, 1, lambda b: wait_tile_free(act, tile_of[N_WO + 3] + b))
            for k in range(KT):
                act_feature_tile(act, N_MLP, k, 1, V_MLP)
            with act.Fori(0, 4) as r:
                for j in range(MLP_SLABS):
                    split_hi(act, N_MLP + j + 1, r)
                    for i in range(tiles_of(N_MLP + j)):
                        act_evacuate(act, N_MLP + j, i, r)
            act_rms(act, 2, lambda b: wait_tile_free(act, tile_of[N_NQ - 1] + b))
            for k in range(KT):
                act_feature_tile(act, N_NQ, k, 2, V_PRE)
            def hidden(which):
                act.wait_ge(hid_mm, which + 1)
                for m in range(2):
                    src, dst = ps_t[:, m * 512:m * 512 + GN * NCMP], hid[:, m, :]
                    if which:
                        src = src.rearrange("p (g c) -> p g c", c=NCMP).unsqueeze(2)\
                            .broadcast_to([P, GN, 4, NCMP])
                        dst = hid_v[:, m, :, :, 0:NCMP]
                    ins = nc.scalar.activation(dst, src, ACT.Silu)
                ins.then_inc(hid_ready, 1)

            for n in range(N_NQ, N_KS + 1):
                split_hi(act, n + 1)
                if n == N_KC:
                    wait_tile_free(act, norm_tile_of[N_NQ] + 1)
                for i in range(tiles_of(n)):
                    act_evacuate(act, n, i)
            split_hi(act, N_KW + 1)
            hidden(0)
            act_evacuate(act, N_KW, 0)
            hidden(1)
            act_evacuate(act, N_KW, 1)

            def q_hi(u):
                h = u % HN
                half = 64 * (h // 4 % 2)
                if u >= 2:
                    act.wait_ge(s_scores, u - 1)
                elif u == 0:
                    act.wait_ge(hid_mm, 2)
                nc.scalar.copy(q_parts[u % 2][half:half + 64, :],
                               qn[half:half + 64, 4 * (h // 8) + h % 4, :]).then_inc(s_q_hi, 1)

            def key_hi(c):
                keys, g = (ks, kw)[c // GN], c % GN
                half = 64 * (g % 2)
                if c == 0:
                    wait_tile_free(act, end_tile(N_KW) - 1)
                    wait_tile_free(act, end_tile(N_KW) - 2)
                elif c >= 2:
                    act.wait_ge(s_scores, 4 * (c - 1))
                for to in (0, 64):
                    ins = nc.scalar.copy(k_hi[c % 2][to:to + 64, :], keys[half:half + 64, g // 2, :])
                ins.then_inc(s_k_hi, 1)

            def exps(u):
                act.wait_ge(s_max, u + 1)
                for b in range(TB):
                    p = probs[u % 2][:, ROWS_AT[b]:ROWS_AT[b] + ROWS_W[b]]
                    ins = nc.scalar.activation(p, p, ACT.Exp, bias=rneg[:, u % 2, b:b + 1],
                                               accum_out=rsum[:, u % 2, b:b + 1])
                ins.then_inc(s_probs, 1)

            def cmp_exp(b):
                act.wait_ge(c_log, b + 1)
                log = clog[b % 2][:, :, 0:NCMP]
                nc.scalar.activation(log, log, ACT.Exp).then_inc(c_exp, 1)

            split_hi(act, N_VS + 1)
            cmp_exp(0)
            act_evacuate(act, N_VS, 0)
            act_evacuate(act, N_VS, 1)
            for b in range(TB):
                if b == 1:
                    key_hi(0)
                    q_hi(0)
                if b == 2:
                    q_hi(1)
                act.wait_ge(c_t, b + 1)
                if b >= 2:
                    act.wait_ge(c_pv, b - 1)
                nc.scalar.copy(cpt[b % 2][:], ps_t[:, 512 * (b % 2):512 * (b % 2) + 512]
                               .rearrange("p (g t) -> p g t", t=P)).then_inc(c_tc, 1)
                if b < TB - 1:
                    cmp_exp(b + 1)
                for n, i in CMP_TILES[b]:
                    if (n, i) == (N_VW, 3):
                        exps(0)
                    act_evacuate(act, n, i)
                    if (n, i) == (N_VS, 3):
                        split_hi(act, N_VW + 1)

            for u in range(32):
                act.wait_ge(s_t, u + 1)
                if u:
                    act.wait_ge(s_pv, u)
                nc.scalar.copy(probs_t[:, 0:512], ps_t[:, 0:512]).then_inc(s_ta, 1)
                if u < 30:
                    q_hi(u + 2)
                if u < 31:
                    exps(u + 1)
                act_evacuate(act, N_NZ + u // 4, u % 4)
                act.wait_ge(s_pv, u + 1)
                if u:
                    act.wait_ge(s_back, u)
                nc.scalar.copy(out_f[:], ps_z[:, CAUSAL:CAUSAL + 2 * P]
                               .rearrange("p (c t) -> p c t", t=P)).then_inc(s_f, 1)
                if u % 4 == 0:
                    split_hi(act, N_NZ + u // 4 + 1)
                if u % 4 == 1 and u < 29:
                    key_hi(u // 4 + 1)
            for n in range(N_NZ + 8, N_NO):
                split_hi(act, n + 1)
                for i in range(tiles_of(n)):
                    act_evacuate(act, n, i)
            for k in range(KT):
                act_feature_tile(act, N_NO, k, 3, None)
            for n in range(N_NO, N_ALL):
                split_hi(act, n + 1)
                for i in range(tiles_of(n)):
                    act_evacuate(act, n, i)
                    if n == N_ALL - 1:
                        act.wait_ge(var_ready, parts_before(3) + i + 1)
                        r = rstd[:, 3, i:i + 1]
                        nc.scalar.activation(r, r, ACT.Sqrt).then_inc(std_ready, 1)

        @block.vector
        def _(dve):
            order = Order(dve, dve_order)
            order.link(nc.vector.memset(ones_row[:], 1.0))
            dve.wait_ge(const_in, 16)
            dve_rms(dve, order, 0)
            dve.wait_ge(vec_t, 1)
            nc.vector.tensor_copy(vec[:], ps_g[:, 0, 0:V_ROWS]).then_inc(vec_ready, 1)
            dve.wait_ge(vec_ready, 1)
            order.link(nc.vector.tensor_scalar(gq_s[:], col(V_QN, 0), HD ** -0.5, None, ALU.mult))
            order.link(nc.vector.memset(k_diag[:], 0.0))
            nc.vector.tensor_copy(picks[:], cst[0:64, C_ID:C_ID + 64])
            nc.vector.tensor_scalar(mn_q[:], vec[:, V_MNORM:V_MNORM + HA], 0.25, None, ALU.mult)
            order.link(nc.vector.tensor_scalar(half_bg[:], vec[:, V_BGATE:V_BGATE + HA], 0.5, None, ALU.mult))
            split_lo(dve, 0)
            for k in range(KT):
                dve_feature_tile(dve, N_QA, k, 0, V_MIX)
            def a_lo(h):
                half, ft = 64 * (h % 2), h // 2
                own, other = slice(half, half + 64), slice(64 - half, 128 - half)
                dve.wait_ge(a_qk_hi, h + 1)
                nc.vector.tensor_tensor(a_keys[other, :], qk_a[own, 4 + ft, :],
                                        a_keys[own, :].bitcast(F32), ALU.subtract)
                for to in (own, other):
                    ins = nc.vector.tensor_tensor(a_q_lo[to, :], qk_a[own, ft, :],
                                                  a_q_hi[own, :].bitcast(F32), ALU.subtract)
                ins.then_inc(a_qk, 1)

            for n in range(N_QA, N_QB):
                split_lo(dve, n + 1)
                for i in range(tiles_of(n)):
                    dve_evacuate(dve, order, n, i)
                if n == N_QA:
                    dve.wait_ge(oh_mm, 1)
                    nc.vector.tensor_copy(bias_rev_sb[:], ps_t[0:HN, 512:1152]).then_inc(oh_cp, 1)
                    nc.vector.tensor_copy(bias_fwd_sb[:], ps_t[:, 1152:1152 + 8 * HN]
                                          .rearrange("p (c h) -> p c h", h=HN)).then_inc(oh_cp, 1)
                if n == N_VA:
                    wait_tile_free(dve, tile_of[N_IF])
                    dve.wait_ge(gate_act, 1)
                    order.link(nc.vector.tensor_scalar(rows[1][:], rows[2][:], 0.0, None, ALU.min))
                    order.link(nc.vector.tensor_tensor(rows[1][:], rows[1][:], rows[0][:], ALU.subtract))
                    order.link(nc.vector.tensor_tensor_scan(rows[2][:], ones_row[:], rows[1][:], 0.0,
                                                            ALU.mult, ALU.add))
                    nc.vector.tensor_tensor(rows[3][:], rows[3][:], rows[2][:], ALU.subtract)\
                        .then_inc(u_ready, 1)
                    dve.wait_ge(u_ready, 1)
                    order.link(nc.vector.tensor_tensor_scan(rows[0][:], rows[3][:], rows[3][:], 0.0,
                                                            ALU.max, ALU.max))
                    nc.vector.tensor_tensor(rows[1][:], rows[2][:], rows[0][:], ALU.add).then_inc(gate_dve, 1)
                    nc.vector.tensor_scalar(rows[0][:], rows[0][:], -1.0, None, ALU.mult).then_inc(gate_dve, 1)
                if n == N_VA + 1:
                    a_lo(0)
                if n == N_VA + 2:
                    dve.wait_ge(u_t, 1)
                    nc.vector.tensor_copy(u_col[:], ps_t[:, 1024:1024 + TB * HA]
                                          .rearrange("p (b h) -> p b h", h=HA)).then_inc(u_col_ready, 1)
                    dve.wait_ge(m_parts, 1)
                    nc.vector.tensor_tensor(m_lo[:], rows[0][:], m_hi[:].bitcast(F32), ALU.subtract)\
                        .then_inc(m_parts, 1)

            for h in range(HA):
                split_lo(dve, N_QB + h + 1)
                dve.wait_ge(a_masked, h + 1)
                nc.vector.scalar_tensor_tensor(decay[:], ps_z[:, 0:CAUSAL], DQK ** -0.5, decay[:], ALU.mult,
                                               ALU.mult).then_inc(a_probs, 1)
                if h < HA - 1:
                    a_lo(h + 1)

            for j in range(16):
                n = N_VB + j // 4
                if j % 4 == 0:
                    split_lo(dve, n + 1)
                if j == 0:
                    dve.wait_ge(a_fin_a, 2)
                    order.link(nc.vector.tensor_tensor(rows[2][:], rows[2][:], rows[1][:], ALU.max))
                    order.link(nc.vector.reciprocal(rows[2][:], rows[2][:]))
                    order.link(nc.vector.tensor_tensor(rows[3][:], rows[3][:], rows[2][:], ALU.mult))
                    order.link(nc.vector.tensor_tensor(rows[3][:], rows[3][:], rows[2][:], ALU.mult))
                    nc.vector.tensor_scalar(rows[3][:], rows[3][:], EPS, None, ALU.add).then_inc(a_fin_d, 1)
                if j == 4:
                    dve.wait_ge(a_fin_a, 3)
                    order.link(nc.vector.reciprocal(rows[3][:], rows[3][:]))
                    nc.vector.tensor_tensor(rows[2][:], rows[2][:], rows[3][:], ALU.mult).then_inc(a_scale, 1)
                if j == 5:
                    dve.wait_ge(b_stat, HB)
                    nc.vector.tensor_scalar(stat_row[:], ps_z[0:64, 0:512], 1.0 / HD, EPS, ALU.mult,
                                            ALU.add).then_inc(b_var, 1)
                    dve.wait_ge(b_std, 1)
                    nc.vector.reciprocal(stat_row[:], stat_row[:]).then_inc(b_rstd, 1)
                    dve.wait_ge(scale_ready, 1)
                    nc.vector.tensor_tensor(scale_parts[1][:], rows[2][:], scale_parts[0][:].bitcast(F32),
                                            ALU.subtract).then_inc(scale_ready, 1)
                    dve.wait_ge(stat_ready, 1)
                    nc.vector.tensor_tensor(stat_parts[1][:], stat_row[:], stat_parts[0][:].bitcast(F32),
                                            ALU.subtract).then_inc(stat_ready, 1)
                if j >= 8:
                    for i in (2 * (j - 8), 2 * (j - 8) + 1):
                        dve.wait_ge(b_bc, i + 1)
                        q = q_b[:, i, :] if i < HB else k_b[:, i - HB, :]
                        gain = gq_s[:] if i < HB else col(V_KN, 0)
                        at = 512 * (1 + i % 2)
                        nc.vector.scalar_tensor_tensor(q, q, gain, ps_z[:, at:at + 512], ALU.mult,
                                                       ALU.mult).then_inc(b_normed, 1)
                    h = j - 8
                    dve.wait_ge(a_bc, h + 1)
                    at = 512 * (h % 2)
                    nc.vector.scalar_tensor_tensor(y_f[:, h, :], y_f[:, h, :], mn_q[:, h:h + 1],
                                                   ps_t[:, at:at + 512], ALU.mult, ALU.mult).then_inc(a_y, 1)

            for h in range(HB):
                n = N_OA + h
                split_lo(dve, n + 1)
                dve.wait_ge(b_ln, h + 1)
                nc.vector.scalar_tensor_tensor(sp_t[:], ps_z[:, 0:CAUSAL], 0.0, sp_t[:], ALU.max,
                                               ALU.add).then_inc(b_sp, 1)
                if h == 0:
                    dve.wait_ge(a_y, HA)
                dve_evacuate(dve, order, n, 0)
                dve.wait_ge(b_sfx, h + 1)
                for b in range(TB):
                    zd = ps_z[:, CAUSAL_AT[b]:CAUSAL_AT[b] + P]
                    ins = nc.vector.tensor_tensor(zd, zd, cst[:, C_MIN:C_MIN + P], ALU.min)
                ins.then_inc(b_min, 1)
                dve_evacuate(dve, order, n, 1)
            dve.wait_ge(b_out, HB)
            for n in range(N_GB, N_MLP):
                dve_slab(dve, order, n)
            dve_rms(dve, order, 1)
            for k in range(KT):
                dve_feature_tile(dve, N_MLP, k, 1, V_MLP)
            with dve.Fori(0, 4) as r:
                for j in range(MLP_SLABS):
                    dve_slab(dve, order, N_MLP + j, r)
            dve_rms(dve, order, 2)
            for k in range(KT):
                dve_feature_tile(dve, N_NQ, k, 2, V_PRE)
            for n in range(N_NQ, N_KS + 1):
                split_lo(dve, n + 1)
            nc.vector.memset(hid_v[:, :, :, :, NCMP:CPAD], 0.0).then_inc(hid_pad, 1)
            dve.wait_ge(gates_mm, 1)
            nc.vector.tensor_scalar(gates_n[:], ps_t[:, 1024:1024 + TB * 48]
                                    .rearrange("p (b c) -> p b c", c=48), 1.0, 0.25, ALU.add,
                                    ALU.mult).then_inc(gates_ready, 1)
            split_lo(dve, N_KW + 1)
            dve.wait_ge(kvc_mm, 1)
            for e in range(2):
                half = slice(64 * e, 64 * e + 64)
                ins = nc.vector.tensor_copy(k_diag[half, :, e, 0:NCMP],
                                            ps_z[half, 0:2 * NCMP].rearrange("p (t c) -> p t c", c=NCMP))
            ins.then_inc(kvc_ready, 1)
            dve.wait_ge(hid_mm, 2)
            order.link(nc.vector.memset(v_diag[:], 0.0))
            for i in range(2):
                order.link(nc.vector.memset(clog[i][:, :, NCMP:CPAD], 0.0))

            def cmp_logits(b):
                dve.wait_ge(c_scores, b + 1)
                if b == 0:
                    dve.wait_ge(cb_ready, 16 * TB)
                if b >= 2:
                    dve.wait_ge(c_t, b - 1)
                log = clog[b % 2][:, :, 0:NCMP]
                for gg in range(2):
                    at = 512 * (b % 2) + 4 * gg * 2 * CPAD
                    ins = nc.vector.tensor_tensor(
                        log[:, 8 * gg:8 * gg + 8, :].rearrange("p (e r) c -> p e r c", e=2),
                        ps_z[:, at:at + 8 * CPAD].rearrange("p (r e c) -> p e r c", e=2, c=CPAD)[:, :, :, 0:NCMP],
                        cbias[:, b, :, 8 * gg:8 * gg + 8].rearrange("p c (e r) -> p e r c", e=2), ALU.add)
                order.link(ins)
                order.link(nc.vector.tensor_reduce(cmax[:], log, AX_X, ALU.max))
                nc.vector.tensor_tensor(log, log, cmax[:].unsqueeze(2).broadcast_to([P, HN, NCMP]),
                                        ALU.subtract).then_inc(c_log, 1)

            def cmp_sums(b):
                dve.wait_ge(c_exp, b + 1)
                cs = csum[:, b % 2, :]
                order.link(nc.vector.tensor_reduce(cs, clog[b % 2][:, :, 0:NCMP], AX_X, ALU.add))
                order.link(nc.vector.reciprocal(cs, cs))
                order.link(nc.vector.scalar_tensor_tensor(cs, cs, cst[:, C_VALID + b:C_VALID + b + 1],
                                                          gates_n[:, b, 0:HN], ALU.mult, ALU.mult))

            def row_max(u):
                dve.wait_ge(s_scores, u + 1)
                dve.wait_ge(bias_in[u % 2], 16 * (u // 2 + 1))
                if u >= 2:
                    dve.wait_ge(s_t, u - 1)
                for b in range(TB):
                    at, w = ROWS_AT[b], ROWS_W[b]
                    ins = nc.vector.tensor_tensor_reduce(probs[u % 2][:, at:at + w], ps_z[:, at:at + w],
                                                         tile_t[u % 2][:, S - w:S], 1.0, -3.0e38, ALU.add,
                                                         ALU.max, rmax[:, u % 2, b:b + 1])
                order.link(ins)
                nc.vector.tensor_scalar(rneg[:, u % 2, :], rmax[:, u % 2, :], -1.0, None, ALU.mult)\
                    .then_inc(s_max, 1)

            split_lo(dve, N_VS + 1)
            cmp_logits(0)
            dve.wait_ge(gates_ready, 1)
            dve.wait_ge(kvc_mm, 2)
            for r in range(4):
                rows_r = slice(CPAD * r, CPAD * (r + 1))
                ins = nc.vector.tensor_copy(v_diag[rows_r, :, r, :], ps_z[rows_r, 1024:1024 + GN * DH]
                                            .rearrange("p (g d) -> p g d", d=DH))
            ins.then_inc(kvc_ready, 1)
            cmp_sums(0)
            for b in range(TB):
                if b < TB - 1:
                    cmp_logits(b + 1)
                    cmp_sums(b + 1)
                if b == 1:
                    split_lo(dve, N_VW + 1)
                if b == TB - 1:
                    row_max(0)
                dve.wait_ge(c_pv, b + 1)
                for e, ps in enumerate(cmp_outputs(b)):
                    ins = nc.vector.tensor_tensor(
                        o_a[:, b, 512 * e:512 * e + 512].rearrange("p (h d) -> p h d", d=DH),
                        ps.rearrange("p (h d) -> p h d", d=DH),
                        csum[:, b % 2, 8 * e:8 * e + 8].unsqueeze(2).broadcast_to([P, 8, DH]), ALU.mult)
                ins.then_inc(c_out, 1)

            for u in range(32):
                h, branch = u % HN, 1 + u // HN
                if u < 31:
                    row_max(u + 1)
                dve.wait_ge(s_t, u + 1)
                if u:
                    dve.wait_ge(s_pv, u)
                nc.vector.tensor_copy(probs_t[:, 512:CAUSAL], ps_t[:, 512:CAUSAL]).then_inc(s_td, 1)
                if u % 4 == 1:
                    split_lo(dve, N_NZ + u // 4 + 1)
                dve_evacuate(dve, order, N_NZ + u // 4, u % 4)
                dve.wait_ge(s_probs, u + 1)
                order.link(nc.vector.reciprocal(rgate[:], rsum[:, u % 2, :]))
                order.link(nc.vector.tensor_tensor(rgate[:], rgate[:],
                                                   gates_n[:, :, branch * HN + h], ALU.mult))
                dve.wait_ge(s_back, u + 1)
                for c, back in ((0, 1), (1, -1)):
                    if u < 28:
                        o = o_b[:, 2 * c:2 * c + 2, h * DH:(h + 1) * DH]
                    else:
                        o = o_w[c][:, :, (u - 28) * DH:(u - 27) * DH]
                    src = ps_t[:, CAUSAL + c * P:CAUSAL + (c + 1) * P].rearrange("p (b d) -> p b d", d=DH)
                    ins = nc.vector.tensor_tensor(
                        o, src[:, ::back, :],
                        rgate[:, 2 * c:2 * c + 2].unsqueeze(2).broadcast_to([P, 2, DH]), ALU.mult)
                ins.then_inc(s_out, 1)
            dve.wait_ge(s_out, 32)
            for n in range(N_NZ + 8, N_NO):
                dve_slab(dve, order, n)
            for k in range(KT):
                dve_feature_tile(dve, N_NO, k, 3, None)
            dve.wait_ge(gain_in, 16)
            for n in range(N_NO, N_ALL - 1):
                dve_slab(dve, order, n)
            for b in range(TB):
                dve_evacuate(dve, order, N_ALL - 1, b)
                r = rstd[:, 3, b:b + 1]
                order.link(nc.vector.tensor_reduce(r, ssq_y[:, b, :], AX_X, ALU.add))
                nc.vector.tensor_scalar(r, r, 1.0 / D, EPS, ALU.mult, ALU.add).then_inc(var_ready, 1)
                dve.wait_ge(std_ready, parts_before(3) + b + 1)
                order.link(nc.vector.reciprocal(r, r))
                wait_tile_free(dve, tile_of[N_ALL - 1] + b)
                nc.vector.scalar_tensor_tensor(xo[:, b, :], y2[:, b, :], r, x_sb[:, b, :],
                                               ALU.mult, ALU.add).then_inc(out_ready, 1)

        @block.gpsimd
        def _(pool):
            order = Order(pool, pool_order)

            def mask_diagonals(t, keep):
                for b in range(TB):
                    d = t[:, CAUSAL_AT[b]:CAUSAL_AT[b] + P]
                    ins = nc.gpsimd.affine_select(out=d, in_=d, compare_op=keep, fill=0.0, base=0,
                                                  pattern=[[1, P]], channel_multiplier=-1)
                return ins

            for name, (r0, k) in VEC_PARTS[SYNC_VECS:]:
                pool.dma_start(vec_rows[r0:r0 + k, :], a[name]).then_inc(vec_in_pool, 16)
            for c in range(2):
                pool.dma_start(bif[32 * c:32 * c + HA, :], a["b_if"][HA * c:HA * (c + 1), :])\
                    .then_inc(vec_in_pool, 16)
            pool.dma_start(table[:], a["table"]).then_inc(nsa_in, 16)
            pool.dma_start(onehot[:], a["onehot"]).then_inc(nsa_in, 16)

            pool.wait_ge(oh_cp, 2)
            pool.dma_start(a["bias_rev"], bias_rev_sb[:].unsqueeze(1).broadcast_to([HN, P, REV]))\
                .then_inc(bias_out, 16)
            pool.dma_start(a["bias_fwd"].rearrange("(c p) h -> p c h", p=P), bias_fwd_sb[:])\
                .then_inc(bias_out, 16)

            for h in range(HA):
                pool.wait_ge(a_decay, h + 1)
                mask_diagonals(decay, ALU.is_ge).then_inc(a_masked, 1)
                pool.wait_ge(a_probs, h + 1)
                if h:
                    pool.wait_ge(a_ssq, h)
                s0, s1, s2, s3 = (decay[:, CAUSAL_AT[b]:CAUSAL_AT[b] + CAUSAL_W[b]] for b in range(TB))
                order.link(nc.gpsimd.tensor_tensor(den_sum[:], s0[:, P:S], s1, ALU.add))
                order.link(nc.gpsimd.tensor_tensor(den_sum[:, P:], den_sum[:, P:], s2, ALU.add))
                nc.gpsimd.tensor_tensor(den_sum[:, 2 * P:], den_sum[:, 2 * P:], s3, ALU.add)\
                    .then_inc(a_den, 1)
            for h in range(HB):
                pool.wait_ge(b_sp, h + 1)
                if h:
                    pool.wait_ge(b_sfx, h)
                order.link(mask_diagonals(sp_t, ALU.is_gt))
                s1, s2, s3 = (sp_t[:, CAUSAL_AT[b]:CAUSAL_AT[b] + CAUSAL_W[b]] for b in (1, 2, 3))
                order.link(nc.gpsimd.tensor_tensor(later1[:], s2[:, P:2 * P], s3, ALU.add))
                nc.gpsimd.tensor_tensor(later0[:, 0:P], s1[:, P:2 * P], s2[:, 0:P], ALU.add)
                nc.gpsimd.tensor_tensor(later0[:, P:2 * P], s1[:, 2 * P:3 * P], later1[:], ALU.add)\
                    .then_inc(b_later, 1)

            for which, (pair, pos, n) in enumerate(((pairk, V_POSK, N_KC), (pairv, V_POSV, N_VC))):
                wait_tile_free(pool, end_tile(n) - 2)
                wait_tile_free(pool, end_tile(n) - 1)
                if which:
                    pool.wait_ge(cmp_ready, 1)
                for k in range(16):
                    ins = nc.gpsimd.tensor_scalar(
                        cmp_in[which][:, k, :].rearrange("p (g c) -> p g c", c=NCMP),
                        pair[:, :, 2 * k:2 * k + CSTRIDE * (NCMP - 1) + 1:CSTRIDE], col(pos, k), None, ALU.add)
                ins.then_inc(cmp_ready, 1)

            pool.wait_ge(bias_out, 32)
            pool.wait_ge(cmp_ready, 2)
            fwd = a["bias_fwd"]
            for b in range(TB):
                pool.dma_start(cbias[:, b], bass.AP(fwd.tensor, (S - 1 - (CLEN - 1) + b * P) * HN,
                                                    [[HN, P], [-CSTRIDE * HN, NCMP], [1, HN]]))\
                    .then_inc(cb_ready, 16)
            pool.wait_ge(gates_mm, 1)
            rev = a["bias_rev"]
            def q_lo(u):
                h = u % HN
                half = 64 * (h // 4 % 2)
                pool.wait_ge(s_q_hi, u + 1)
                nc.gpsimd.tensor_tensor(q_parts[u % 2][64 - half:128 - half, :],
                                        qn[half:half + 64, 4 * (h // 8) + h % 4, :],
                                        q_parts[u % 2][half:half + 64, :].bitcast(F32),
                                        ALU.subtract).then_inc(s_q, 1)

            def key_lo(c):
                keys, g = (ks, kw)[c // GN], c % GN
                half = 64 * (g % 2)
                pool.wait_ge(s_k_hi, c + 1)
                for to in (0, 64):
                    ins = nc.gpsimd.tensor_tensor(k_lo[c % 2][to:to + 64, :], keys[half:half + 64, g // 2, :],
                                                  k_hi[c % 2][half:half + 64, :].bitcast(F32), ALU.subtract)
                ins.then_inc(s_k, 1)

            def load_bias(u):
                if u >= 2:
                    pool.wait_ge(s_max, u - 1)
                pool.dma_start(tile_t[u % 2][:], bass.AP(rev.tensor, (u % HN) * P * REV + P - 1,
                                                         [[REV - 1, P], [1, S]])).then_inc(bias_in[u % 2], 16)

            load_bias(0)
            load_bias(1)
            key_lo(0)
            q_lo(0)
            q_lo(1)
            for u in range(30):
                if u % 4 == 2 and u < 29:
                    key_lo(u // 4 + 1)
                q_lo(u + 2)
                load_bias(u + 2)


DRAM = dict(
    x=("x", (S, D)), w_in=("w_in", (D, 8208)), w_out=("w_out", (D, D)), w_up=("w_up", (D, DFF)),
    w_down=("w_down", (DFF, D)), nsa_w_in=("nsa_w_in_2", (D, 5680)), nsa_w_out=("nsa_w_out_2", (D, D)),
    nsa_cmp_k_w1=("nsa_cmp_k_w1_2", (2048, 256)), nsa_cmp_v_w1=("nsa_cmp_v_w1_2", (2048, 256)),
    nsa_cmp_k_w2=("nsa_cmp_k_w2_2", (256, DH)), nsa_cmp_v_w2=("nsa_cmp_v_w2_2", (256, DH)),
    mix_g=("norm_mix_g", (8, P)), mlp_g=("norm_mlp_g", (8, P)), pre_g=("pre_norm_gain_2", (8, P)),
    mnorm_g=("mlstm_norm_g", (8, P)), conv_w=("conv_w", (32, P)), b_gate=("b_gate", (16, P)),
    pos_k=("nsa_cmp_k_pos_2", (16, P)), pos_v=("nsa_cmp_v_pos_2", (16, P)),
    qn_g=("sb_q_norm_g", (1, P)), kn_g=("sb_k_norm_g", (1, P)), b_if=("b_if", (16, 1)),
    post_gain=("post_norm_gain_2", (D,)),
)


def build(nc, inputs):
    arrays, aps = {}, {}

    def bring(name, arr):
        arrays[f"in_{name}"] = arr
        aps[name] = nc.dram_tensor(f"in_{name}", arr.shape, F32, kind="ExternalInput").ap()

    for name, (key, shape) in DRAM.items():
        bring(name, np.ascontiguousarray(np.asarray(inputs[key]).reshape(shape)))
    bring("cst", constants())
    bring("onehot", bucket_table())
    table = np.asarray(inputs["rel_bias_table_2"])
    bring("table", np.ascontiguousarray(np.concatenate([table, np.full((1, HN), NEG, table.dtype)])))
    aps["bias_rev"] = nc.dram_tensor("bias_rev_dram", (HN, P, REV), F32, kind="Internal").ap()
    aps["bias_fwd"] = nc.dram_tensor("bias_fwd_dram", (1024, HN), F32, kind="Internal").ap()
    out = nc.dram_tensor("out_dram", (S, D), F32, kind="ExternalOutput").ap()
    program(nc, aps, out)
    return arrays


def kernel(**inputs):
    import concourse.bacc as bacc
    from concourse.bass_utils import run_bass_kernel_spmd
    nc = bacc.Bacc("TRN2", target_bir_lowering=False, num_devices=1)
    arrays = build(nc, inputs)
    r = run_bass_kernel_spmd(nc, [arrays], core_ids=[0])
    return r.results[0]["out_dram"].reshape(1, S, D)
```
